# Optimizing a Trainium2 kernel written in Bass

```python
import jax, jax.numpy as jnp
from jax import lax
import numpy as np

D_MODEL = 2048
BATCH = 1
SEQ = 256
DEPTH = 1

PLE_DIM = 256
HGRN_HEADS = 8
HGRN_HEAD_DIM = 128
HGRN_WIDTH = HGRN_HEADS * HGRN_HEAD_DIM
HGRN_CHUNK = 64
MOBA_HEADS = 8
MOBA_HEAD_DIM = 128
MOBA_WIDTH = MOBA_HEADS * MOBA_HEAD_DIM
MOBA_BLOCK = 256
MOBA_TOPK = 3
MOBA_QBLOCK = 64
ROPE_THETA = 10000.0
N_GROUPS = 4
EXPERTS_PER_GROUP = 8
N_EXPERTS = N_GROUPS * EXPERTS_PER_GROUP
TOPK_IN_GROUP = 2
D_EXPERT = 512
MOE_ROW_BLOCK = 128
IN_COLS = 4 * HGRN_WIDTH + 3 * MOBA_WIDTH + 2 * D_MODEL
EPS = 1e-6
NEG_INF = -1e30

kernel_name = "hybrid_hgrn2_moba_hmoe_block"

def rmsnorm(x, g):
    x32 = x.astype(jnp.float32)
    y = x32 * lax.rsqrt(jnp.mean(x32 * x32, axis=-1, keepdims=True) + EPS) * g.astype(jnp.float32)
    return y.astype(x.dtype)

def rope(x, positions):
    half = x.shape[-1] // 2
    inv_freq = ROPE_THETA ** (-jnp.arange(half, dtype=jnp.float32) / half)
    ang = positions.astype(jnp.float32)[:, None] * inv_freq[None, :]
    cos = jnp.cos(ang)[None, :, None, :]
    sin = jnp.sin(ang)[None, :, None, :]
    x32 = x.astype(jnp.float32)
    x1, x2 = x32[..., :half], x32[..., half:]
    out = jnp.concatenate([x1 * cos - x2 * sin, x2 * cos + x1 * sin], axis=-1)
    return out.astype(x.dtype)

def hgrn2_mixer(q_raw, f_raw, i_raw, og_raw, lb, norm_g):
    B, T, _ = q_raw.shape
    H, dk, C = HGRN_HEADS, HGRN_HEAD_DIM, HGRN_CHUNK
    nc = T // C
    f32 = jnp.float32
    q = jax.nn.silu(q_raw.astype(f32))
    lb32 = lb.astype(f32)
    log_f = jnp.logaddexp(jnp.log(lb32), jnp.log1p(-lb32) + jax.nn.log_sigmoid(f_raw.astype(f32)))
    k = -jnp.expm1(log_f)
    v = i_raw.astype(f32)

    def to_chunks(a):
        return a.reshape(B, nc, C, H, dk).transpose(1, 0, 3, 2, 4)

    causal = jnp.tril(jnp.ones((C, C), dtype=bool))[:, :, None]

    def step(S, inp):
        qc, kc, vc, gc = inp
        b = jnp.cumsum(gc, axis=2)
        diff = b[:, :, :, None, :] - b[:, :, None, :, :]
        decay = jnp.where(causal, jnp.exp(jnp.where(causal, diff, 0.0)), 0.0)
        scores = jnp.einsum('bhtk,bhsk,bhtsk->bhts', qc, kc, decay)
        o = (jnp.einsum('bhts,bhsv->bhtv', scores, vc)
             + jnp.einsum('bhtk,bhkv->bhtv', qc * jnp.exp(b), S))
        b_last = b[:, :, -1:, :]
        S = (jnp.exp(b_last)[:, :, 0, :, None] * S
             + jnp.einsum('bhsk,bhsv->bhkv', kc * jnp.exp(b_last - b), vc))
        return S, o

    S0 = jnp.zeros((B, H, dk, dk), f32)
    _, o = lax.scan(step, S0, (to_chunks(q), to_chunks(k), to_chunks(v), to_chunks(log_f)))
    o = o.transpose(1, 0, 3, 2, 4).reshape(B, T, H, dk)
    o = o * lax.rsqrt(jnp.mean(o * o, axis=-1, keepdims=True) + EPS) * norm_g.astype(f32)
    o = o.reshape(B, T, H * dk) * jax.nn.silu(og_raw.astype(f32))
    return o.astype(q_raw.dtype)

def moba_mixer(q, k, v):
    B, T, H, hd = q.shape
    BS, QB = MOBA_BLOCK, MOBA_QBLOCK
    f32 = jnp.float32
    nb = -(-T // BS)
    t_pad = nb * BS
    nq = T // QB
    k_sel_n = min(MOBA_TOPK, nb)
    pad = ((0, 0), (0, t_pad - T), (0, 0), (0, 0))
    kbh = jnp.pad(k, pad).reshape(B, nb, BS, H, hd).transpose(0, 3, 1, 2, 4)
    vbh = jnp.pad(v, pad).reshape(B, nb, BS, H, hd).transpose(0, 3, 1, 2, 4)
    k_mean = jnp.mean(kbh.astype(f32), axis=3)
    scale = hd ** -0.5
    bi = jnp.arange(B)[:, None, None, None]
    hi = jnp.arange(H)[None, None, :, None]
    q_chunks = q.reshape(B, nq, QB, H, hd).transpose(1, 0, 2, 3, 4)

    def attend(args):
        qc, ci = args
        q_pos = ci * QB + jnp.arange(QB)
        cur = (ci * QB) // BS
        gate = jnp.einsum('bqhd,bhnd->bqhn', qc.astype(f32), k_mean)
        gate = jnp.where(jnp.arange(nb) < cur, gate, NEG_INF)
        _, sel = lax.top_k(gate, k_sel_n)
        valid = sel < cur
        kg = kbh[bi, hi, sel]
        vg = vbh[bi, hi, sel]
        s_sel = jnp.einsum('bqhd,bqhjsd->bqhjs', qc, kg).astype(f32) * scale
        s_sel = jnp.where(valid[..., None], s_sel, NEG_INF).reshape(B, QB, H, k_sel_n * BS)
        k_own = lax.dynamic_index_in_dim(kbh, cur, axis=2, keepdims=False)
        v_own = lax.dynamic_index_in_dim(vbh, cur, axis=2, keepdims=False)
        s_own = jnp.einsum('bqhd,bhsd->bqhs', qc, k_own).astype(f32) * scale
        key_pos = cur * BS + jnp.arange(BS)
        s_own = jnp.where((key_pos[None, :] <= q_pos[:, None])[None, :, None, :], s_own, NEG_INF)
        probs = jax.nn.softmax(jnp.concatenate([s_sel, s_own], axis=-1), axis=-1).astype(v.dtype)
        p_sel = probs[..., :k_sel_n * BS].reshape(B, QB, H, k_sel_n, BS)
        p_own = probs[..., k_sel_n * BS:]
        return (jnp.einsum('bqhjs,bqhjsd->bqhd', p_sel, vg)
                + jnp.einsum('bqhs,bhsd->bqhd', p_own, v_own))

    o = lax.map(attend, (q_chunks, jnp.arange(nq)))
    return o.transpose(1, 0, 2, 3, 4).reshape(B, T, H * hd)

def hier_moe(h, w_router_group, w_router_expert, w_gate, w_up, w_down):
    B, T, D = h.shape
    N = B * T
    f32 = jnp.float32
    hf = h.reshape(N, D)
    g_logits = (hf @ w_router_group).astype(f32)
    g_probs = jax.nn.softmax(g_logits, axis=-1)
    g_sel = jnp.argmax(g_logits, axis=-1)
    p_group = jnp.take_along_axis(g_probs, g_sel[:, None], axis=-1)
    e_logits = (hf @ w_router_expert).astype(f32).reshape(N, N_GROUPS, EXPERTS_PER_GROUP)
    e_logits = jnp.take_along_axis(e_logits, g_sel[:, None, None], axis=1)[:, 0]
    top_p, top_i = lax.top_k(jax.nn.softmax(e_logits, axis=-1), TOPK_IN_GROUP)
    weights = p_group * top_p / jnp.sum(top_p, axis=-1, keepdims=True)
    eid = g_sel[:, None] * EXPERTS_PER_GROUP + top_i

    R = MOE_ROW_BLOCK
    M = N * TOPK_IN_GROUP
    flat_e = eid.reshape(M).astype(jnp.int32)
    flat_tok = jnp.repeat(jnp.arange(N, dtype=jnp.int32), TOPK_IN_GROUP)
    flat_w = weights.reshape(M)
    order = jnp.argsort(flat_e)
    es, ts, ws = flat_e[order], flat_tok[order], flat_w[order]
    counts = jnp.bincount(flat_e, length=N_EXPERTS).astype(jnp.int32)
    padded = (counts + R - 1) // R * R
    start = jnp.cumsum(counts) - counts
    pad_end = jnp.cumsum(padded)
    pad_start = pad_end - padded
    dest = pad_start[es] + jnp.arange(M, dtype=jnp.int32) - start[es]
    n_blocks = -(-M // R) + N_EXPERTS
    m_pad = n_blocks * R
    tok_pad = jnp.zeros((m_pad,), jnp.int32).at[dest].set(ts)
    w_pad = jnp.zeros((m_pad,), f32).at[dest].set(ws)
    block_expert = jnp.minimum(
        jnp.searchsorted(pad_end, jnp.arange(n_blocks, dtype=jnp.int32) * R, side='right'),
        N_EXPERTS - 1)
    xb = hf[tok_pad].reshape(n_blocks, R, D)

    def expert_block(args):
        xr, e = args
        return (jax.nn.silu(xr @ w_gate[e]) * (xr @ w_up[e])) @ w_down[e]

    yb = lax.map(expert_block, (xb, block_expert)).reshape(m_pad, D)
    y = jnp.zeros((N, D), f32).at[tok_pad].add(yb.astype(f32) * w_pad[:, None])
    return y.reshape(B, T, D).astype(h.dtype)

def setup_inputs(seed: int = 0) -> dict:
    key = jax.random.key(seed)
    ks = jax.random.split(key, 20)
    f32 = jnp.float32
    nrm = lambda k, shape, s: jax.random.normal(k, shape, f32) * s
    gain = lambda k, shape: 1.0 + 0.02 * jax.random.normal(k, shape, f32)
    return {
        "x": nrm(ks[0], (BATCH, SEQ, D_MODEL), 1.0),
        "p": nrm(ks[1], (DEPTH, BATCH, SEQ, PLE_DIM), 1.0),
        "norm_mix_g": gain(ks[2], (DEPTH, D_MODEL)),
        "w_in": nrm(ks[3], (DEPTH, D_MODEL, IN_COLS), D_MODEL ** -0.5),
        "hgrn_lb_raw": nrm(ks[4], (DEPTH + 1, HGRN_WIDTH), 0.5),
        "hgrn_norm_g": gain(ks[5], (DEPTH, HGRN_HEAD_DIM)),
        "w_up_hgrn": nrm(ks[6], (DEPTH, HGRN_WIDTH, D_MODEL), HGRN_WIDTH ** -0.5),
        "w_up_moba": nrm(ks[7], (DEPTH, MOBA_WIDTH, D_MODEL), MOBA_WIDTH ** -0.5),
        "w_out": nrm(ks[8], (DEPTH, D_MODEL, D_MODEL), D_MODEL ** -0.5),
        "norm_ffn_g": gain(ks[9], (DEPTH, D_MODEL)),
        "w_router_group": nrm(ks[10], (DEPTH, D_MODEL, N_GROUPS), D_MODEL ** -0.5),
        "w_router_expert": nrm(ks[11], (DEPTH, D_MODEL, N_EXPERTS), D_MODEL ** -0.5),
        "w_exp_gate": nrm(ks[12], (DEPTH, N_EXPERTS, D_MODEL, D_EXPERT), D_MODEL ** -0.5),
        "w_exp_up": nrm(ks[13], (DEPTH, N_EXPERTS, D_MODEL, D_EXPERT), D_MODEL ** -0.5),
        "w_exp_down": nrm(ks[14], (DEPTH, N_EXPERTS, D_EXPERT, D_MODEL), D_EXPERT ** -0.5),
        "norm_ple_g": gain(ks[15], (DEPTH, D_MODEL)),
        "w_ple_gate": nrm(ks[16], (DEPTH, D_MODEL, D_MODEL), D_MODEL ** -0.5),
        "w_ple_proj": nrm(ks[17], (DEPTH, PLE_DIM, D_MODEL), PLE_DIM ** -0.5),
        "norm_final_g": gain(ks[18], (D_MODEL,)),
    }

def reference(x, p, norm_mix_g, w_in, hgrn_lb_raw, hgrn_norm_g, w_up_hgrn, w_up_moba, w_out,
              norm_ffn_g, w_router_group, w_router_expert, w_exp_gate, w_exp_up, w_exp_down,
              norm_ple_g, w_ple_gate, w_ple_proj, norm_final_g):
    B, T, D = x.shape
    positions = jnp.arange(T)
    lower_bounds = jnp.cumsum(jax.nn.softmax(hgrn_lb_raw.astype(jnp.float32), axis=0), axis=0)
    sizes = [HGRN_WIDTH] * 4 + [MOBA_WIDTH] * 3 + [D_MODEL] * 2
    offsets = []
    acc = 0
    for s in sizes[:-1]:
        acc += s
        offsets.append(acc)
    for i in range(DEPTH):
        h = rmsnorm(x, norm_mix_g[i])
        proj = h @ w_in[i]
        hq, hf_, hi_, hog, mq, mk, mv, gate_a, gate_b = jnp.split(proj, offsets, axis=-1)
        o_hgrn = hgrn2_mixer(hq, hf_, hi_, hog, lower_bounds[i], hgrn_norm_g[i])
        mq = rope(mq.reshape(B, T, MOBA_HEADS, MOBA_HEAD_DIM), positions)
        mk = rope(mk.reshape(B, T, MOBA_HEADS, MOBA_HEAD_DIM), positions)
        mv = mv.reshape(B, T, MOBA_HEADS, MOBA_HEAD_DIM)
        o_moba = moba_mixer(mq, mk, mv)
        merged = (jax.nn.sigmoid(gate_a) * (o_hgrn @ w_up_hgrn[i])
                  + jax.nn.sigmoid(gate_b) * (o_moba @ w_up_moba[i]))
        x = x + merged @ w_out[i]
        x = x + hier_moe(rmsnorm(x, norm_ffn_g[i]), w_router_group[i], w_router_expert[i],
                         w_exp_gate[i], w_exp_up[i], w_exp_down[i])
        hp = rmsnorm(x, norm_ple_g[i])
        x = x + jax.nn.sigmoid(hp @ w_ple_gate[i]) * (p[i] @ w_ple_proj[i])
    return rmsnorm(x, norm_final_g)


_drawn_inputs = setup_inputs


def setup_inputs(seed=0):
    import zlib

    import numpy as np

    out = dict(_drawn_inputs(seed))
    spreads = {}
    factors = {'hgrn_norm_g': 3.319, 'norm_ple_g': 49.601, 'norm_final_g': 8.09, 'norm_ffn_g': 2.817}
    for name, (base, spread) in spreads.items():
        noise = np.random.default_rng([zlib.crc32(name.encode()), seed]).standard_normal(out[name].shape)
        drawn = base * np.exp(spread * noise) if base else spread * noise
        out[name] = __import__('jax').numpy.asarray(drawn.astype(out[name].dtype))
    for name, factor in factors.items():
        out[name] = (out[name] * factor).astype(out[name].dtype)
    return out
```

```python
from contextlib import ExitStack

import concourse.bass as bass
import numpy as np
from concourse import mybir

F32 = mybir.dt.float32
I32 = mybir.dt.int32
U8 = mybir.dt.uint8
ALU = mybir.AluOpType
ACT = mybir.ActivationFunctionType
AX = mybir.AxisListType

P = 128
TOK = 256
TT = TOK // P
D = 2048
DC = D // P
HEADS = 8
HW = HEADS * P
EXPERTS, GROUPS = 32, 4
PER_GROUP = EXPERTS // GROUPS
FE = 512
FC = FE // P
SLOTS = 2 * TOK
WIN = 64
PLE = 256
EPS = 1e-6
SCALE = float(P) ** -0.5
RING = 3
PIECE = 8192

N_IN, N_UP, N_OUT, N_PLE = 22, 4, 4, 4
DENSE = N_IN + N_UP + N_OUT
assert DENSE % RING == 0
U_HF, U_HI, U_HOG, U_MQ, U_MV, U_GA, U_GB, U_UPH, U_UPM, U_OUT, U_END = (
    4, 8, 12, 16, 24, 28, 36, 44, 52, 60, 68)
LEVELS = 9
AT_LEVEL0, AT_O, AT_OT, AT_ATT = 16, 25, 26, (27, 30)

CONSTS = dict(ident=128, rot=128, cos=256, sin=256, causal=128, before=128, ones=128, desc=8)
LEARNED = dict(g_mix=16, g_ffn=16, g_ple=16, g_hgrn=1, lb_raw=16)


def units_through(i):
    return 2 * (i + 1) + 2 * min(max(i + 1 - N_IN, 0), N_UP)


def columns(table):
    out, at = {}, 0
    for name, n in table.items():
        out[name] = (at, at + n)
        at += n
    return out, at


CONST_AT, N_CONST = columns(CONSTS)
LEARNED_AT, N_LEARNED = columns(LEARNED)


def build_layer(nc, x, pt, pieces, ple_proj, learned, router, consts, iota_row, masks, w_gate, w_up,
                w_down, g_final, out):
    y_rows = nc.dram_tensor("y_rows", [SLOTS + WIN, D], F32).ap()
    gate_v = w_gate.rearrange("e (p j) f -> e p (j f)", p=P)
    up_v = w_up.rearrange("e (p j) f -> e p (j f)", p=P)
    down_v = w_down.rearrange("e (c p) d -> e p c d", p=P)

    with ExitStack() as ctx:
        def sb(name, shape, dt=F32):
            return ctx.enter_context(nc.sbuf_tensor(name, shape, dt))

        def sem(name):
            return ctx.enter_context(nc.semaphore(name))

        ring = [sb(f"ring{n}", [P, PIECE]) for n in range(RING)]
        xtok = sb("xtok", [P, TT * D])
        hT_all = sb("hT_all", [P, DC * TOK])
        arena = sb("arena", [P, 16384])
        work = sb("work", [P, 2048])
        cst = sb("cst", [P, N_CONST])
        lrn = sb("lrn", [P, N_LEARNED])
        mask = sb("mask", [P, 7, P], U8)
        stat = sb("stat", [P, 192])

        def const(name):
            a, b = CONST_AT[name]
            return cst[:, a:b]

        def learnt(name):
            a, b = LEARNED_AT[name]
            return lrn[:, a:b]

        ident, ones = const("ident"), const("ones")
        x_t = [xtok[:, t * D:(t + 1) * D] for t in range(TT)]
        hT = hT_all[:, :].rearrange("p (j t) -> p j t", j=DC)

        def slab(n, k=1):
            return arena[:, 2048 * n:2048 * (n + k)]

        q_T, k_T, f_T = slab(0), slab(1), slab(2)
        v_tok, og_tok, mq_T, mk_T, mv_tok = slab(3), slab(4), slab(5), slab(6), slab(7)
        by_head = lambda ap: ap.rearrange("p (h t) -> p h t", h=HEADS)
        gate_a, gate_b = slab(1, 2), slab(5, 2)
        oh_T, om_T = slab(0), slab(3)
        probs_T = og_tok[:, 0:4 * 384]
        sc_T = xtok[:, 0:2048].rearrange("p (h b t) -> p h b t", h=HEADS, b=2)
        sc_off = xtok[:, 2048:3072].rearrange("p (h t) -> p h t", h=HEADS)
        spans = [f_T, xtok[:, 3072:4096], f_T[:, 0:512], f_T[:, 512:768], f_T[:, 768:896],
                 f_T[:, 896:960], f_T[:, 960:992]]
        h_tok = arena[:, 0:4096]
        XW = SLOTS + WIN
        xg_T = arena[:, 4096:4096 + DC * XW].rearrange("p (j s) -> p j s", j=DC)
        win_T = arena[:, 13312:13312 + DC * WIN].rearrange("p (j s) -> p j s", j=DC)
        wr = arena[:, 14336:14336 + DC * 36].rearrange("p (j e) -> p j e", j=DC)
        silu_g = arena[0:WIN, 14336:14336 + FE]
        hid_all = arena[:, 14848:14848 + FE]
        hid = hid_all[0:WIN, :]
        rt = arena[:, 15360:16384]
        sel = hT_all[:, 0:1024].rearrange("p (t s) -> p t s", t=TT)
        selw = hT_all[:, 1024:2048].rearrange("p (t s) -> p t s", t=TT)
        selw_T = hT_all[:, 2048:3072].rearrange("p (c t) -> p c t", c=4)
        hid_T = hT_all[:, 3072:3072 + FC * WIN].rearrange("p (c s) -> p c s", c=FC)
        iota = work[:, 0:SLOTS]
        y_sb = work[0:WIN, :]
        y_all = arena[:, 0:8192].rearrange("p (c d) -> p c d", c=4)
        hp_tok = arena[:, 8192:12288]
        proj_sb = arena[:, 12288:16384].rearrange("p (c d) -> p c d", c=2)
        p_T = work[:, 0:512].rearrange("p (c t) -> p c t", c=2)
        sig_p = work[:, 512:1536].rearrange("p (b d) -> p b d", b=2)
        g_fin = arena[:, 0:2048]

        tab = sb("tab", [1, 2 * (EXPERTS + 1)], I32)
        PASS0, SLOT0 = 0, EXPERTS + 1

        acc = [ctx.enter_context(nc.psum_tensor(f"acc{b}", [P, 512], F32)) for b in range(2)]
        mid = ctx.enter_context(nc.psum_tensor("mid", [P, 1024], F32))
        big = ctx.enter_context(nc.psum_tensor("big", [P, 2048], F32))

        ring_full = [sem(f"ring_full{n}") for n in range(RING)]
        x_in = [sem(f"x_in{t}") for t in range(TT)]
        consts_in = sem("consts_in")
        unit_ready = sem("unit_ready")
        bank_free = [sem(f"bank_free{b}") for b in range(2)]
        dve_step = sem("dve_step")
        act_step = sem("act_step")
        names = ("sq_done ms_ready root_ready h_ready hT_bank hT_out raw_ready rot_ready rope_used roped "
                 "fk_sig lvl_ready lvl_done off_copied o_ready osq_done oms_ready oroot_ready on_ready oT_ready "
                 "oh_done s_ready sm_ready mx_ready exp_done pn_ready pT_ready pT_out pv_ready om_done "
                 "lb_exp lb_ready lb_max v_ready "
                 "merged_ready x_again router_in iota_in logits_ready gexp_in gexp_out wexp_in wexp_out "
                 "onehot_ready counts_ready sel_ready gather_bank gathered_act gathered_dve padded selwT_ready selwT_out "
                 "tab_ready win_ready gate_done up_done silu_done hid_ready hidT_ready hidT_out y_done "
                 "y_act y_dve y_stored y_back comb_ready comb_out ple_in p_ready p_out_act p_out "
                 "g_fin_in fin_ready stored copied").split()
        s = {n: sem(n) for n in names}

        block = ctx.enter_context(nc.Block())

        @block.sync
        def _(sp):
            xv = x.rearrange("(t p) d -> t p d", p=P)
            for t in range(TT):
                sp.dma_start(x_t[t], xv[t]).then_inc(x_in[t], 16)

            def load_dense(i, slot, src=None):
                sp.dma_start(ring[slot][:, :], pieces[i]).then_inc(ring_full[slot], 16)

            for i in range(DENSE):
                if i >= RING:
                    sp.wait_ge(unit_ready, units_through(i - RING))
                load_dense(i, i % RING)
                if i == N_IN - 2:
                    sp.wait_ge(s["pT_ready"], 2)
                    for t in range(TT):
                        sp.dma_start(x_t[t], xv[t]).then_inc(s["x_again"], 16)

            def load_expert(e, n):
                if n < 2:
                    src = (gate_v, up_v)[n][bass.ds(e, 1)].rearrange("e p f -> (e p) f")
                    sp.dma_start(ring[n][:, :], src).then_inc(ring_full[n], 16)
                else:
                    src = down_v[bass.ds(e, 1)].rearrange("e p c d -> (e p) c d")
                    sp.dma_start(ring[2][:, :].rearrange("p (c d) -> p c d", c=FC), src)\
                      .then_inc(ring_full[2], 16)

            for n in range(RING):
                sp.wait_ge(unit_ready, units_through(DENSE - RING + n))
                load_expert(0, n)
            sp.wait_ge(s["om_done"], 2)
            sp.dma_start(wr, router).then_inc(s["router_in"], 16)
            for b in range(2):
                sp.wait_ge(bank_free[b], U_END // 2)
            sp.dma_start(iota, iota_row.partition_broadcast(P)).then_inc(s["iota_in"], 16)
            sp.wait_ge(s["tab_ready"], 1)
            with sp.Fori(1, EXPERTS) as e:
                passes = sp.value_load(tab[0:1, bass.ds(e, 1)], min_val=1, max_val=SLOTS)
                sp.wait_ge(s["gate_done"], passes)
                load_expert(e, 0)
                sp.wait_ge(s["up_done"], passes)
                load_expert(e, 1)
                sp.wait_ge(s["y_done"], passes * 4)
                load_expert(e, 2)
            total = sp.value_load(tab[0:1, EXPERTS:EXPERTS + 1], min_val=1, max_val=SLOTS)
            for n, done in enumerate(("gate_done", "up_done", "y_done")):
                sp.wait_ge(s[done], total * (4 if n == 2 else 1))
                load_dense(DENSE + n, n)
            sp.dma_start(proj_sb, ple_proj).then_inc(s["ple_in"], 16)
            sp.wait_ge(s["y_stored"], total * 16)
            sp.dma_start(y_all, y_rows[0:SLOTS, :].rearrange("(c p) d -> p c d", p=P))\
              .then_inc(s["y_back"], 16)
            sp.dma_start(p_T, pt).then_inc(s["ple_in"], 16)
            sp.wait_ge(s["comb_ready"], 8)
            sp.dma_start(g_fin, g_final.partition_broadcast(P)).then_inc(s["g_fin_in"], 16)
            sp.wait_ge(s["p_ready"], TT)
            load_dense(DENSE + 3, 0)
            ov = out.rearrange("(t p) d -> t p d", p=P)
            for t in range(TT):
                sp.wait_ge(s["fin_ready"], t + 1)
                sp.dma_start(ov[t], x_t[t]).then_inc(s["stored"], 16)
            sp.wait_ge(s["stored"], 16 * TT)

        @block.gpsimd
        def _(pool):
            pool.wait_ge(s["gathered_act"], DC // 2)
            pool.wait_ge(s["gathered_dve"], DC // 2)
            nc.gpsimd.memset(xg_T[:, :, SLOTS:XW], 0.0).then_inc(s["padded"], 1)
            pool.wait_ge(s["padded"], 1)
            nc.gpsimd.memset(hid_all[WIN:P, :], 0.0).then_inc(s["padded"], 1)
            pool.wait_ge(s["padded"], 2)
            pool.wait_ge(s["tab_ready"], 1)
            with pool.Fori(0, EXPERTS) as e:
                first = pool.value_load(tab[0:1, bass.ds(e, 1)], min_val=0, max_val=SLOTS)
                last = pool.value_load(tab[0:1, bass.ds(e + 1, 1)], min_val=0, max_val=SLOTS)
                slot0 = pool.value_load(tab[0:1, bass.ds(e + SLOT0, 1)], min_val=0, max_val=SLOTS)
                with pool.Fori(first, last) as n:
                    slot = nc.s_assert_within(slot0 + (n - first) * WIN, 0, SLOTS,
                                              skip_runtime_bounds_check_because="an expert's last pass starts below its last slot")
                    pool.wait_ge(s["up_done"], n)
                    nc.gpsimd.tensor_copy(win_T, xg_T[:, :, bass.ds(slot, WIN)]).then_inc(s["win_ready"], 1)

        @block.scalar
        def _(act):
            act.dma_start(cst[:, :], consts).then_inc(consts_in, 16)
            act.dma_start(lrn[:, :], learned).then_inc(consts_in, 16)
            act.dma_start(work[:, 0:7 * P], masks).then_inc(consts_in, 16)
            count = [0]

            def then(ins):
                count[0] += 1
                ins.then_inc(act_step, 1)
                act.wait_ge(act_step, count[0])

            def squares(n, into, src):
                for t in range(TT):
                    nc.scalar.activation(into[:, t * D:(t + 1) * D], src[t], ACT.Square,
                                         accum_out=stat[:, 2 * n + t:2 * n + t + 1]).then_inc(s["sq_done"], 1)

            def root(n):
                act.wait_ge(s["ms_ready"], n + 1)
                nc.scalar.activation(stat[:, 8 + 2 * n:10 + 2 * n], stat[:, 8 + 2 * n:10 + 2 * n],
                                     ACT.Sqrt).then_inc(s["root_ready"], 1)

            for t in range(TT):
                act.wait_ge(x_in[t], 16)
            squares(0, arena[:, 0:4096], x_t)
            root(0)

            lb = stat[:, 32:48]
            act.wait_ge(s["lb_max"], 1)
            nc.scalar.activation(lb, lb, ACT.Exp).then_inc(s["lb_exp"], 1)

            def evacuate(u):
                bank, n = acc[u % 2], u // 2 + 1
                act.wait_ge(unit_ready, u + 1)
                free = bank_free[u % 2]
                if u == 0:
                    act.wait_ge(s["h_ready"], TT)
                    act.wait_ge(s["hT_bank"], DC)
                if u < U_HF:
                    nc.scalar.activation(q_T[:, 512 * u:512 * (u + 1)], bank[:, :], ACT.Silu).then_inc(free, 1)
                elif u < U_HI:
                    w = slice(512 * (u - U_HF), 512 * (u - U_HF + 1))
                    nc.scalar.activation(f_T[:, w], bank[:, :], ACT.Sigmoid).then_inc(s["fk_sig"], 1)
                    nc.scalar.activation(k_T[:, w], bank[:, :], ACT.Sigmoid, scale=-1.0).then_inc(free, 1)
                elif u < U_MQ:
                    base, dst = (U_HI, v_tok) if u < U_HOG else (U_HOG, og_tok)
                    c, t = (u - base) // 2, (u - base) % 2
                    nc.scalar.activation(dst[:, t * HW + 512 * c:t * HW + 512 * (c + 1)], bank[:, :],
                                         ACT.Copy if dst is v_tok else ACT.Silu).then_inc(free, 1)
                elif u < U_MV:
                    k = u - U_MQ
                    dst = (mq_T, mk_T)[k // 4][:, 512 * (k % 4):512 * (k % 4 + 1)]
                    nc.scalar.activation(dst, bank[:, :], ACT.Copy).then_inc(free, 1)
                elif u < U_GA:
                    c, t = (u - U_MV) // 2, (u - U_MV) % 2
                    nc.scalar.activation(mv_tok[:, t * HW + 512 * c:t * HW + 512 * (c + 1)], bank[:, :],
                                         ACT.Copy).then_inc(free, 1)
                elif u < U_UPH:
                    if u == U_GA:
                        act.wait_ge(s["lvl_done"], LEVELS)
                        act.wait_ge(s["off_copied"], 1)
                    if u == U_GB:
                        act.wait_ge(s["s_ready"], 2)
                    dst, base = (gate_a, U_GA) if u < U_GB else (gate_b, U_GB)
                    w = slice(512 * (u - base), 512 * (u - base + 1))
                    nc.scalar.activation(dst[:, w], bank[:, :], ACT.Sigmoid).then_inc(free, 1)

            def softmax(r):
                act.wait_ge(s["mx_ready"], r + 1)
                sm = xtok[:, 1536 * r:1536 * (r + 1)].rearrange("p (h s) -> p h s", h=4)
                for h in range(4):
                    for t, (a, b) in enumerate(((0, 128), (128, 384))):
                        k = 4 * t + h
                        nc.scalar.activation(sm[:, h, a:b], sm[:, h, a:b], ACT.Exp,
                                             bias=stat[:, 112 + k:113 + k], scale=SCALE,
                                             accum_out=stat[:, 120 + k:121 + k]).then_inc(s["exp_done"], 1)

            for u in range(U_UPH):
                evacuate(u)
                if u == AT_LEVEL0 + LEVELS - 1:
                    act.wait_ge(s["lvl_done"], LEVELS)
                    nc.scalar.activation(sc_off, big[:, 0:1024].rearrange("p (h t) -> p h t", h=HEADS),
                                         ACT.Copy).then_inc(s["off_copied"], 1)
                if u == AT_O:
                    act.wait_ge(s["o_ready"], 1)
                    act.wait_ge(s["roped"], 8)
                    nc.scalar.activation(work[:, :], big[:, :], ACT.Square).then_inc(s["osq_done"], 1)
                    act.wait_ge(s["oms_ready"], 1)
                    nc.scalar.activation(stat[:, 48:64], stat[:, 48:64], ACT.Sqrt).then_inc(s["oroot_ready"], 1)
                if u == AT_OT:
                    act.wait_ge(s["oT_ready"], 1)
                    act.wait_ge(s["lvl_done"], LEVELS)
                    nc.scalar.activation(oh_T, big[:, :], ACT.Copy, scale=learnt("g_hgrn"))\
                      .then_inc(s["oh_done"], 1)
                for r, at in enumerate(AT_ATT):
                    if u == at:
                        softmax(r)
                    if u == at + 2:
                        act.wait_ge(s["pv_ready"], r + 1)
                        nc.scalar.activation(om_T[:, 1024 * r:1024 * (r + 1)], mid[:, :], ACT.Copy)\
                          .then_inc(s["om_done"], 1)

            for b in range(2):
                act.wait_ge(bank_free[b], U_END // 2)
            squares(1, h_tok, x_t)
            root(1)
            act.wait_ge(s["gexp_in"], 1)
            ge = rt[:, 72:80]
            nc.scalar.activation(ge, ge, ACT.Exp).then_inc(s["gexp_out"], 1)
            act.wait_ge(s["wexp_in"], 1)
            we = rt[:, 200:202]
            nc.scalar.activation(we, we, ACT.Exp).then_inc(s["wexp_out"], 1)

            act.wait_ge(s["tab_ready"], 1)
            for j in range(1, DC, 2):
                act.wait_ge(s["gather_bank"], j + 1)
                nc.scalar.activation(xg_T[:, j, 0:SLOTS], big[:, 512 * (j % 4):512 * (j % 4 + 1)], ACT.Copy,
                                     scale=learnt("g_ffn")[:, j:j + 1]).then_inc(s["gathered_act"], 1)

            with act.Fori(0, EXPERTS) as e:
                first = act.value_load(tab[0:1, bass.ds(e, 1)], min_val=0, max_val=SLOTS)
                last = act.value_load(tab[0:1, bass.ds(e + 1, 1)], min_val=0, max_val=SLOTS)
                slot0 = act.value_load(tab[0:1, bass.ds(e + SLOT0, 1)], min_val=0, max_val=SLOTS)
                with act.Fori(first, last) as n:
                    slot = nc.s_assert_within(slot0 + (n - first) * WIN, 0, SLOTS,
                                              skip_runtime_bounds_check_because="an expert's last pass starts below its last slot")
                    act.wait_ge(s["gate_done"], n + 1)
                    act.wait_ge(s["hid_ready"], n)
                    nc.scalar.activation(silu_g, acc[0][0:WIN, :], ACT.Silu).then_inc(s["silu_done"], 1)
                    act.wait_ge(s["y_stored"], n * 16)
                    for b in range(2):
                        act.wait_ge(s["y_done"], n * 4 + b + 1)
                        nc.scalar.activation(y_sb[:, 512 * b:512 * (b + 1)], big[0:WIN, 512 * b:512 * (b + 1)],
                                             ACT.Copy).then_inc(s["y_act"], 1)
                    act.wait_ge(s["y_act"], n * 2 + 2)
                    act.wait_ge(s["y_dve"], n * 2 + 2)
                    act.dma_start(y_rows[bass.ds(slot, WIN), :], y_sb).then_inc(s["y_stored"], 16)

            act.wait_ge(s["comb_out"], 8)
            squares(2, hp_tok, x_t)
            root(2)
            for v in range(8):
                act.wait_ge(s["p_ready"], v + 1)
                if v >= 2:
                    act.wait_ge(s["p_out"], v - 1)
                nc.scalar.activation(sig_p[:, v % 2, :], big[:, 512 * (v % 2):512 * (v % 2 + 1)],
                                     ACT.Sigmoid).then_inc(s["p_out_act"], 1)
            act.wait_ge(s["p_out"], 8)
            squares(3, hp_tok, x_t)
            root(3)

        @block.vector
        def _(dve):
            count = [0]
            tt, ts, stt = nc.vector.tensor_tensor, nc.vector.tensor_scalar, nc.vector.scalar_tensor_tensor

            def then(ins):
                count[0] += 1
                ins.then_inc(dve_step, 1)
                dve.wait_ge(dve_step, count[0])

            def normed(n, into, src):
                dve.wait_ge(s["sq_done"], 2 * (n + 1))
                r = stat[:, 8 + 2 * n:10 + 2 * n]
                ts(r, stat[:, 2 * n:2 * n + 2], 1.0 / D, EPS, ALU.mult, ALU.add).then_inc(s["ms_ready"], 1)
                dve.wait_ge(s["root_ready"], n + 1)
                then(nc.vector.reciprocal(r, r))
                if into is not None:
                    for t in range(TT):
                        ts(into[:, t * D:(t + 1) * D], src[t], r[:, t:t + 1], None, ALU.mult)\
                            .then_inc(s["h_ready"], 1)
                return r

            def turned(n, gain):
                for j in range(DC):
                    dve.wait_ge(s["hT_bank"], DC * n + 2 * (j // 2) + 2)
                    q = (j // 2 % 4) * 512 + 256 * (j % 2)
                    ts(hT[:, j, :], big[:, q:q + 256], gain[:, j:j + 1], None, ALU.mult)\
                        .then_inc(s["hT_out"], 1)

            normed(0, arena[:, 0:4096], x_t)
            dve.wait_ge(consts_in, 48)
            turned(0, learnt("g_mix"))
            then(nc.vector.tensor_copy(mask[:, :, :], work[:, 0:7 * P].rearrange("p (n t) -> p n t", n=7)))

            lb = stat[:, 32:48]
            raw = learnt("lb_raw")
            then(tt(stat[:, 64:72], raw[:, 0:8], raw[:, 8:16], ALU.max))
            then(tt(lb[:, 0:8], raw[:, 0:8], stat[:, 64:72], ALU.subtract))
            tt(lb[:, 8:16], raw[:, 8:16], stat[:, 64:72], ALU.subtract).then_inc(s["lb_max"], 1)
            dve.wait_ge(s["lb_exp"], 1)
            then(tt(stat[:, 64:72], lb[:, 0:8], lb[:, 8:16], ALU.add))
            then(nc.vector.reciprocal(stat[:, 64:72], stat[:, 64:72]))
            then(tt(stat[:, 72:80], lb[:, 0:8], stat[:, 64:72], ALU.mult))
            then(tt(stat[:, 80:88], lb[:, 8:16], stat[:, 64:72], ALU.mult))
            lbv, lbc = stat[:, 72:80], stat[:, 80:88]

            def forget(u):
                dve.wait_ge(s["fk_sig"], u - U_HF + 1)
                dve.wait_ge(bank_free[u % 2], u // 2 + 1)
                for h in range(2 * (u - U_HF), 2 * (u - U_HF) + 2):
                    w = slice(TOK * h, TOK * (h + 1))
                    ts(f_T[:, w], f_T[:, w], lbc[:, h:h + 1], lbv[:, h:h + 1], ALU.mult, ALU.add)
                    ins = ts(k_T[:, w], k_T[:, w], lbc[:, h:h + 1], None, ALU.mult)
                then(ins)

            def rope(k):
                raw_u = (mq_T, mk_T)[k // 4][:, 512 * (k % 4):512 * (k % 4 + 1)].rearrange("p (h t) -> p h t", h=2)
                tmp = work[:, 0:512].rearrange("p (h t) -> p h t", h=2)
                wide = lambda n: const(n).unsqueeze(1).broadcast_to([P, 2, TOK])
                dve.wait_ge(s["rot_ready"], k + 1)
                rot_ps = mid[:, 0:512].rearrange("p (h t) -> p h t", h=2)
                then(tt(tmp, rot_ps, wide("sin"), ALU.mult))
                then(tt(raw_u, raw_u, wide("cos"), ALU.mult))
                ins = tt(raw_u, raw_u, tmp, ALU.add)
                ins.then_inc(s["roped"], 1)
                dve.wait_ge(s["roped"], k + 1)

            def level(n):
                dve.wait_ge(s["lvl_done"], n + 1)
                sc = xtok[:, 0:2048].rearrange("p (m t) -> p m t", m=16)
                ps = big[:, :].rearrange("p (m t) -> p m t", m=16)
                if n == 0:
                    then(tt(sc, ps, ident.unsqueeze(1).broadcast_to([P, 16, P]), ALU.mult))
                    tt(q_T, q_T, f_T, ALU.mult).then_inc(s["lvl_ready"], 1)
                    dve.wait_ge(s["lvl_ready"], n + 2)
                    return
                if n < LEVELS - 1:
                    L = 1 << (n - 1)
                    then(nc.vector.copy_predicated(sc, mask[:, n - 1, :].unsqueeze(1).broadcast_to([P, 16, P]), ps))
                    m = HEADS * TOK // (2 * L)
                    two = lambda ap: ap.rearrange("p (m two l) -> p m two l", m=m, two=2)
                    qv, kv = two(q_T), two(k_T)
                    tot = spans[n - 1][:, 0:2 * m].rearrange("p (m two) -> p m two", two=2)
                    wide = lambda k: tot[:, :, k:k + 1].broadcast_to([P, m, L])
                    then(tt(qv[:, :, 1, :], qv[:, :, 1, :], wide(0), ALU.mult))
                    then(tt(kv[:, :, 0, :], kv[:, :, 0, :], wide(1), ALU.mult))
                    if n < LEVELS - 2:
                        then(tt(spans[n][:, 0:m], tot[:, :, 0], tot[:, :, 1], ALU.mult))
                    ts(stat[:, 188:189], lbv[:, 0:1], 1.0, None, ALU.mult).then_inc(s["lvl_ready"], 1)

            def hgrn_norm():
                dve.wait_ge(s["osq_done"], 1)
                r = stat[:, 48:64]
                then(nc.vector.tensor_reduce(r, work[:, :].rearrange("p (m v) -> p m v", m=16), AX.X, ALU.add))
                ts(r, r, 1.0 / P, EPS, ALU.mult, ALU.add).then_inc(s["oms_ready"], 1)
                dve.wait_ge(s["oroot_ready"], 1)
                then(nc.vector.reciprocal(r, r))
                wv = work[:, :].rearrange("p (m v) -> p m v", m=16)
                then(tt(wv, big[:, :].rearrange("p (m v) -> p m v", m=16),
                        r.unsqueeze(2).broadcast_to([P, 16, P]), ALU.mult))
                tt(work[:, :], work[:, :], og_tok, ALU.mult).then_inc(s["on_ready"], 1)

            def scores(r):
                dve.wait_ge(s["s_ready"], r + 1)
                sm = xtok[:, 1536 * r:1536 * (r + 1)].rearrange("p (h b s) -> p h b s", h=4, b=3)
                ps = big[:, :].rearrange("p (h b s) -> p h b s", h=4, b=4)
                bias = const("causal").unsqueeze(1).unsqueeze(1).broadcast_to([P, 4, 2, P])
                tt(sm[:, :, 0:3:2, :], ps[:, :, 0:3:2, :], bias, ALU.add)
                then(nc.vector.tensor_copy(sm[:, :, 1, :], ps[:, :, 1, :]))
                flat = xtok[:, 1536 * r:1536 * (r + 1)].rearrange("p (h s) -> p h s", h=4)
                mx = stat[:, 112:120]
                nc.vector.tensor_reduce(mx[:, 0:4], flat[:, :, 0:128], AX.X, ALU.max)
                then(nc.vector.tensor_reduce(mx[:, 4:8], flat[:, :, 128:384], AX.X, ALU.max))
                ts(mx, mx, -SCALE, None, ALU.mult).then_inc(s["mx_ready"], 1)
                dve.wait_ge(s["exp_done"], 8 * (r + 1))
                rs = stat[:, 120:128]
                then(nc.vector.reciprocal(rs, rs))
                then(tt(flat[:, :, 0:128], flat[:, :, 0:128], rs[:, 0:4].unsqueeze(2).broadcast_to([P, 4, 128]), ALU.mult))
                tt(flat[:, :, 128:384], flat[:, :, 128:384], rs[:, 4:8].unsqueeze(2).broadcast_to([P, 4, 256]),
                   ALU.mult).then_inc(s["pn_ready"], 1)

            def probs_out(r):
                dve.wait_ge(s["pT_ready"], r + 1)
                if r:
                    dve.wait_ge(s["pv_ready"], r)
                nc.vector.tensor_copy(probs_T.rearrange("p (h s) -> p h s", h=4),
                                      big[:, :].rearrange("p (h s) -> p h s", h=4)[:, :, 0:384])\
                    .then_inc(s["pT_out"], 1)

            for u in range(U_UPH):
                if U_HF <= u < U_HI:
                    forget(u)
                    if u == U_HI - 1:
                        ts(stat[:, 188:189], lbv[:, 0:1], 1.0, None, ALU.mult).then_inc(s["lvl_ready"], 1)
                if AT_LEVEL0 <= u < AT_LEVEL0 + LEVELS - 1:
                    level(u - AT_LEVEL0)
                if U_MQ < u <= U_MV:
                    rope(u - 1 - U_MQ)
                if u == AT_O:
                    hgrn_norm()
                for r, at in enumerate(AT_ATT):
                    if u == at:
                        scores(r)
                    if u == at + 1:
                        probs_out(r)

            for u in range(U_UPH, U_OUT):
                dve.wait_ge(unit_ready, u + 1)
                if u == U_UPH:
                    dve.wait_ge(bank_free[1], U_UPH // 2)
                    dve.wait_ge(bank_free[0], U_UPH // 2)
                w = slice(512 * ((u - U_UPH) % 8), 512 * ((u - U_UPH) % 8 + 1))
                if u < U_UPM:
                    ins = tt(gate_a[:, w], gate_a[:, w], acc[u % 2][:, :], ALU.mult)
                    ins.then_inc(bank_free[u % 2], 1)
                    dve.wait_ge(bank_free[u % 2], u // 2 + 1)
                else:
                    ins = tt(gate_b[:, w], gate_b[:, w], acc[u % 2][:, :], ALU.mult)
                    ins.then_inc(bank_free[u % 2], 1)
                    dve.wait_ge(bank_free[u % 2], u // 2 + 1)
                    tt(gate_a[:, w], gate_a[:, w], gate_b[:, w], ALU.add).then_inc(s["merged_ready"], 1)
            dve.wait_ge(s["x_again"], 16 * TT)
            for u in range(U_OUT, U_END):
                dve.wait_ge(unit_ready, u + 1)
                c, t = (u - U_OUT) // 2, (u - U_OUT) % 2
                xs = x_t[t][:, 512 * c:512 * (c + 1)]
                tt(xs, xs, acc[u % 2][:, :], ALU.add).then_inc(bank_free[u % 2], 1)

            for b in range(2):
                dve.wait_ge(bank_free[b], U_END // 2)
            normed(1, h_tok, x_t)
            turned(1, learnt("g_ffn"))

            dve.wait_ge(s["logits_ready"], 1)
            lg = rt[:, 0:72].rearrange("p (t e) -> p t e", t=TT)
            then(nc.vector.tensor_copy(lg, mid[:, 0:72].rearrange("p (t e) -> p t e", t=TT)))
            g_l, e_l = lg[:, :, 0:GROUPS], lg[:, :, GROUPS:36]
            ge = rt[:, 72:80].rearrange("p (t g) -> p t g", t=TT)
            gmax, pg = rt[:, 80:82], rt[:, 82:84]
            wide = lambda ap, n: ap.unsqueeze(2).broadcast_to([P, TT, n])
            desc = const("desc")

            def first_max(vals, top, onehot, n):
                down_counting = desc[:, 8 - n:8].unsqueeze(1).broadcast_to([P, TT, n])
                then(nc.vector.tensor_reduce(top, vals, AX.X, ALU.max))
                then(tt(onehot, vals, wide(top, n), ALU.is_equal))
                then(tt(onehot, onehot, down_counting, ALU.mult))
                then(nc.vector.tensor_reduce(rt[:, 84:86], onehot, AX.X, ALU.max))
                then(tt(onehot, onehot, wide(rt[:, 84:86], n), ALU.is_equal))

            goh = rt[:, 86:94].rearrange("p (t g) -> p t g", t=TT)
            first_max(g_l, gmax, goh, GROUPS)
            tt(ge, g_l, wide(gmax, GROUPS), ALU.subtract).then_inc(s["gexp_in"], 1)
            dve.wait_ge(s["gexp_out"], 1)
            then(nc.vector.tensor_reduce(pg, ge, AX.X, ALU.add))
            then(nc.vector.reciprocal(pg, pg))
            grid = [P, TT, GROUPS, PER_GROUP]
            prod = rt[:, 96:160].rearrange("p (t g i) -> p t g i", t=TT, g=GROUPS)
            for t in range(TT):
                then(tt(prod[:, t], e_l[:, t, :].rearrange("p (g i) -> p g i", g=GROUPS),
                        goh[:, t, :].unsqueeze(2).broadcast_to([P, GROUPS, PER_GROUP]), ALU.mult))
            e8 = rt[:, 160:176].rearrange("p (t i) -> p t i", t=TT)
            for t in range(TT):
                then(nc.vector.tensor_reduce(e8[:, t, :], prod[:, t].rearrange("p g i -> p i g"), AX.X, ALU.add))
            oh = [rt[:, 208 + 16 * k:224 + 16 * k].rearrange("p (t i) -> p t i", t=TT) for k in range(2)]
            tops = [rt[:, 196 + 2 * k:198 + 2 * k] for k in range(2)]
            first_max(e8, tops[0], oh[0], PER_GROUP)
            e8b = rt[:, 176:192].rearrange("p (t i) -> p t i", t=TT)
            then(stt(e8b, oh[0], -1e30, e8, ALU.mult, ALU.add))
            first_max(e8b, tops[1], oh[1], PER_GROUP)
            we = rt[:, 200:202]
            tt(we, tops[1], tops[0], ALU.subtract).then_inc(s["wexp_in"], 1)
            dve.wait_ge(s["wexp_out"], 1)
            w_k = [rt[:, 202 + 2 * k:204 + 2 * k] for k in range(2)]
            then(ts(w_k[0], we, 1.0, None, ALU.add))
            then(nc.vector.reciprocal(w_k[0], w_k[0]))
            then(tt(w_k[0], w_k[0], pg, ALU.mult))
            then(tt(w_k[1], w_k[0], we, ALU.mult))
            OH = [rt[:, 256 + 64 * k:320 + 64 * k].rearrange("p (t e) -> p t e", t=TT) for k in range(2)]
            both = rt[:, 384:448].rearrange("p (t e) -> p t e", t=TT)
            for k in range(2):
                for t in range(TT):
                    then(tt(OH[k][:, t, :].rearrange("p (g i) -> p g i", g=GROUPS),
                            goh[:, t, :].unsqueeze(2).broadcast_to([P, GROUPS, PER_GROUP]),
                            oh[k][:, t, :].unsqueeze(1).broadcast_to([P, GROUPS, PER_GROUP]), ALU.mult))
            tt(both, OH[0], OH[1], ALU.add).then_inc(s["onehot_ready"], 1)

            dve.wait_ge(s["counts_ready"], 1)
            cnt, incl, slot0 = rt[:, 448:480], rt[:, 480:512], rt[:, 512:544]
            pos = rt[:, 544:608].rearrange("p (t e) -> p t e", t=TT)
            then(nc.vector.tensor_copy(cnt, mid[:, 512:544]))
            then(nc.vector.tensor_tensor_scan(incl, ones[:, 0:EXPERTS], cnt, 0.0, ALU.mult, ALU.add))
            then(tt(slot0, incl, cnt, ALU.subtract))
            then(tt(pos, mid[:, 544:608].rearrange("p (t e) -> p t e", t=TT),
                    slot0.unsqueeze(1).broadcast_to([P, TT, EXPERTS]), ALU.add))
            slot_k = [rt[:, 608 + 2 * k:610 + 2 * k] for k in range(2)]
            tmp = rt[:, 612:676].rearrange("p (t e) -> p t e", t=TT)
            for k in range(2):
                then(tt(tmp, pos, OH[k], ALU.mult))
                then(nc.vector.tensor_reduce(slot_k[k], tmp, AX.X, ALU.add))
            npass, many = rt[:, 676:708], rt[:, 708:740]
            then(ts(npass, cnt, float(WIN), 1.0, ALU.is_gt, ALU.add))
            for m in range(2, TOK // WIN):
                then(stt(npass, cnt, float(WIN * m), npass, ALU.is_gt, ALU.add))
            then(nc.vector.tensor_tensor_scan(many, ones[:, 0:EXPERTS], npass, 0.0, ALU.mult, ALU.add))
            then(tt(npass, many, npass, ALU.subtract))
            then(nc.vector.tensor_copy(tab[0:1, 0:EXPERTS], npass[0:1, :]))
            then(nc.vector.tensor_copy(tab[0:1, EXPERTS:EXPERTS + 1], many[0:1, EXPERTS - 1:EXPERTS]))
            then(nc.vector.memset(tab[0:1, SLOT0 + EXPERTS:SLOT0 + EXPERTS + 1], 0))
            nc.vector.tensor_copy(tab[0:1, SLOT0:SLOT0 + EXPERTS], slot0[0:1, :]).then_inc(s["tab_ready"], 1)
            dve.wait_ge(s["iota_in"], 16)
            for t in range(TT):
                at = [slot_k[k][:, t:t + 1] for k in range(2)]
                wt = [w_k[k][:, t:t + 1] for k in range(2)]
                then(ts(sel[:, t, :], iota, at[0], None, ALU.is_equal))
                stt(sel[:, t, :], iota, at[1], sel[:, t, :], ALU.is_equal, ALU.add).then_inc(s["sel_ready"], 1)
            for t in range(TT):
                at = [slot_k[k][:, t:t + 1] for k in range(2)]
                wt = [w_k[k][:, t:t + 1] for k in range(2)]
                then(ts(selw[:, t, :], iota, at[0], wt[0], ALU.is_equal, ALU.mult))
                then(ts(work[:, 512:1024], iota, at[1], wt[1], ALU.is_equal, ALU.mult))
                tt(selw[:, t, :], selw[:, t, :], work[:, 512:1024], ALU.add).then_inc(s["sel_ready"], 1)
            for j in range(0, DC, 2):
                dve.wait_ge(s["gather_bank"], j + 1)
                ts(xg_T[:, j, 0:SLOTS], big[:, 512 * (j % 4):512 * (j % 4 + 1)], learnt("g_ffn")[:, j:j + 1],
                   None, ALU.mult).then_inc(s["gathered_dve"], 1)
            dve.wait_ge(s["selwT_ready"], 1)
            nc.vector.tensor_copy(selw_T, mid[:, :].rearrange("p (c t) -> p c t", c=4)).then_inc(s["selwT_out"], 1)

            with dve.Fori(0, EXPERTS) as e:
                first = dve.value_load(tab[0:1, bass.ds(e, 1)], min_val=0, max_val=SLOTS)
                last = dve.value_load(tab[0:1, bass.ds(e + 1, 1)], min_val=0, max_val=SLOTS)
                with dve.Fori(first, last) as n:
                    dve.wait_ge(s["up_done"], n + 1)
                    dve.wait_ge(s["silu_done"], n + 1)
                    tt(hid, silu_g, acc[1][0:WIN, :], ALU.mult).then_inc(s["hid_ready"], 1)
                    dve.wait_ge(s["hidT_ready"], n + 1)
                    nc.vector.tensor_copy(hid_T, mid[:, 0:FC * P].rearrange("p (c s) -> p c s", c=FC)[:, :, 0:WIN])\
                        .then_inc(s["hidT_out"], 1)
                    dve.wait_ge(s["y_stored"], n * 16)
                    for b in range(2, 4):
                        dve.wait_ge(s["y_done"], n * 4 + b + 1)
                        nc.vector.tensor_copy(y_sb[:, 512 * b:512 * (b + 1)], big[0:WIN, 512 * b:512 * (b + 1)])\
                            .then_inc(s["y_dve"], 1)

            for v in range(8):
                dve.wait_ge(s["comb_ready"], v + 1)
                n, t = v // 2, v % 2
                xs = x_t[t][:, 512 * n:512 * (n + 1)]
                tt(xs, xs, big[:, 512 * (v % 4):512 * (v % 4 + 1)], ALU.add).then_inc(s["comb_out"], 1)
            dve.wait_ge(s["comb_out"], 8)
            normed(2, hp_tok, x_t)
            turned(2, learnt("g_ple"))
            for v in range(8):
                n, t = v // 2, v % 2
                dve.wait_ge(s["p_out_act"], v + 1)
                xs = x_t[t][:, 512 * n:512 * (n + 1)]
                then(tt(sig_p[:, v % 2, :], sig_p[:, v % 2, :], big[:, 1024 + 512 * (v % 2):1536 + 512 * (v % 2)],
                        ALU.mult))
                tt(xs, xs, sig_p[:, v % 2, :], ALU.add).then_inc(s["p_out"], 1)
            dve.wait_ge(s["p_out"], 8)
            r = normed(3, None, x_t)
            dve.wait_ge(s["g_fin_in"], 16)
            for t in range(TT):
                stt(x_t[t], x_t[t], r[:, t:t + 1], g_fin, ALU.mult, ALU.mult).then_inc(s["fin_ready"], 1)

        @block.tensor
        def _(pe):
            mm = nc.tensor.matmul

            def turn(n, src):
                if n == 0:
                    pe.wait_ge(consts_in, 48)
                pe.wait_ge(s["h_ready"], TT * (n + 1))
                for j in range(DC):
                    if j >= 8:
                        pe.wait_ge(s["hT_out"], DC * n + 2 * (j // 2) - 6)
                    for t in range(TT):
                        rows = src[:, t * D:(t + 1) * D].rearrange("p (c j) -> p j c", j=DC)[:, j, :]
                        q = (j // 2 % 4) * 512 + 256 * (j % 2) + P * t
                        ins = nc.tensor.transpose(big[:, q:q + P], rows, ident)
                    ins.then_inc(s["hT_bank"], 1)

            def open_bank(u):
                if u >= 2:
                    pe.wait_ge(bank_free[u % 2], u // 2)

            def extras(u):
                n = u - AT_LEVEL0
                if 0 <= n < LEVELS:
                    level(n)
                if U_MQ < u <= U_MV:
                    k = u - 1 - U_MQ
                    raw_u = (mq_T, mk_T)[k // 4][:, 512 * (k % 4):512 * (k % 4 + 1)]
                    pe.wait_ge(bank_free[(u - 1) % 2], (u - 1) // 2 + 1)
                    if k:
                        pe.wait_ge(s["roped"], k)
                    mm(mid[:, 0:512], const("rot"), raw_u, start=True, stop=True).then_inc(s["rot_ready"], 1)
                if u == AT_O:
                    hgrn_out()
                if u == AT_OT:
                    pe.wait_ge(s["on_ready"], 1)
                    ov = big[:, :].rearrange("p (h t k) -> p h t k", h=HEADS, t=TT)
                    for h in range(HEADS):
                        for t in range(TT):
                            ins = nc.tensor.transpose(ov[:, h, t, :], work[:, t * HW + P * h:t * HW + P * (h + 1)], ident)
                    ins.then_inc(s["oT_ready"], 1)
                for r, at in enumerate(AT_ATT):
                    if u == at:
                        att_scores(r)
                    if u == at + 1:
                        att_turn(r)
                    if u == at + 2:
                        att_values(r)

            def level(n):
                pe.wait_ge(s["lvl_ready"], n + 1)
                if n == 0:
                    pe.wait_ge(bank_free[1], U_HI // 2)
                q_h, k_h = by_head(q_T), by_head(k_T)
                if n < LEVELS - 1:
                    for h in range(HEADS):
                        for b in range(2):
                            m = 2 * h + b
                            ins = mm(big[:, P * m:P * (m + 1)], k_h[:, h, P * b:P * (b + 1)],
                                     q_h[:, h, P * b:P * (b + 1)], start=True, stop=True)
                else:
                    for h in range(HEADS):
                        ins = mm(big[:, P * h:P * (h + 1)], k_h[:, h, 0:P], q_h[:, h, P:2 * P], start=True, stop=True)
                ins.then_inc(s["lvl_done"], 1)

            def hgrn_out():
                pe.wait_ge(s["off_copied"], 1)
                v = v_tok.rearrange("p (t c) -> p t c", t=TT)
                for t in range(TT):
                    for h in range(HEADS):
                        dst = big[:, t * HW + P * h:t * HW + P * (h + 1)]
                        if t:
                            mm(dst, sc_off[:, h, :], v[:, 0, P * h:P * (h + 1)], start=True, stop=False)
                        ins = mm(dst, sc_T[:, h, t, :], v[:, t, P * h:P * (h + 1)], start=not t, stop=True)
                ins.then_inc(s["o_ready"], 1)

            def att_scores(r):
                pe.wait_ge(s["roped"], 8)
                pe.wait_ge(s["oh_done"], 1) if r == 0 else pe.wait_ge(s["pT_out"], r)
                q_h, k_h = by_head(mq_T), by_head(mk_T)
                for i in range(4):
                    h, at = 4 * r + i, 512 * i
                    mm(big[:, at:at + 128], q_h[:, h, 0:P], k_h[:, h, 0:P], start=True, stop=True)
                    ins = mm(big[:, at + 128:at + 384], q_h[:, h, P:TOK], k_h[:, h, :], start=True, stop=True)
                ins.then_inc(s["s_ready"], 1)

            def att_turn(r):
                pe.wait_ge(s["pn_ready"], r + 1)
                pv = xtok[:, 1536 * r:1536 * (r + 1)].rearrange("p (h b s) -> p h b s", h=4, b=3)
                for i in range(4):
                    for b in range(3):
                        at = 512 * i + P * b
                        ins = nc.tensor.transpose(big[:, at:at + P], pv[:, i, b, :], ident)
                ins.then_inc(s["pT_ready"], 1)

            def att_values(r):
                pe.wait_ge(s["pT_out"], r + 1)
                if r == 0:
                    pe.wait_ge(bank_free[1], U_GA // 2)
                    pe.wait_ge(bank_free[0], U_GA // 2)
                else:
                    pe.wait_ge(s["om_done"], r)
                v = mv_tok.rearrange("p (t c) -> p t c", t=TT)
                pt_v = probs_T.rearrange("p (h s) -> p h s", h=4)
                for i in range(4):
                    h, at = 4 * r + i, TOK * i
                    mm(mid[:, at:at + TOK], v[:, 0, P * h:P * (h + 1)], pt_v[:, i, 0:TOK], start=True, stop=False)
                    ins = mm(mid[:, at + P:at + TOK], v[:, 1, P * h:P * (h + 1)], pt_v[:, i, TOK:384],
                             start=False, stop=True)
                ins.then_inc(s["pv_ready"], 1)

            turn(0, arena[:, 0:4096])
            pe.wait_ge(s["hT_out"], DC)
            u = 0
            for i in range(DENSE):
                pe.wait_ge(ring_full[i % RING], 16 * (i // RING + 1))
                buf = ring[i % RING]
                tokens_out = i in (4, 5, 6, 7, 12, 13) or i >= N_IN + N_UP
                if N_IN <= i < N_IN + N_UP:
                    w = buf[:, :].rearrange("p (k c) -> p k c", k=HEADS)
                    src = by_head(oh_T if i < N_IN + 2 else om_T)
                    if i == N_IN:
                        pe.wait_ge(s["oh_done"], 1)
                    if i == N_IN + 2:
                        pe.wait_ge(s["om_done"], 2)
                    for _ in range(4):
                        open_bank(u)
                        for c in range(2):
                            col = P * (2 * ((u - U_UPH) % 4) + c)
                            for k in range(HEADS):
                                ins = mm(acc[u % 2][:, TOK * c:TOK * (c + 1)], w[:, k, col:col + P], src[:, k, :],
                                         start=k == 0, stop=k == HEADS - 1)
                        ins.then_inc(unit_ready, 1)
                        u += 1
                    ins = None
                    last_mm = None
                elif tokens_out:
                    w = buf[:, :].rearrange("p (k c) -> p k c", k=DC)
                    if i == N_IN + N_UP:
                        pe.wait_ge(s["merged_ready"], 8)
                        src = gate_a.rearrange("p (c t) -> p c t", c=DC)
                    elif i < N_IN:
                        src = hT
                    for t in range(TT):
                        open_bank(u)
                        for k in range(DC):
                            ins = mm(acc[u % 2][:, :], src[:, k, P * t:P * (t + 1)], w[:, k, :],
                                     start=k == 0, stop=k == DC - 1)
                        ins.then_inc(unit_ready, 1)
                        u += 1
                        if u - 1 < U_UPH:
                            extras(u - 1)
                else:
                    w = buf[:, :].rearrange("p (k c) -> p k c", k=DC)
                    for half in range(2):
                        open_bank(u)
                        for c in range(2):
                            col = P * (2 * half + c)
                            for k in range(DC):
                                ins = mm(acc[u % 2][:, TOK * c:TOK * (c + 1)], w[:, k, col:col + P], hT[:, k, :],
                                         start=k == 0, stop=k == DC - 1)
                        ins.then_inc(unit_ready, 1)
                        u += 1
                        extras(u - 1)
                assert u == units_through(i)
            assert u == U_END

            turn(1, h_tok)
            pe.wait_ge(s["hT_out"], 2 * DC)
            pe.wait_ge(s["router_in"], 16)
            for t in range(TT):
                for j in range(DC):
                    ins = mm(mid[:, 36 * t:36 * (t + 1)], hT[:, j, P * t:P * (t + 1)], wr[:, j, :],
                             start=j == 0, stop=j == DC - 1)
            ins.then_inc(s["logits_ready"], 1)
            pe.wait_ge(s["onehot_ready"], 1)
            both = rt[:, 384:448].rearrange("p (t e) -> p t e", t=TT)
            before = const("before")
            mm(mid[:, 512:544], ones, both[:, 0, :], start=True, stop=False)
            mm(mid[:, 512:544], ones, both[:, 1, :], start=False, stop=True)
            mm(mid[:, 544:576], before, both[:, 0, :], start=True, stop=True)
            mm(mid[:, 576:608], before, both[:, 1, :], start=True, stop=False)
            mm(mid[:, 576:608], ones, both[:, 0, :], start=False, stop=True).then_inc(s["counts_ready"], 1)
            pe.wait_ge(s["sel_ready"], TT)
            for j in range(DC):
                if j >= 4:
                    pe.wait_ge(s["gathered_act" if j % 2 else "gathered_dve"], (j - 4) // 2 + 1)
                for t in range(TT):
                    rows = h_tok[:, t * D:(t + 1) * D].rearrange("p (c j) -> p j c", j=DC)[:, j, :]
                    ins = mm(big[:, 512 * (j % 4):512 * (j % 4 + 1)], rows, sel[:, t, :], start=t == 0, stop=t == 1)
                ins.then_inc(s["gather_bank"], 1)
            pe.wait_ge(s["sel_ready"], 2 * TT)
            for c in range(4):
                for t in range(TT):
                    ins = nc.tensor.transpose(mid[:, TOK * c + P * t:TOK * c + P * (t + 1)],
                                              selw[:, t, P * c:P * (c + 1)], ident)
            ins.then_inc(s["selwT_ready"], 1)
            pe.wait_ge(s["selwT_out"], 1)
            pe.wait_ge(s["gathered_act"], DC // 2)
            pe.wait_ge(s["gathered_dve"], DC // 2)
            pe.wait_ge(s["padded"], 2)

            with pe.Fori(0, EXPERTS) as e:
                first = pe.value_load(tab[0:1, bass.ds(e, 1)], min_val=0, max_val=SLOTS)
                last = pe.value_load(tab[0:1, bass.ds(e + 1, 1)], min_val=0, max_val=SLOTS)
                full0 = 16 * (DENSE // RING + 1)
                with pe.Fori(first, last) as n:
                    pe.wait_ge(s["win_ready"], n + 1)
                    for k, done in ((0, "gate_done"), (1, "up_done")):
                        pe.wait_ge(ring_full[k], e * 16 + full0)
                        w = ring[k][:, :].rearrange("p (j f) -> p j f", j=DC)
                        if k == 1:
                            pe.wait_ge(s["hid_ready"], n)
                        else:
                            pe.wait_ge(s["silu_done"], n)
                        for j in range(DC):
                            ins = mm(acc[k][0:WIN, :], win_T[:, j, :], w[:, j, :], start=j == 0, stop=j == DC - 1)
                        ins.then_inc(s[done], 1)
                    pe.wait_ge(s["hid_ready"], n + 1)
                    for c in range(FC):
                        ins = nc.tensor.transpose(mid[:, P * c:P * (c + 1)], hid_all[:, P * c:P * (c + 1)], ident)
                    ins.then_inc(s["hidT_ready"], 1)
                    pe.wait_ge(s["hidT_out"], n + 1)
                    pe.wait_ge(ring_full[2], e * 16 + full0)
                    w = ring[2][:, :].rearrange("p (c d) -> p c d", c=FC)
                    pe.wait_ge(s["y_act"], n * 2)
                    pe.wait_ge(s["y_dve"], n * 2)
                    for b in range(4):
                        for c in range(FC):
                            ins = mm(big[0:WIN, 512 * b:512 * (b + 1)], hid_T[:, c, :], w[:, c, 512 * b:512 * (b + 1)],
                                     start=c == 0, stop=c == FC - 1)
                        ins.then_inc(s["y_done"], 1)

            total = pe.value_load(tab[0:1, EXPERTS:EXPERTS + 1], min_val=1, max_val=SLOTS)
            pe.wait_ge(s["y_act"], total * 2)
            pe.wait_ge(s["y_dve"], total * 2)
            pe.wait_ge(s["y_back"], 16)
            for v in range(8):
                n, t = v // 2, v % 2
                if v >= 4:
                    pe.wait_ge(s["comb_out"], v - 3)
                for c in range(4):
                    ins = mm(big[:, 512 * (v % 4):512 * (v % 4 + 1)], selw_T[:, c, P * t:P * (t + 1)],
                             y_all[:, c, 512 * n:512 * (n + 1)], start=c == 0, stop=c == 3)
                ins.then_inc(s["comb_ready"], 1)
            pe.wait_ge(s["comb_out"], 8)
            turn(2, hp_tok)
            pe.wait_ge(s["hT_out"], 3 * DC)
            pe.wait_ge(s["ple_in"], 32)
            for i in range(N_PLE):
                slot = i % RING
                pe.wait_ge(ring_full[slot], 16 * (DENSE // RING + EXPERTS + i // RING + 1))
                w = ring[slot][:, :].rearrange("p (k c) -> p k c", k=DC)
                for t in range(TT):
                    v = 2 * i + t
                    if v >= 2:
                        pe.wait_ge(s["p_out"], v - 1)
                    for k in range(2):
                        mm(big[:, 1024 + 512 * (v % 2):1536 + 512 * (v % 2)], p_T[:, k, P * t:P * (t + 1)],
                           proj_sb[:, k, 512 * i:512 * (i + 1)], start=k == 0, stop=k == 1)
                    for k in range(DC):
                        ins = mm(big[:, 512 * (v % 2):512 * (v % 2 + 1)], hT[:, k, P * t:P * (t + 1)], w[:, k, :],
                                 start=k == 0, stop=k == DC - 1)
                    ins.then_inc(s["p_ready"], 1)


def shape_constants():
    half = P // 2
    inv = 10000.0 ** (-np.arange(half, dtype=np.float32) / half)
    ang = np.arange(TOK, dtype=np.float32)[None, :] * inv.astype(np.float32)[:, None]
    cos = np.concatenate([np.cos(ang), np.cos(ang)], 0)
    sin = np.concatenate([np.sin(ang), np.sin(ang)], 0)
    rot = np.zeros((P, P), np.float32)
    for d in range(half):
        rot[d + half, d] = -1.0
        rot[d, d + half] = 1.0
    i = np.arange(P)
    parts = dict(ident=np.eye(P), rot=rot, cos=cos, sin=sin,
                 causal=np.where(i[None, :] <= i[:, None], 0.0, -1e30),
                 before=(i[:, None] < i[None, :]), ones=np.ones((P, P)),
                 desc=np.tile(np.arange(8, 0, -1), (P, 1)))
    consts = np.concatenate([np.asarray(parts[n], np.float32) for n in CONSTS], 1)
    masks = np.zeros((P, 7, P), np.float32)
    for n in range(7):
        span = i >> n
        masks[:, n, :] = (span[:, None] % 2 == 0) & (span[None, :] == span[:, None] + 1)
    return np.ascontiguousarray(consts), masks.reshape(P, 7 * P), np.arange(SLOTS, dtype=np.float32)[None, :]


def kernel(x, p, norm_mix_g, w_in, hgrn_lb_raw, hgrn_norm_g, w_up_hgrn, w_up_moba, w_out, norm_ffn_g,
           w_router_group, w_router_expert, w_exp_gate, w_exp_up, w_exp_down, norm_ple_g, w_ple_gate,
           w_ple_proj, norm_final_g):
    import concourse.bacc as bacc
    from concourse.bass_utils import run_bass_kernel_spmd

    a = np.asarray
    split = lambda w, n: a(w).reshape(P, DC, n, 512).transpose(2, 0, 1, 3).reshape(n, P, PIECE)
    plain = lambda w, k, n, c: a(w).reshape(k, P, n, c).transpose(2, 1, 0, 3).reshape(n, P, PIECE)
    pieces = np.concatenate([split(w_in[0], N_IN), plain(w_up_hgrn[0], HEADS, 2, 1024),
                             plain(w_up_moba[0], HEADS, 2, 1024), plain(w_out[0], DC, 4, 512),
                             split(w_ple_gate[0], N_PLE)], 0)
    cols = lambda g: a(g).reshape(P, DC)
    learned = np.concatenate([cols(norm_mix_g), cols(norm_ffn_g), cols(norm_ple_g),
                              a(hgrn_norm_g).reshape(P, 1),
                              a(hgrn_lb_raw).reshape(2, HEADS, P).transpose(2, 0, 1).reshape(P, 16)], 1)
    router = np.concatenate([a(w_router_group[0]).reshape(P, DC, GROUPS),
                             a(w_router_expert[0]).reshape(P, DC, EXPERTS)], 2)
    pt = a(p).reshape(TOK, 2, P).transpose(2, 1, 0)
    proj = a(w_ple_proj[0]).reshape(2, P, D).transpose(1, 0, 2)
    consts, masks, iota_row = shape_constants()
    arrays = dict(x=a(x).reshape(TOK, D), pt=pt, pieces=pieces, ple_proj=proj, learned=learned, router=router,
                  consts=consts, iota_row=iota_row, masks=masks, w_gate=a(w_exp_gate[0]), w_up=a(w_exp_up[0]),
                  w_down=a(w_exp_down[0]), g_final=a(norm_final_g).reshape(1, D))
    nc = bacc.Bacc("TRN2", target_bir_lowering=False, num_devices=1)
    arrays = {n: np.ascontiguousarray(v) for n, v in arrays.items()}
    aps = [nc.dram_tensor("in_" + n, v.shape, mybir.dt.from_np(v.dtype), kind="ExternalInput").ap()
           for n, v in arrays.items()]
    out = nc.dram_tensor("out", (TOK, D), F32, kind="ExternalOutput").ap()
    build_layer(nc, *aps, out)
    r = run_bass_kernel_spmd(nc, [{"in_" + n: v for n, v in arrays.items()}], core_ids=[0])
    return r.results[0]["out"].reshape(1, TOK, D)
```

```python
from contextlib import ExitStack

import concourse.bass as bass
import numpy as np
from concourse import mybir

F32 = mybir.dt.float32
F32R = mybir.dt.float32r
I32 = mybir.dt.int32
U8 = mybir.dt.uint8
ALU = mybir.AluOpType
ACT = mybir.ActivationFunctionType
AX = mybir.AxisListType

P = 128
TOK = 256
TT = TOK // P
D = 2048
DC = D // P
HEADS = 8
HW = HEADS * P
EXPERTS, GROUPS = 32, 4
PER_GROUP = EXPERTS // GROUPS
FE = 512
FC = FE // P
SLOTS = 2 * TOK
WIN = 64
PLE = 256
EPS = 1e-6
SCALE = float(P) ** -0.5
RING = 3
HALF = 4096
BITE = 1024
PER_HALF = HALF // BITE
BUFS = 4
MAX_PASSES = EXPERTS + SLOTS // WIN
MAX_PAIRS = MAX_PASSES // 2
TIMES = MAX_PASSES + 2

N_IN, N_UP, N_OUT, N_PLE = 22, 8, 4, 4
IN_BITES, UP_BITES = DC // 2, HEADS // 2
FIRST_UP = N_IN * IN_BITES
FIRST_OUT = FIRST_UP + N_UP * UP_BITES
DENSE = FIRST_OUT + N_OUT * IN_BITES
PASS = 24
PAIR = 2 * PASS
assert DENSE % (PER_HALF * RING) == 0 and PASS % (PER_HALF * RING) == 0
DENSE_HALVES, PLE_HALVES = DENSE // PER_HALF, N_PLE * IN_BITES // PER_HALF
U_HF, U_HI, U_HOG, U_MQ, U_MV, U_GA, U_GB, U_UPH, U_UPM, U_OUT, U_END = (
    4, 8, 12, 16, 24, 28, 36, 44, 52, 60, 68)
LEVELS = 9
AT_LEVEL, LEVEL_STEP = 36, 6
AT_O, AT_OT, AT_ATT = 104, 114, (122, 144)
GU, DOWN = 16, 8
FIRST_AT, PAIR_AT = (0, GU), (0, PASS)
AT_FOLD_G, AT_FOLD_U, AT_SELT = 12, 20, 16
AT_GATE_OUT, AT_SILU, AT_UP_OUT, AT_HID, AT_SELT_OUT = 11, 16, 19, 24, 21
AT_Y, AT_COMB = 2, 2
LAG = 3

CONSTS = dict(ident=128, rot=128, cos=256, sin=256, causal=128, before=128, ones=128, zeros=64, desc=8, fold=64, times=42)
LEARNED = dict(g_mix=16, g_ffn=16, g_ple=16, g_hgrn=1, lb_raw=16)


def last_bite(block):
    return block * IN_BITES + IN_BITES - 1 if block < N_IN else (
        FIRST_UP + (block - N_IN + 1) * UP_BITES - 1 if block < N_IN + N_UP
        else FIRST_OUT + (block - N_IN - N_UP + 1) * IN_BITES - 1)


def at_rotate(k):
    return last_bite(U_MQ // 2 + k // 2) + 4 + 2 * (k % 2)


def block_ending(g):
    for block in range(N_IN + N_UP + N_OUT):
        if last_bite(block) == g:
            return block
    return None


def columns(table):
    out, at = {}, 0
    for name, n in table.items():
        out[name] = (at, at + n)
        at += n
    return out, at


CONST_AT, N_CONST = columns(CONSTS)
LEARNED_AT, N_LEARNED = columns(LEARNED)


def build_layer(nc, x, pt, halves, ple_proj, learned, router, consts, iota_row, masks, w_gate, w_up,
                w_down, g_final, out):
    gate_v = w_gate.rearrange("e (p j) f -> e p (j f)", p=P).rearrange("e p (two f) -> two e p f", two=2)
    up_v = w_up.rearrange("e (p j) f -> e p (j f)", p=P).rearrange("e p (two f) -> two e p f", two=2)
    down_v = w_down.rearrange("e (two c p) d -> two e p c d", two=2, p=P)

    with ExitStack() as ctx:
        def sb(name, shape, dt=F32):
            return ctx.enter_context(nc.sbuf_tensor(name, shape, dt))

        def sem(name):
            return ctx.enter_context(nc.semaphore(name))

        ring = [sb(f"ring{n}", [P, HALF]) for n in range(RING)]
        bite_hi = sb("bite_hi", [P, BUFS * BITE], F32R)
        bite_lo = sb("bite_lo", [P, BUFS * BITE], F32R)
        xtok = sb("xtok", [P, TT * D])
        hT_all = sb("hT_all", [P, 2 * DC * TOK])
        hT_at = nc.sbuf_base - 4 * 2 * DC * TOK
        arena = sb("arena", [P, 16384])
        arena_at = nc.sbuf_base - 4 * 16384
        work = sb("work", [P, 2048])

        def over(name, base, first, n, dt=F32R):
            return nc.alloc_sbuf_tensor_at(name, [P, n], dt, offset=base + 4 * first)
        cst = sb("cst", [P, N_CONST])
        lrn = sb("lrn", [P, N_LEARNED])
        mask = sb("mask", [P, 7, P], U8)
        stat = sb("stat", [P, 192])

        def const(name):
            a, b = CONST_AT[name]
            return cst[:, a:b]

        def learnt(name):
            a, b = LEARNED_AT[name]
            return lrn[:, a:b]

        ident, ones = const("ident"), const("ones")
        x_t = [xtok[:, t * D:(t + 1) * D] for t in range(TT)]
        chunks = lambda ap, n: ap.rearrange("p (j t) -> p j t", j=n)
        hT_hi = chunks(over("hT_hi", hT_at, 0, DC * TOK)[:, :], DC)
        hT_lo = chunks(over("hT_lo", hT_at, DC * TOK, DC * TOK)[:, :], DC)
        merged_hi, merged_lo = hT_hi, hT_lo
        hT = chunks(hT_all[:, 0:DC * TOK], DC)

        def slab(n, k=1):
            return arena[:, 2048 * n:2048 * (n + k)]

        q_T, k_T, f_T = slab(0), slab(1), slab(2)
        v_tok, og_tok, mq_T, mk_T, mv_tok = slab(3), slab(4), slab(5), slab(6), slab(7)
        by_head = lambda ap: ap.rearrange("p (h t) -> p h t", h=HEADS)
        gate_a, gate_b = slab(1, 2), slab(5, 2)
        oh_hi, oh_lo = over("oh_hi", arena_at, 0, 2048), over("oh_lo", arena_at, 3 * 2048, 2048)
        om_hi, om_lo = over("om_hi", arena_at, 4 * 2048, 2048), over("om_lo", arena_at, 7 * 2048, 2048)
        probs_T = og_tok[:, 0:4 * 384]
        sc_T = xtok[:, 0:2048].rearrange("p (h b t) -> p h b t", h=HEADS, b=2)
        sc_off = xtok[:, 2048:3072].rearrange("p (h t) -> p h t", h=HEADS)
        spans = [f_T, xtok[:, 3072:4096], f_T[:, 0:512], f_T[:, 512:768], f_T[:, 768:896],
                 f_T[:, 896:960], f_T[:, 960:992]]
        h_tok = arena[:, 0:4096]
        XW = SLOTS + WIN
        steps = cst[:, CONST_AT["ones"][0] + WIN:CONST_AT["zeros"][0] + WIN]
        xg_T = arena[:, 4096:4096 + DC * XW].rearrange("p (j s) -> p j s", j=DC)
        wr = arena[:, 14336:14336 + DC * 36].rearrange("p (j e) -> p j e", j=DC)
        rt = arena[:, 15360:16384]
        win = [over(f"win{a}", *at, DC * P)[:, :].rearrange("p (j s) -> p j s", j=DC)
               for a, at in enumerate(((arena_at, 0), (hT_at, 2048)))]
        gu_sb = arena[:, 2048:3072]
        hid_hi = [over(f"hid_hi{a}", *at, FC * P)[:, :].rearrange("p (c s) -> p c s", c=FC)
                  for a, at in enumerate(((arena_at, 3072), (hT_at, 0)))]
        hid_lo = [over(f"hid_lo{a}", *at, FC * P)[:, :].rearrange("p (c s) -> p c s", c=FC)
                  for a, at in enumerate(((arena_at, 3584), (hT_at, 512)))]
        rows_of = [slice(WIN * a, WIN * (a + 1)) for a in range(2)]
        silu_g = arena[:, 14336:14592]
        hid = arena[:, 14592:14848]
        table = hT_all[0:1, 2048:2048 + TIMES * EXPERTS].rearrange("p (n e) -> p n e", e=EXPERTS)
        sel = hT_all[:, 4096:5120].rearrange("p (t s) -> p t s", t=TT)
        selw = hT_all[:, 5120:5120 + TT * XW].rearrange("p (t s) -> p t s", t=TT)
        part0 = 5120 + TT * XW
        sel_cols = hT_all[:, part0:part0 + 256].rearrange("p (t s) -> p t s", t=TT)
        own = hT_all[:, part0 + 256:part0 + 384]
        sel_pair = hT_all[:, part0 + 384:part0 + 640].rearrange("p (t s) -> p t s", t=TT)
        sel_T = hT_all[:, part0 + 640:part0 + 896].rearrange("p (t s) -> p t s", t=TT)
        iota = work[:, 0:SLOTS]
        wait_taker = hT_all[0:1, part0 + 896:part0 + 897]
        y_sb = work[:, :]
        table_2 = work[0:1, 512:512 + TIMES * EXPERTS].rearrange("p (n e) -> p n e", e=EXPERTS)
        hp_tok = arena[:, 8192:12288]
        proj_sb = arena[:, 4096:8192].rearrange("p (c d) -> p c d", c=2)
        p_T = work[:, 0:512].rearrange("p (c t) -> p c t", c=2)
        sig_p = work[:, 512:1536].rearrange("p (b d) -> p b d", b=2)
        g_fin = arena[:, 0:2048]

        tab = sb("tab", [1, 3 * TIMES + 2], I32)
        EXPERT_OF, SLOT_OF, OFF_OF, PASSES, PAIRS = 0, TIMES, 2 * TIMES, 3 * TIMES, 3 * TIMES + 1

        acc = [ctx.enter_context(nc.psum_tensor(f"acc{b}", [P, 512], F32)) for b in range(2)]
        mid = ctx.enter_context(nc.psum_tensor("mid", [P, 1024], F32))
        big = ctx.enter_context(nc.psum_tensor("big", [P, 2048], F32))

        raw_in = [sem(f"raw_in{n}") for n in range(RING)]
        x_in = [sem(f"x_in{t}") for t in range(TT)]
        consts_in = sem("consts_in")
        hi_ready, lo_ready = sem("hi_ready"), sem("lo_ready")
        bite_used = sem("bite_used")
        first_ready = sem("first_ready")
        bank_free = [sem(f"bank_free{b}") for b in range(2)]
        dve_step = sem("dve_step")
        act_step = sem("act_step")
        names = ("sq_done ms_ready root_ready h_ready hT_bank hT_hi_out hT_out rot_ready roped "
                 "fk_sig lvl_ready lvl_done off_copied o_ready osq_done oms_ready oroot_ready on_ready oT_ready "
                 "oh_hi_out oh_done s_ready mx_ready exp_done pn_ready pT_ready pT_out pv_ready om_out om_hi_out "
                 "om_done lb_exp lb_max sum_ready merged_hi_out merged_ready x_again router_in logits_ready "
                 "gexp_in gexp_out wexp_in wexp_out onehot_ready counts_ready sel_ready big_filled "
                 "big_act big_dve padded tab_ready win_hi_out win_ready cols_ready pair_ready selT_ready selT_out gu_out folded "
                 "silu_done hid_hi_out hid_ready iota_in ple_in p_first "
                 "p_out_act p_out g_fin_in fin_ready stored").split()
        s = {n: sem(n) for n in names}

        block = ctx.enter_context(nc.Block())

        def p_bank(v):
            return acc[v % 2][:, :] if v // 2 % 2 == 0 else mid[:, 512 * (v % 2):512 * (v % 2 + 1)]

        def unit_stands(engine, u):
            if u % 2:
                engine.wait_ge(bite_used, last_bite(u // 2) + 1)
            else:
                engine.wait_ge(first_ready, u // 2 + 1)

        def pair_start(m):
            return m * PAIR + (DENSE - DOWN)

        def later(m, b):
            h = (DENSE - DOWN + b) // PER_HALF
            return (h % RING, b % PER_HALF, b % BUFS, m * (16 * PAIR // PER_HALF // RING) + landed(h),
                    m * PAIR + (DENSE - DOWN + b))

        def landed(half):
            return 16 * (half // RING + 1)

        @block.sync
        def _(sp):
            xv = x.rearrange("(t p) d -> t p d", p=P)
            for t in range(TT):
                sp.dma_start(x_t[t], xv[t]).then_inc(x_in[t], 16)

            def load_dense(i, slot):
                sp.dma_start(ring[slot][:, :], halves[i]).then_inc(raw_in[slot], 16)

            def load_expert(e, i, slot):
                if i < 4:
                    src = (gate_v, up_v)[i // 2][i % 2][bass.ds(e, 1)].rearrange("e p f -> (e p) f")
                    sp.dma_start(ring[slot][:, :], src).then_inc(raw_in[slot], 16)
                else:
                    src = down_v[i % 2][bass.ds(e, 1)].rearrange("e p c d -> (e p) c d")
                    sp.dma_start(ring[slot][:, :].rearrange("p (c d) -> p c d", c=2), src)\
                      .then_inc(raw_in[slot], 16)

            for h in range(DENSE_HALVES):
                if h >= RING:
                    sp.wait_ge(lo_ready, PER_HALF * (h - RING + 1))
                load_dense(h, h % RING)
                if h == (AT_ATT[1] + 20) // PER_HALF + 2:
                    sp.wait_ge(s["pT_ready"], 2)
                    for t in range(TT):
                        sp.dma_start(x_t[t], xv[t]).then_inc(s["x_again"], 16)
            for i in range(4):
                if i == RING:
                    sp.wait_ge(bite_used, FIRST_OUT)
                    sp.dma_start(wr, router).then_inc(s["router_in"], 16)
                    for b in range(2):
                        sp.wait_ge(bank_free[b], U_END // 2)
                    sp.dma_start(iota, iota_row.partition_broadcast(P)).then_inc(s["iota_in"], 16)
                sp.wait_ge(lo_ready, DENSE + PER_HALF * (i - RING + 1))
                load_expert(0, i, i % RING)
            sp.wait_ge(s["tab_ready"], 1)
            passes = sp.value_load(tab[0:1, PASSES:PASSES + 1], min_val=EXPERTS, max_val=MAX_PASSES)

            def load_pass(n, part):
                e = sp.value_load(tab[0:1, bass.ds(n + (EXPERT_OF - (part[0] >= 4)), 1)], min_val=0,
                                  max_val=EXPERTS - 1)
                for i in part:
                    sp.wait_ge(lo_ready, n * PASS + (DENSE - DOWN + PER_HALF * (i - RING + 1)))
                    load_expert(e, i, (i + 1) % RING)

            with sp.Fori(1, passes) as n:
                load_pass(n, range(4))
                load_pass(n, range(4, 6))
            e = sp.value_load(tab[0:1, bass.ds(passes + (EXPERT_OF - 1), 1)], min_val=0, max_val=EXPERTS - 1)
            for i in range(2):
                sp.wait_ge(lo_ready, passes * PASS + (DENSE - DOWN + PER_HALF * (i - RING + 1)))
                load_expert(e, 4 + i, (i + 1) % RING)

            def load_ple(i):
                sp.wait_ge(lo_ready, passes * PASS + (DENSE + PER_HALF * (i - RING + 1)))
                load_dense(DENSE_HALVES + i, i % RING)

            load_ple(0)
            sp.wait_ge(s["win_ready"], passes + 2)
            sp.dma_start(proj_sb, ple_proj).then_inc(s["ple_in"], 16)
            load_ple(1)
            load_ple(2)
            pairs = sp.value_load(tab[0:1, PAIRS:PAIRS + 1], min_val=EXPERTS // 2, max_val=MAX_PAIRS)
            sp.wait_ge(s["big_filled"], pairs * 8 + DC)
            sp.dma_start(p_T, pt).then_inc(s["ple_in"], 16)
            sp.dma_start(g_fin, g_final.partition_broadcast(P)).then_inc(s["g_fin_in"], 16)
            for i in range(RING, PLE_HALVES):
                load_ple(i)
            ov = out.rearrange("(t p) d -> t p d", p=P)
            for t in range(TT):
                sp.wait_ge(s["fin_ready"], t + 1)
                sp.dma_start(ov[t], x_t[t]).then_inc(s["stored"], 16)
            sp.wait_ge(s["stored"], 16 * TT)

        @block.gpsimd
        def _(pool):
            tt, copy = nc.gpsimd.tensor_tensor, nc.gpsimd.tensor_copy
            pool.wait_ge(s["om_out"], 2)
            copy(om_hi[:, :], work[:, :]).then_inc(s["om_hi_out"], 1)
            pool.wait_ge(s["om_hi_out"], 1)
            tt(om_lo[:, :], work[:, :], om_hi[:, :].bitcast(F32), ALU.subtract).then_inc(s["om_done"], 1)
            for i in range(8):
                pool.wait_ge(s["sum_ready"], i + 1)
                part = gate_a[:, 512 * i:512 * (i + 1)].rearrange("p (c t) -> p c t", c=2)
                hi, lo = merged_hi[:, 2 * i:2 * i + 2, :], merged_lo[:, 2 * i:2 * i + 2, :]
                copy(hi, part).then_inc(s["merged_hi_out"], 1)
                pool.wait_ge(s["merged_hi_out"], i + 1)
                tt(lo, part, hi.bitcast(F32), ALU.subtract).then_inc(s["merged_ready"], 1)

            def window(a, slot, hi_count):
                src = xg_T[:, :, bass.ds(slot, WIN)]
                copy(win[a][:, :, 0:WIN], src).then_inc(s["win_hi_out"], 1)
                pool.wait_ge(s["win_hi_out"], hi_count)
                tt(wait_taker, ident[0:1, 0:1], ident[0:1, 0:1], ALU.mult).then_inc(s["win_hi_out"], 1)
                tt(win[a][:, :, WIN:P], src, win[a][:, :, 0:WIN].bitcast(F32), ALU.subtract)\
                    .then_inc(s["win_ready"], 1)

            pool.wait_ge(s["big_act"], DC // 2)
            pool.wait_ge(s["big_dve"], DC // 2)
            nc.gpsimd.memset(xg_T[:, :, SLOTS:XW], 0.0).then_inc(s["padded"], 1)
            for a in range(2):
                other = rows_of[1 - a]
                nc.gpsimd.memset(hid_hi[a][:, :, other].bitcast(F32), 0.0).then_inc(s["padded"], 1)
                nc.gpsimd.memset(hid_lo[a][:, :, other].bitcast(F32), 0.0).then_inc(s["padded"], 1)
            pool.wait_ge(s["padded"], 5)
            window(0, 0, 1)

            def index(first, n, top):
                return pool.value_load(tab[0:1, bass.ds(n + first, 1)], min_val=0, max_val=top)

            def pair_part(n, count, turned=None):
                slots = [index(SLOT_OF + a, n, SLOTS) for a in range(2)]
                offs = [index(OFF_OF + a, n, WIN) for a in range(2)]
                if turned is not None:
                    pool.wait_ge(s["selT_ready"], turned)
                for a in range(2):
                    copy(sel_cols[:, :, rows_of[a]], selw[:, :, bass.ds(slots[a], WIN)]).then_inc(s["cols_ready"], 1)
                for a in range(2):
                    copy(own[:, rows_of[a]], steps[:, bass.ds(offs[a], WIN)]).then_inc(s["cols_ready"], 1)
                pool.wait_ge(s["cols_ready"], count)
                tt(sel_pair, sel_cols, own.unsqueeze(1).broadcast_to([P, TT, P]), ALU.mult)\
                    .then_inc(s["pair_ready"], 1)

            pool.wait_ge(s["tab_ready"], 1)
            pool.wait_ge(s["sel_ready"], 2 * TT)
            window(1, index(SLOT_OF + 1, 0, SLOTS), 3)
            pair_part(0, 4)
            pairs = pool.value_load(tab[0:1, PAIRS:PAIRS + 1], min_val=EXPERTS // 2, max_val=MAX_PAIRS)

            def next_pair(m, start, at):
                for a in range(2):
                    slot = index(SLOT_OF + a + 2, m * 2, SLOTS)
                    pool.wait_ge(bite_used, start + (at[a] + GU))
                    window(a, slot, m * 4 + (2 * a + 5))
                pair_part(m * 2 + 2, m * 4 + 8, m + 1)

            next_pair(0, DENSE, FIRST_AT)
            with pool.Fori(1, pairs) as m:
                next_pair(m, pair_start(m), PAIR_AT)

        @block.scalar
        def _(act):
            act.dma_start(cst[:, :], consts).then_inc(consts_in, 16)
            act.dma_start(lrn[:, :], learned).then_inc(consts_in, 16)
            act.dma_start(work[:, 0:7 * P], masks).then_inc(consts_in, 16)
            count = [0]

            def then(ins):
                count[0] += 1
                ins.then_inc(act_step, 1)
                act.wait_ge(act_step, count[0])

            def squares(n, into, src):
                for t in range(TT):
                    nc.scalar.activation(into[:, t * D:(t + 1) * D], src[t], ACT.Square,
                                         accum_out=stat[:, 2 * n + t:2 * n + t + 1]).then_inc(s["sq_done"], 1)

            def root(n):
                act.wait_ge(s["ms_ready"], n + 1)
                nc.scalar.activation(stat[:, 8 + 2 * n:10 + 2 * n], stat[:, 8 + 2 * n:10 + 2 * n],
                                     ACT.Sqrt).then_inc(s["root_ready"], 1)

            def hi(slot, quarter, buf, fallen, used):
                if fallen is not None:
                    act.wait_ge(raw_in[slot], fallen)
                if used is not None:
                    act.wait_ge(bite_used, used)
                nc.scalar.activation(bite_hi[:, BITE * buf:BITE * (buf + 1)],
                                     ring[slot][:, BITE * quarter:BITE * (quarter + 1)], ACT.Copy)\
                    .then_inc(hi_ready, 1)

            def hi_dense(g):
                h = g // PER_HALF
                hi(h % RING, g % PER_HALF, g % BUFS, landed(h) if g % PER_HALF == 0 else None,
                   g - BUFS + 1 if g >= BUFS else None)

            def hi_later(m, b):
                slot, quarter, buf, fallen, number = later(m, b)
                hi(slot, quarter, buf, fallen if quarter == 0 else None, number - (BUFS - 1))

            def turned_hi(n, k, gain):
                for j in range(DC):
                    act.wait_ge(s["hT_bank"], DC * n + 2 * (j // 2) + 2)
                    q = (j // 2 % 4) * 512 + 256 * (j % 2)
                    nc.scalar.activation(hT_hi[:, j, :], big[:, q:q + 256], ACT.Copy, scale=gain[:, j:j + 1])\
                        .then_inc(s["hT_hi_out"], 1)

            for t in range(TT):
                act.wait_ge(x_in[t], 16)
            squares(0, arena[:, 0:4096], x_t)
            root(0)
            act.wait_ge(consts_in, 48)
            turned_hi(0, 0, learnt("g_mix"))

            lb = stat[:, 32:48]

            def evacuate(u):
                bank = acc[u % 2]
                unit_stands(act, u)
                free = bank_free[u % 2]
                if u == 0:
                    act.wait_ge(s["h_ready"], TT)
                    act.wait_ge(s["hT_bank"], DC)
                if u < U_HF:
                    nc.scalar.activation(q_T[:, 512 * u:512 * (u + 1)], bank[:, :], ACT.Silu).then_inc(free, 1)
                elif u < U_HI:
                    w = slice(512 * (u - U_HF), 512 * (u - U_HF + 1))
                    nc.scalar.activation(f_T[:, w], bank[:, :], ACT.Sigmoid).then_inc(s["fk_sig"], 1)
                    nc.scalar.activation(k_T[:, w], bank[:, :], ACT.Sigmoid, scale=-1.0).then_inc(free, 1)
                elif u < U_MQ:
                    base, dst = (U_HI, v_tok) if u < U_HOG else (U_HOG, og_tok)
                    c, t = (u - base) // 2, (u - base) % 2
                    nc.scalar.activation(dst[:, t * HW + 512 * c:t * HW + 512 * (c + 1)], bank[:, :],
                                         ACT.Copy if dst is v_tok else ACT.Silu).then_inc(free, 1)
                elif u < U_MV:
                    k = u - U_MQ
                    dst = (mq_T, mk_T)[k // 4][:, 512 * (k % 4):512 * (k % 4 + 1)]
                    nc.scalar.activation(dst, bank[:, :], ACT.Copy).then_inc(free, 1)
                elif u < U_GA:
                    c, t = (u - U_MV) // 2, (u - U_MV) % 2
                    nc.scalar.activation(mv_tok[:, t * HW + 512 * c:t * HW + 512 * (c + 1)], bank[:, :],
                                         ACT.Copy).then_inc(free, 1)
                elif u < U_UPH:
                    if u == U_GA:
                        act.wait_ge(s["lvl_done"], LEVELS)
                        act.wait_ge(s["off_copied"], 1)
                    if u == U_GB:
                        act.wait_ge(s["s_ready"], 2)
                    dst, base = (gate_a, U_GA) if u < U_GB else (gate_b, U_GB)
                    w = slice(512 * (u - base), 512 * (u - base + 1))
                    nc.scalar.activation(dst[:, w], bank[:, :], ACT.Sigmoid).then_inc(free, 1)

            def softmax(r):
                act.wait_ge(s["mx_ready"], r + 1)
                sm = xtok[:, 1536 * r:1536 * (r + 1)].rearrange("p (h s) -> p h s", h=4)
                for h in range(4):
                    for t, (a, b) in enumerate(((0, 128), (128, 384))):
                        k = 4 * t + h
                        nc.scalar.activation(sm[:, h, a:b], sm[:, h, a:b], ACT.Exp,
                                             bias=stat[:, 112 + k:113 + k], scale=SCALE,
                                             accum_out=stat[:, 120 + k:121 + k]).then_inc(s["exp_done"], 1)

            for g in range(DENSE + LAG):
                hi_dense(g)
                block = block_ending(g - LAG)
                if block is not None and block < U_UPH // 2:
                    evacuate(2 * block)
                    evacuate(2 * block + 1)
                if g == LAG:
                    act.wait_ge(s["lb_max"], 1)
                    nc.scalar.activation(lb, lb, ACT.Exp).then_inc(s["lb_exp"], 1)
                if g == AT_LEVEL + LEVEL_STEP * (LEVELS - 1) + LAG:
                    act.wait_ge(s["lvl_done"], LEVELS)
                    nc.scalar.activation(sc_off, big[:, 0:1024].rearrange("p (h t) -> p h t", h=HEADS),
                                         ACT.Copy).then_inc(s["off_copied"], 1)
                if g == AT_O + LAG:
                    act.wait_ge(s["o_ready"], 1)
                    act.wait_ge(s["roped"], 8)
                    nc.scalar.activation(work[:, :], big[:, :], ACT.Square).then_inc(s["osq_done"], 1)
                if g == AT_O + LAG + 2:
                    act.wait_ge(s["oms_ready"], 1)
                    nc.scalar.activation(stat[:, 48:64], stat[:, 48:64], ACT.Sqrt).then_inc(s["oroot_ready"], 1)
                if g == AT_OT + LAG:
                    act.wait_ge(s["oT_ready"], 1)
                    act.wait_ge(s["lvl_done"], LEVELS)
                    nc.scalar.activation(oh_hi[:, :], big[:, :], ACT.Copy, scale=learnt("g_hgrn"))\
                      .then_inc(s["oh_hi_out"], 1)
                for r, at in enumerate(AT_ATT):
                    if g == at + LAG + 2:
                        softmax(r)
                    if g == at + 20:
                        act.wait_ge(s["pv_ready"], r + 1)
                        nc.scalar.activation(work[:, 1024 * r:1024 * (r + 1)], mid[:, :], ACT.Copy)\
                          .then_inc(s["om_out"], 1)

            for b in range(2):
                act.wait_ge(bank_free[b], U_END // 2)
            squares(1, h_tok, x_t)
            root(1)
            act.wait_ge(s["gexp_in"], 1)
            ge = rt[:, 72:80]
            nc.scalar.activation(ge, ge, ACT.Exp).then_inc(s["gexp_out"], 1)
            act.wait_ge(s["wexp_in"], 1)
            we = rt[:, 200:202]
            nc.scalar.activation(we, we, ACT.Exp).then_inc(s["wexp_out"], 1)

            for j in range(1, DC, 2):
                act.wait_ge(s["big_filled"], j + 1)
                nc.scalar.activation(xg_T[:, j, 0:SLOTS], big[:, 512 * (j % 4):512 * (j % 4 + 1)], ACT.Copy,
                                     scale=learnt("g_ffn")[:, j:j + 1]).then_inc(s["big_act"], 1)

            act.wait_ge(s["tab_ready"], 1)
            pairs = act.value_load(tab[0:1, PAIRS:PAIRS + 1], min_val=EXPERTS // 2, max_val=MAX_PAIRS)

            def beside(m, start, at, b):
                for a in range(2):
                    if b == at[a] + AT_GATE_OUT:
                        act.wait_ge(bite_used, start + (at[a] + GU // 2))
                        nc.scalar.activation(gu_sb[:, 0:FE], acc[0][:, :], ACT.Copy).then_inc(s["gu_out"], 1)
                    if b == at[a] + AT_UP_OUT:
                        act.wait_ge(bite_used, start + (at[a] + GU))
                        nc.scalar.activation(gu_sb[:, FE:2 * FE], acc[1][:, :], ACT.Copy).then_inc(s["gu_out"], 1)
                    if b == at[a] + AT_SILU:
                        act.wait_ge(s["folded"], m * 4 + (2 * a + 1))
                        nc.scalar.activation(silu_g, mid[:, 0:FC * WIN], ACT.Silu).then_inc(s["silu_done"], 1)

            def turned_weights(m):
                act.wait_ge(s["selT_ready"], m)
                nc.scalar.activation(sel_T, acc[0][:, 0:TOK].rearrange("p (t s) -> p t s", t=TT),
                                     ACT.Copy).then_inc(s["selT_out"], 1)

            def rows_out(stands):
                act.wait_ge(bite_used, stands)
                for k in range(2):
                    nc.scalar.activation(y_sb[:, 512 * k:512 * (k + 1)], big[:, 512 * k:512 * (k + 1)],
                                         ACT.Copy).then_inc(s["big_act"], 1)

            for b in range(LAG, PAIR - DOWN + LAG):
                hi_dense(DENSE + b)
                beside(0, DENSE, FIRST_AT, b)
            with act.Fori(1, pairs) as m:
                for b in range(LAG, PAIR + LAG):
                    hi_later(m, b)
                    beside(m, pair_start(m), PAIR_AT, b)
                    if b == AT_SELT_OUT:
                        turned_weights(m)
                    if b == PASS + AT_Y:
                        rows_out(pair_start(m) + PASS)
            for b in range(LAG, DOWN + LAG + 1):
                hi_later(pairs, b)
                if b == LAG:
                    turned_weights(pairs)
                if b == DOWN + AT_Y:
                    rows_out(pair_start(pairs) + DOWN)

            act.wait_ge(s["win_ready"], pairs * 2 + 2)
            act.wait_ge(s["big_dve"], pairs * 10 + DC // 2)
            squares(2, hp_tok, x_t)
            root(2)
            act.wait_ge(s["pair_ready"], pairs + 1)
            turned_hi(2, 1, learnt("g_ple"))
            for b in range(LAG + 1, N_PLE * IN_BITES + LAG):
                if b < N_PLE * IN_BITES:
                    hi_later(pairs, DOWN + b)
                if (b - LAG) % IN_BITES == IN_BITES - 1:
                    for t in range(TT):
                        v = 2 * ((b - LAG) // IN_BITES) + t
                        if t == 0:
                            act.wait_ge(s["p_first"], v // 2 + 1)
                        else:
                            act.wait_ge(bite_used, pair_start(pairs) + (DOWN + b - LAG + 1))
                        if v >= 2:
                            act.wait_ge(s["p_out"], v - 1)
                        nc.scalar.activation(sig_p[:, v % 2, :], p_bank(v), ACT.Sigmoid).then_inc(s["p_out_act"], 1)
            act.wait_ge(s["p_out"], 8)
            squares(3, hp_tok, x_t)
            root(3)

        @block.vector
        def _(dve):
            count = [0]
            tt, ts, stt = nc.vector.tensor_tensor, nc.vector.tensor_scalar, nc.vector.scalar_tensor_tensor

            def then(ins):
                count[0] += 1
                ins.then_inc(dve_step, 1)
                dve.wait_ge(dve_step, count[0])

            def normed(n, into, src):
                dve.wait_ge(s["sq_done"], 2 * (n + 1))
                r = stat[:, 8 + 2 * n:10 + 2 * n]
                ts(r, stat[:, 2 * n:2 * n + 2], 1.0 / D, EPS, ALU.mult, ALU.add).then_inc(s["ms_ready"], 1)
                dve.wait_ge(s["root_ready"], n + 1)
                then(nc.vector.reciprocal(r, r))
                if into is not None:
                    for t in range(TT):
                        ts(into[:, t * D:(t + 1) * D], src[t], r[:, t:t + 1], None, ALU.mult)\
                            .then_inc(s["h_ready"], 1)
                return r

            def turned(n, gain):
                for j in range(DC):
                    dve.wait_ge(s["hT_bank"], DC * n + 2 * (j // 2) + 2)
                    q = (j // 2 % 4) * 512 + 256 * (j % 2)
                    ts(hT[:, j, :], big[:, q:q + 256], gain[:, j:j + 1], None, ALU.mult)\
                        .then_inc(s["hT_out"], 1)

            def turned_lo(k, gain):
                for j in range(DC):
                    dve.wait_ge(s["hT_hi_out"], DC * k + 2 * (j // 2) + 2)
                    q = (j // 2 % 4) * 512 + 256 * (j % 2)
                    stt(hT_lo[:, j, :], big[:, q:q + 256], gain[:, j:j + 1], hT_hi[:, j, :].bitcast(F32),
                        ALU.mult, ALU.subtract).then_inc(s["hT_out"], 1)

            def lo(slot, quarter, buf, ready):
                at = slice(BITE * buf, BITE * (buf + 1))
                dve.wait_ge(hi_ready, ready)
                tt(bite_lo[:, at], ring[slot][:, BITE * quarter:BITE * (quarter + 1)], bite_hi[:, at].bitcast(F32),
                   ALU.subtract).then_inc(lo_ready, 1)

            def lo_dense(g):
                lo(g // PER_HALF % RING, g % PER_HALF, g % BUFS, g + 1)

            def lo_later(m, b):
                slot, quarter, buf, _, number = later(m, b)
                lo(slot, quarter, buf, number + 1)

            normed(0, arena[:, 0:4096], x_t)
            dve.wait_ge(consts_in, 48)
            turned_lo(0, learnt("g_mix"))
            for g in range(LAG):
                lo_dense(g)
            then(nc.vector.tensor_copy(mask[:, :, :], work[:, 0:7 * P].rearrange("p (n t) -> p n t", n=7)))

            lb = stat[:, 32:48]
            raw = learnt("lb_raw")
            then(tt(stat[:, 64:72], raw[:, 0:8], raw[:, 8:16], ALU.max))
            then(tt(lb[:, 0:8], raw[:, 0:8], stat[:, 64:72], ALU.subtract))
            tt(lb[:, 8:16], raw[:, 8:16], stat[:, 64:72], ALU.subtract).then_inc(s["lb_max"], 1)
            lo_dense(LAG)
            dve.wait_ge(s["lb_exp"], 1)
            then(tt(stat[:, 64:72], lb[:, 0:8], lb[:, 8:16], ALU.add))
            then(nc.vector.reciprocal(stat[:, 64:72], stat[:, 64:72]))
            then(tt(stat[:, 72:80], lb[:, 0:8], stat[:, 64:72], ALU.mult))
            then(tt(stat[:, 80:88], lb[:, 8:16], stat[:, 64:72], ALU.mult))
            lbv, lbc = stat[:, 72:80], stat[:, 80:88]

            def forget(u):
                dve.wait_ge(s["fk_sig"], u - U_HF + 1)
                dve.wait_ge(bank_free[u % 2], u // 2 + 1)
                for h in range(2 * (u - U_HF), 2 * (u - U_HF) + 2):
                    w = slice(TOK * h, TOK * (h + 1))
                    ts(f_T[:, w], f_T[:, w], lbc[:, h:h + 1], lbv[:, h:h + 1], ALU.mult, ALU.add)
                    ins = ts(k_T[:, w], k_T[:, w], lbc[:, h:h + 1], None, ALU.mult)
                then(ins)

            def rope(k):
                raw_u = (mq_T, mk_T)[k // 4][:, 512 * (k % 4):512 * (k % 4 + 1)].rearrange("p (h t) -> p h t", h=2)
                tmp = work[:, 0:512].rearrange("p (h t) -> p h t", h=2)
                wide = lambda n: const(n).unsqueeze(1).broadcast_to([P, 2, TOK])
                dve.wait_ge(s["rot_ready"], k + 1)
                rot_ps = mid[:, 0:512].rearrange("p (h t) -> p h t", h=2)
                then(tt(tmp, rot_ps, wide("sin"), ALU.mult))
                then(tt(raw_u, raw_u, wide("cos"), ALU.mult))
                ins = tt(raw_u, raw_u, tmp, ALU.add)
                ins.then_inc(s["roped"], 1)
                dve.wait_ge(s["roped"], k + 1)

            def level(n):
                dve.wait_ge(s["lvl_done"], n + 1)
                sc = xtok[:, 0:2048].rearrange("p (m t) -> p m t", m=16)
                ps = big[:, :].rearrange("p (m t) -> p m t", m=16)
                if n == 0:
                    then(tt(sc, ps, ident.unsqueeze(1).broadcast_to([P, 16, P]), ALU.mult))
                    tt(q_T, q_T, f_T, ALU.mult).then_inc(s["lvl_ready"], 1)
                    dve.wait_ge(s["lvl_ready"], n + 2)
                    return
                if n < LEVELS - 1:
                    L = 1 << (n - 1)
                    then(nc.vector.copy_predicated(sc, mask[:, n - 1, :].unsqueeze(1).broadcast_to([P, 16, P]), ps))
                    m = HEADS * TOK // (2 * L)
                    two = lambda ap: ap.rearrange("p (m two l) -> p m two l", m=m, two=2)
                    qv, kv = two(q_T), two(k_T)
                    tot = spans[n - 1][:, 0:2 * m].rearrange("p (m two) -> p m two", two=2)
                    wide = lambda k: tot[:, :, k:k + 1].broadcast_to([P, m, L])
                    then(tt(qv[:, :, 1, :], qv[:, :, 1, :], wide(0), ALU.mult))
                    then(tt(kv[:, :, 0, :], kv[:, :, 0, :], wide(1), ALU.mult))
                    if n < LEVELS - 2:
                        then(tt(spans[n][:, 0:m], tot[:, :, 0], tot[:, :, 1], ALU.mult))
                    ts(stat[:, 188:189], lbv[:, 0:1], 1.0, None, ALU.mult).then_inc(s["lvl_ready"], 1)

            def hgrn_mean():
                dve.wait_ge(s["osq_done"], 1)
                r = stat[:, 48:64]
                then(nc.vector.tensor_reduce(r, work[:, :].rearrange("p (m v) -> p m v", m=16), AX.X, ALU.add))
                ts(r, r, 1.0 / P, EPS, ALU.mult, ALU.add).then_inc(s["oms_ready"], 1)

            def hgrn_norm():
                r = stat[:, 48:64]
                dve.wait_ge(s["oroot_ready"], 1)
                then(nc.vector.reciprocal(r, r))
                wv = work[:, :].rearrange("p (m v) -> p m v", m=16)
                then(tt(wv, big[:, :].rearrange("p (m v) -> p m v", m=16),
                        r.unsqueeze(2).broadcast_to([P, 16, P]), ALU.mult))
                tt(work[:, :], work[:, :], og_tok, ALU.mult).then_inc(s["on_ready"], 1)

            def scores(r):
                dve.wait_ge(s["s_ready"], r + 1)
                sm = xtok[:, 1536 * r:1536 * (r + 1)].rearrange("p (h b s) -> p h b s", h=4, b=3)
                ps = big[:, :].rearrange("p (h b s) -> p h b s", h=4, b=4)
                bias = const("causal").unsqueeze(1).unsqueeze(1).broadcast_to([P, 4, 2, P])
                tt(sm[:, :, 0:3:2, :], ps[:, :, 0:3:2, :], bias, ALU.add)
                then(nc.vector.tensor_copy(sm[:, :, 1, :], ps[:, :, 1, :]))
                flat = xtok[:, 1536 * r:1536 * (r + 1)].rearrange("p (h s) -> p h s", h=4)
                mx = stat[:, 112:120]
                nc.vector.tensor_reduce(mx[:, 0:4], flat[:, :, 0:128], AX.X, ALU.max)
                then(nc.vector.tensor_reduce(mx[:, 4:8], flat[:, :, 128:384], AX.X, ALU.max))
                ts(mx, mx, -SCALE, None, ALU.mult).then_inc(s["mx_ready"], 1)

            def probabilities(r):
                flat = xtok[:, 1536 * r:1536 * (r + 1)].rearrange("p (h s) -> p h s", h=4)
                dve.wait_ge(s["exp_done"], 8 * (r + 1))
                rs = stat[:, 120:128]
                then(nc.vector.reciprocal(rs, rs))
                then(tt(flat[:, :, 0:128], flat[:, :, 0:128], rs[:, 0:4].unsqueeze(2).broadcast_to([P, 4, 128]), ALU.mult))
                tt(flat[:, :, 128:384], flat[:, :, 128:384], rs[:, 4:8].unsqueeze(2).broadcast_to([P, 4, 256]),
                   ALU.mult).then_inc(s["pn_ready"], 1)

            def probs_out(r):
                dve.wait_ge(s["pT_ready"], r + 1)
                if r:
                    dve.wait_ge(s["pv_ready"], r)
                nc.vector.tensor_copy(probs_T.rearrange("p (h s) -> p h s", h=4),
                                      big[:, :].rearrange("p (h s) -> p h s", h=4)[:, :, 0:384])\
                    .then_inc(s["pT_out"], 1)

            def gated(u):
                unit_stands(dve, u)
                if u == U_UPH:
                    dve.wait_ge(bank_free[1], U_UPH // 2)
                    dve.wait_ge(bank_free[0], U_UPH // 2)
                w = slice(512 * ((u - U_UPH) % 8), 512 * ((u - U_UPH) % 8 + 1))
                gate = gate_a if u < U_UPM else gate_b
                tt(gate[:, w], gate[:, w], acc[u % 2][:, :], ALU.mult).then_inc(bank_free[u % 2], 1)
                dve.wait_ge(bank_free[u % 2], u // 2 + 1)
                if u >= U_UPM:
                    tt(gate_a[:, w], gate_a[:, w], gate_b[:, w], ALU.add).then_inc(s["sum_ready"], 1)

            def added(u):
                if u == U_OUT:
                    dve.wait_ge(s["x_again"], 16 * TT)
                unit_stands(dve, u)
                c, t = (u - U_OUT) // 2, (u - U_OUT) % 2
                xs = x_t[t][:, 512 * c:512 * (c + 1)]
                tt(xs, xs, acc[u % 2][:, :], ALU.add).then_inc(bank_free[u % 2], 1)

            for g in range(LAG + 1, DENSE + LAG):
                lo_dense(g)
                block = block_ending(g - LAG)
                if block is not None and U_HF // 2 <= block < U_HI // 2:
                    forget(2 * block)
                    forget(2 * block + 1)
                    if block == U_HI // 2 - 1:
                        ts(stat[:, 188:189], lbv[:, 0:1], 1.0, None, ALU.mult).then_inc(s["lvl_ready"], 1)
                n, rest = divmod(g - LAG - AT_LEVEL, LEVEL_STEP)
                if rest == 0 and 0 <= n < LEVELS - 1:
                    level(n)
                for k in range(U_MV - U_MQ):
                    if g == at_rotate(k) + 2:
                        rope(k)
                if g == AT_O + LAG + 1:
                    hgrn_mean()
                if g == AT_O + LAG + 3:
                    hgrn_norm()
                if g == AT_OT + LAG + 1:
                    dve.wait_ge(s["oh_hi_out"], 1)
                    stt(oh_lo[:, :], big[:, :], learnt("g_hgrn"), oh_hi[:, :].bitcast(F32), ALU.mult,
                        ALU.subtract).then_inc(s["oh_done"], 1)
                for r, at in enumerate(AT_ATT):
                    if g == at + LAG:
                        scores(r)
                    if g == at + LAG + 5:
                        probabilities(r)
                    if g == at + 14:
                        probs_out(r)
                block = block_ending(g - LAG + 1)
                if block is not None and block >= U_UPH // 2:
                    for u in (2 * block, 2 * block + 1):
                        gated(u) if u < U_OUT else added(u)

            for b in range(2):
                dve.wait_ge(bank_free[b], U_END // 2)
            normed(1, h_tok, x_t)
            turned(1, learnt("g_ffn"))

            dve.wait_ge(s["logits_ready"], 1)
            lg = rt[:, 0:72].rearrange("p (t e) -> p t e", t=TT)
            then(nc.vector.tensor_copy(lg, mid[:, 0:72].rearrange("p (t e) -> p t e", t=TT)))
            g_l, e_l = lg[:, :, 0:GROUPS], lg[:, :, GROUPS:36]
            ge = rt[:, 72:80].rearrange("p (t g) -> p t g", t=TT)
            gmax, pg = rt[:, 80:82], rt[:, 82:84]
            wide = lambda ap, n: ap.unsqueeze(2).broadcast_to([P, TT, n])
            desc = const("desc")

            def first_max(vals, top, onehot, n):
                down_counting = desc[:, 8 - n:8].unsqueeze(1).broadcast_to([P, TT, n])
                then(nc.vector.tensor_reduce(top, vals, AX.X, ALU.max))
                then(tt(onehot, vals, wide(top, n), ALU.is_equal))
                then(tt(onehot, onehot, down_counting, ALU.mult))
                then(nc.vector.tensor_reduce(rt[:, 84:86], onehot, AX.X, ALU.max))
                then(tt(onehot, onehot, wide(rt[:, 84:86], n), ALU.is_equal))

            goh = rt[:, 86:94].rearrange("p (t g) -> p t g", t=TT)
            first_max(g_l, gmax, goh, GROUPS)
            tt(ge, g_l, wide(gmax, GROUPS), ALU.subtract).then_inc(s["gexp_in"], 1)
            dve.wait_ge(s["gexp_out"], 1)
            then(nc.vector.tensor_reduce(pg, ge, AX.X, ALU.add))
            then(nc.vector.reciprocal(pg, pg))
            grid = [P, TT, GROUPS, PER_GROUP]
            prod = rt[:, 96:160].rearrange("p (t g i) -> p t g i", t=TT, g=GROUPS)
            for t in range(TT):
                then(tt(prod[:, t], e_l[:, t, :].rearrange("p (g i) -> p g i", g=GROUPS),
                        goh[:, t, :].unsqueeze(2).broadcast_to([P, GROUPS, PER_GROUP]), ALU.mult))
            e8 = rt[:, 160:176].rearrange("p (t i) -> p t i", t=TT)
            for t in range(TT):
                then(nc.vector.tensor_reduce(e8[:, t, :], prod[:, t].rearrange("p g i -> p i g"), AX.X, ALU.add))
            oh = [rt[:, 208 + 16 * k:224 + 16 * k].rearrange("p (t i) -> p t i", t=TT) for k in range(2)]
            tops = [rt[:, 196 + 2 * k:198 + 2 * k] for k in range(2)]
            first_max(e8, tops[0], oh[0], PER_GROUP)
            e8b = rt[:, 176:192].rearrange("p (t i) -> p t i", t=TT)
            then(stt(e8b, oh[0], -1e30, e8, ALU.mult, ALU.add))
            first_max(e8b, tops[1], oh[1], PER_GROUP)
            we = rt[:, 200:202]
            tt(we, tops[1], tops[0], ALU.subtract).then_inc(s["wexp_in"], 1)
            dve.wait_ge(s["wexp_out"], 1)
            w_k = [rt[:, 202 + 2 * k:204 + 2 * k] for k in range(2)]
            then(ts(w_k[0], we, 1.0, None, ALU.add))
            then(nc.vector.reciprocal(w_k[0], w_k[0]))
            then(tt(w_k[0], w_k[0], pg, ALU.mult))
            then(tt(w_k[1], w_k[0], we, ALU.mult))
            OH = [rt[:, 256 + 64 * k:320 + 64 * k].rearrange("p (t e) -> p t e", t=TT) for k in range(2)]
            both = rt[:, 384:448].rearrange("p (t e) -> p t e", t=TT)
            for k in range(2):
                for t in range(TT):
                    then(tt(OH[k][:, t, :].rearrange("p (g i) -> p g i", g=GROUPS),
                            goh[:, t, :].unsqueeze(2).broadcast_to([P, GROUPS, PER_GROUP]),
                            oh[k][:, t, :].unsqueeze(1).broadcast_to([P, GROUPS, PER_GROUP]), ALU.mult))
            tt(both, OH[0], OH[1], ALU.add).then_inc(s["onehot_ready"], 1)

            dve.wait_ge(s["counts_ready"], 1)
            cnt, incl, slot0 = rt[:, 448:480], rt[:, 480:512], rt[:, 512:544]
            pos = rt[:, 544:608].rearrange("p (t e) -> p t e", t=TT)
            then(nc.vector.tensor_copy(cnt, mid[:, 512:544]))
            then(nc.vector.tensor_tensor_scan(incl, ones[:, 0:EXPERTS], cnt, 0.0, ALU.mult, ALU.add))
            then(tt(slot0, incl, cnt, ALU.subtract))
            then(tt(pos, mid[:, 544:608].rearrange("p (t e) -> p t e", t=TT),
                    slot0.unsqueeze(1).broadcast_to([P, TT, EXPERTS]), ALU.add))
            slot_k = [rt[:, 608 + 2 * k:610 + 2 * k] for k in range(2)]
            tmp = rt[:, 612:676].rearrange("p (t e) -> p t e", t=TT)
            for k in range(2):
                then(tt(tmp, pos, OH[k], ALU.mult))
                then(nc.vector.tensor_reduce(slot_k[k], tmp, AX.X, ALU.add))
            dve.wait_ge(s["iota_in"], 16)
            at = [[slot_k[k][:, t:t + 1] for k in range(2)] for t in range(TT)]
            wt = [[w_k[k][:, t:t + 1] for k in range(2)] for t in range(TT)]
            for t in range(TT):
                then(ts(sel[:, t, :], iota, at[t][0], None, ALU.is_equal))
                stt(sel[:, t, :], iota, at[t][1], sel[:, t, :], ALU.is_equal, ALU.add).then_inc(s["sel_ready"], 1)
            npass, many = rt[:, 676:708], rt[:, 708:740]
            then(ts(npass, cnt, float(WIN), 1.0, ALU.is_gt, ALU.add))
            for m in range(2, TOK // WIN):
                then(stt(npass, cnt, float(WIN * m), npass, ALU.is_gt, ALU.add))
            then(nc.vector.tensor_tensor_scan(many, ones[:, 0:EXPERTS], npass, 0.0, ALU.mult, ALU.add))
            then(tt(npass, many, npass, ALU.subtract))
            a_e, d_e = rt[:, 740:772], rt[:, 772:804]
            then(stt(a_e, npass, -float(WIN), slot0, ALU.mult, ALU.add))
            then(nc.vector.tensor_copy(d_e[:, 0:1], a_e[:, 0:1]))
            then(tt(d_e[:, 1:EXPERTS], a_e[:, 1:EXPERTS], a_e[:, 0:EXPERTS - 1], ALU.subtract))
            row = lambda v: v[0:1].unsqueeze(1).broadcast_to([1, TIMES, EXPERTS])
            times = const("times")[0:1]
            e_of, s_of, o_of = [rt[0:1, 804 + 44 * k:804 + 44 * k + TIMES] for k in range(3)]
            then(tt(table, row(npass), times.unsqueeze(2).broadcast_to([1, TIMES, EXPERTS]), ALU.is_le))
            then(nc.vector.tensor_reduce(e_of, table, AX.X, ALU.add))
            then(ts(e_of, e_of, -1.0, None, ALU.add))
            then(tt(table_2, table, row(cnt), ALU.mult))
            then(nc.vector.tensor_reduce(o_of, table_2, AX.X, ALU.add))
            then(tt(table, table, row(d_e), ALU.mult))
            then(nc.vector.tensor_reduce(s_of, table, AX.X, ALU.add))
            then(stt(s_of, times, float(WIN), s_of, ALU.mult, ALU.add))
            then(tt(o_of, s_of, o_of, ALU.subtract))
            then(ts(o_of, o_of, float(WIN), 0.0, ALU.add, ALU.max))
            then(ts(o_of, o_of, float(WIN), None, ALU.min))
            then(ts(s_of, s_of, float(SLOTS), None, ALU.min))
            then(nc.vector.tensor_copy(tab[0:1, EXPERT_OF:EXPERT_OF + TIMES], e_of))
            then(nc.vector.tensor_copy(tab[0:1, SLOT_OF:SLOT_OF + TIMES], s_of))
            then(nc.vector.tensor_copy(tab[0:1, OFF_OF:OFF_OF + TIMES], o_of))
            then(ts(e_of, times, 2.0, many[0:1, EXPERTS - 1:EXPERTS], ALU.mult, ALU.is_lt))
            then(nc.vector.tensor_reduce(rt[0:1, 936:937], e_of, AX.X, ALU.add))
            then(ts(rt[0:1, 937:938], rt[0:1, 936:937], 2.0, None, ALU.mult))
            then(nc.vector.tensor_copy(tab[0:1, PAIRS:PAIRS + 1], rt[0:1, 936:937]))
            nc.vector.tensor_copy(tab[0:1, PASSES:PASSES + 1], rt[0:1, 937:938]).then_inc(s["tab_ready"], 1)
            for j in range(0, DC, 2):
                dve.wait_ge(s["big_filled"], j + 1)
                ts(xg_T[:, j, 0:SLOTS], big[:, 512 * (j % 4):512 * (j % 4 + 1)], learnt("g_ffn")[:, j:j + 1],
                   None, ALU.mult).then_inc(s["big_dve"], 1)
            then(nc.vector.memset(selw[:, :, SLOTS:XW], 0.0))
            for t in range(TT):
                then(ts(selw[:, t, 0:SLOTS], iota, at[t][0], wt[t][0], ALU.is_equal, ALU.mult))
                then(ts(work[:, 512:1024], iota, at[t][1], wt[t][1], ALU.is_equal, ALU.mult))
                tt(selw[:, t, 0:SLOTS], selw[:, t, 0:SLOTS], work[:, 512:1024], ALU.add)\
                    .then_inc(s["sel_ready"], 1)

            dve.wait_ge(s["tab_ready"], 1)
            pairs = dve.value_load(tab[0:1, PAIRS:PAIRS + 1], min_val=EXPERTS // 2, max_val=MAX_PAIRS)
            silu_v = silu_g.rearrange("p (c s) -> p c s", c=FC)
            hid_v = hid.rearrange("p (c s) -> p c s", c=FC)
            up_T = mid[:, 512:512 + FC * WIN].rearrange("p (c s) -> p c s", c=FC)

            def hidden(m, a):
                dve.wait_ge(s["folded"], m * 4 + (2 * a + 2))
                dve.wait_ge(s["silu_done"], m * 2 + (a + 1))
                tt(hid_hi[a][:, :, rows_of[a]], silu_v, up_T, ALU.mult).then_inc(s["hid_hi_out"], 1)
                tt(hid_v, silu_v, up_T, ALU.mult).then_inc(s["hid_hi_out"], 1)
                dve.wait_ge(s["hid_hi_out"], m * 4 + (2 * a + 2))
                tt(hid_lo[a][:, :, rows_of[a]], hid_v, hid_hi[a][:, :, rows_of[a]].bitcast(F32),
                   ALU.subtract).then_inc(s["hid_ready"], 1)

            def rows_out(stands):
                dve.wait_ge(bite_used, stands)
                for k in range(2, 4):
                    nc.vector.tensor_copy(y_sb[:, 512 * k:512 * (k + 1)], big[:, 512 * k:512 * (k + 1)])\
                        .then_inc(s["big_dve"], 1)

            def add(m, v):
                dve.wait_ge(s["big_filled"], m * 8 + (DC + v - 7))
                xs = x_t[v % 2][:, 512 * (v // 2):512 * (v // 2 + 1)]
                tt(xs, xs, big[:, 512 * (v % 4):512 * (v % 4 + 1)], ALU.add).then_inc(s["big_dve"], 1)

            for b in range(LAG, PAIR - DOWN + LAG):
                lo_dense(DENSE + b)
                for a in range(2):
                    if b == FIRST_AT[a] + AT_HID:
                        hidden(0, a)
            with dve.Fori(1, pairs) as m:
                for b in range(LAG, PAIR + LAG):
                    lo_later(m, b)
                    for a in range(2):
                        if b == PAIR_AT[a] + AT_HID:
                            hidden(m, a)
                    if b == PASS + AT_Y:
                        rows_out(pair_start(m) + PASS)
                    if 0 <= b - (PASS + AT_COMB + LAG) < 8:
                        add(m, b - (PASS + AT_COMB + LAG))
            for b in range(LAG, DOWN + LAG + 1):
                lo_later(pairs, b)
                if b == DOWN + AT_Y:
                    rows_out(pair_start(pairs) + DOWN)
            for v in range(8):
                add(pairs, v)

            dve.wait_ge(s["big_dve"], pairs * 10 + DC // 2)
            normed(2, hp_tok, x_t)
            turned_lo(1, learnt("g_ple"))
            for b in range(LAG + 1, N_PLE * IN_BITES + LAG):
                if b < N_PLE * IN_BITES:
                    lo_later(pairs, DOWN + b)
                if (b - LAG) % IN_BITES == IN_BITES - 1:
                    for t in range(TT):
                        n = (b - LAG) // IN_BITES
                        v = 2 * n + t
                        dve.wait_ge(s["p_out_act"], v + 1)
                        xs = x_t[t][:, 512 * n:512 * (n + 1)]
                        then(tt(sig_p[:, v % 2, :], sig_p[:, v % 2, :], big[:, 512 * (v % 4):512 * (v % 4 + 1)],
                                ALU.mult))
                        tt(xs, xs, sig_p[:, v % 2, :], ALU.add).then_inc(s["p_out"], 1)
            dve.wait_ge(s["p_out"], 8)
            r = normed(3, None, x_t)
            dve.wait_ge(s["g_fin_in"], 16)
            for t in range(TT):
                stt(x_t[t], x_t[t], r[:, t:t + 1], g_fin, ALU.mult, ALU.mult).then_inc(s["fin_ready"], 1)

        @block.tensor
        def _(pe):
            mm = nc.tensor.matmul

            def turn(n, src):
                if n == 0:
                    pe.wait_ge(consts_in, 48)
                pe.wait_ge(s["h_ready"], TT * (n + 1))
                for j in range(DC):
                    if j >= 8:
                        pe.wait_ge(s["hT_out"], DC * n + 2 * (j // 2) - 6)
                    for t in range(TT):
                        rows = src[:, t * D:(t + 1) * D].rearrange("p (c j) -> p j c", j=DC)[:, j, :]
                        q = (j // 2 % 4) * 512 + 256 * (j % 2) + P * t
                        ins = nc.tensor.transpose(big[:, q:q + P], rows, ident)
                    ins.then_inc(s["hT_bank"], 1)

            def products(dst, x_hi, x_lo, y_hi, y_lo, start, stop, beside=False):
                mm(dst, x_hi, y_hi, start=start, stop=False, skip_group_check=beside)
                mm(dst, x_lo, y_hi, start=False, stop=False, skip_group_check=beside)
                return mm(dst, x_hi, y_lo, start=False, stop=stop, skip_group_check=beside)

            def bite(buf, n, chunk=None):
                a = BITE * buf + 512 * n + (P * chunk if chunk is not None else 0)
                w = slice(a, a + (512 if chunk is None else P))
                return bite_hi[:, w], bite_lo[:, w]

            def open_bank(u):
                if u >= 2:
                    pe.wait_ge(bank_free[u % 2], u // 2)

            def extras(g):
                n, rest = divmod(g - AT_LEVEL, LEVEL_STEP)
                if rest == 0 and 0 <= n < LEVELS:
                    level(n)
                for k in range(U_MV - U_MQ):
                    if g == at_rotate(k):
                        raw_u = (mq_T, mk_T)[k // 4][:, 512 * (k % 4):512 * (k % 4 + 1)]
                        pe.wait_ge(bank_free[k % 2], (U_MQ + k) // 2 + 1)
                        if k:
                            pe.wait_ge(s["roped"], k)
                        mm(mid[:, 0:512], const("rot"), raw_u, start=True, stop=True).then_inc(s["rot_ready"], 1)
                if g == AT_O:
                    hgrn_out()
                if g == AT_OT:
                    pe.wait_ge(s["on_ready"], 1)
                    ov = big[:, :].rearrange("p (h t k) -> p h t k", h=HEADS, t=TT)
                    for h in range(HEADS):
                        for t in range(TT):
                            ins = nc.tensor.transpose(ov[:, h, t, :], work[:, t * HW + P * h:t * HW + P * (h + 1)], ident)
                    ins.then_inc(s["oT_ready"], 1)
                for r, at in enumerate(AT_ATT):
                    if g == at:
                        att_scores(r)
                    if g == at + 11:
                        att_turn(r)
                    if g == at + 17:
                        att_values(r)

            def level(n):
                pe.wait_ge(s["lvl_ready"], n + 1)
                if n == 0:
                    pe.wait_ge(bank_free[1], U_HI // 2)
                q_h, k_h = by_head(q_T), by_head(k_T)
                if n < LEVELS - 1:
                    for h in range(HEADS):
                        for b in range(2):
                            m = 2 * h + b
                            ins = mm(big[:, P * m:P * (m + 1)], k_h[:, h, P * b:P * (b + 1)],
                                     q_h[:, h, P * b:P * (b + 1)], start=True, stop=True)
                else:
                    for h in range(HEADS):
                        ins = mm(big[:, P * h:P * (h + 1)], k_h[:, h, 0:P], q_h[:, h, P:2 * P], start=True, stop=True)
                ins.then_inc(s["lvl_done"], 1)

            def hgrn_out():
                pe.wait_ge(s["off_copied"], 1)
                v = v_tok.rearrange("p (t c) -> p t c", t=TT)
                for t in range(TT):
                    for h in range(HEADS):
                        dst = big[:, t * HW + P * h:t * HW + P * (h + 1)]
                        if t:
                            mm(dst, sc_off[:, h, :], v[:, 0, P * h:P * (h + 1)], start=True, stop=False)
                        ins = mm(dst, sc_T[:, h, t, :], v[:, t, P * h:P * (h + 1)], start=not t, stop=True)
                ins.then_inc(s["o_ready"], 1)

            def att_scores(r):
                pe.wait_ge(s["roped"], 8)
                pe.wait_ge(s["oh_done"], 1) if r == 0 else pe.wait_ge(s["pT_out"], r)
                q_h, k_h = by_head(mq_T), by_head(mk_T)
                for i in range(4):
                    h, at = 4 * r + i, 512 * i
                    mm(big[:, at:at + 128], q_h[:, h, 0:P], k_h[:, h, 0:P], start=True, stop=True)
                    ins = mm(big[:, at + 128:at + 384], q_h[:, h, P:TOK], k_h[:, h, :], start=True, stop=True)
                ins.then_inc(s["s_ready"], 1)

            def att_turn(r):
                pe.wait_ge(s["pn_ready"], r + 1)
                pv = xtok[:, 1536 * r:1536 * (r + 1)].rearrange("p (h b s) -> p h b s", h=4, b=3)
                for i in range(4):
                    for b in range(3):
                        at = 512 * i + P * b
                        ins = nc.tensor.transpose(big[:, at:at + P], pv[:, i, b, :], ident)
                ins.then_inc(s["pT_ready"], 1)

            def att_values(r):
                pe.wait_ge(s["pT_out"], r + 1)
                if r == 0:
                    pe.wait_ge(bank_free[1], U_GA // 2)
                    pe.wait_ge(bank_free[0], U_GA // 2)
                else:
                    pe.wait_ge(s["om_out"], r)
                v = mv_tok.rearrange("p (t c) -> p t c", t=TT)
                pt_v = probs_T.rearrange("p (h s) -> p h s", h=4)
                for i in range(4):
                    h, at = 4 * r + i, TOK * i
                    mm(mid[:, at:at + TOK], v[:, 0, P * h:P * (h + 1)], pt_v[:, i, 0:TOK], start=True, stop=False)
                    ins = mm(mid[:, at + P:at + TOK], v[:, 1, P * h:P * (h + 1)], pt_v[:, i, TOK:384],
                             start=False, stop=True)
                ins.then_inc(s["pv_ready"], 1)

            turn(0, arena[:, 0:4096])
            pe.wait_ge(s["hT_out"], DC)
            g = 0
            for block in range(N_IN + N_UP + N_OUT):
                up = N_IN <= block < N_IN + N_UP
                if block < N_IN:
                    x_hi, x_lo = hT_hi, hT_lo
                elif up:
                    hgrn = block < N_IN + N_UP // 2
                    x_hi, x_lo = [by_head(v[:, :]) for v in ((oh_hi, oh_lo) if hgrn else (om_hi, om_lo))]
                    pe.wait_ge(s["oh_done" if hgrn else "om_done"], 1)
                else:
                    x_hi, x_lo = merged_hi, merged_lo
                tokens_out = block in (4, 5, 6, 7, 12, 13) or block >= N_IN + N_UP
                bites = UP_BITES if up else IN_BITES
                for i in range(bites):
                    pe.wait_ge(lo_ready, g + 1)
                    if block == N_IN + N_UP:
                        pe.wait_ge(s["merged_ready"], i + 1)
                    for half in range(2):
                        u = 2 * block + half
                        if i == 0:
                            open_bank(u)
                        for n in range(2):
                            k = 2 * i + n
                            first, last = k == 0, k == 2 * bites - 1
                            if tokens_out:
                                w_hi, w_lo = bite(g % BUFS, n)
                                toks = slice(P * half, P * (half + 1))
                                ins = products(acc[half][:, :], x_hi[:, k, toks], x_lo[:, k, toks], w_hi, w_lo,
                                               first, last)
                            else:
                                for c in range(2):
                                    w_hi, w_lo = bite(g % BUFS, n, 2 * half + c)
                                    ins = products(acc[half][:, TOK * c:TOK * (c + 1)], w_hi, w_lo,
                                                   x_hi[:, k, :], x_lo[:, k, :], first and c == 0, last and c == 0, c == 1)
                        if half:
                            ins.then_inc(bite_used, 1)
                        elif last:
                            ins.then_inc(first_ready, 1)
                    if block < N_IN:
                        extras(g)
                    g += 1
            assert g == DENSE

            turn(1, h_tok)
            pe.wait_ge(s["hT_out"], 2 * DC)
            pe.wait_ge(s["router_in"], 16)
            for t in range(TT):
                for j in range(DC):
                    ins = mm(mid[:, 36 * t:36 * (t + 1)], hT[:, j, P * t:P * (t + 1)], wr[:, j, :],
                             start=j == 0, stop=j == DC - 1)
            ins.then_inc(s["logits_ready"], 1)
            pe.wait_ge(s["onehot_ready"], 1)
            both = rt[:, 384:448].rearrange("p (t e) -> p t e", t=TT)
            before = const("before")
            mm(mid[:, 512:544], ones, both[:, 0, :], start=True, stop=False)
            mm(mid[:, 512:544], ones, both[:, 1, :], start=False, stop=True)
            mm(mid[:, 544:576], before, both[:, 0, :], start=True, stop=True)
            mm(mid[:, 576:608], before, both[:, 1, :], start=True, stop=False)
            mm(mid[:, 576:608], ones, both[:, 0, :], start=False, stop=True).then_inc(s["counts_ready"], 1)
            pe.wait_ge(s["sel_ready"], TT)
            for j in range(DC):
                if j >= 4:
                    pe.wait_ge(s["big_act" if j % 2 else "big_dve"], (j - 4) // 2 + 1)
                for t in range(TT):
                    rows = h_tok[:, t * D:(t + 1) * D].rearrange("p (c j) -> p j c", j=DC)[:, j, :]
                    ins = mm(big[:, 512 * (j % 4):512 * (j % 4 + 1)], rows, sel[:, t, :], start=t == 0, stop=t == 1)
                ins.then_inc(s["big_filled"], 1)
            pe.wait_ge(s["padded"], 5)

            pe.wait_ge(s["tab_ready"], 1)
            fold = const("fold")

            def folded(m):
                for c in range(FC):
                    ins = mm(mid[:, 512 * m + WIN * c:512 * m + WIN * (c + 1)],
                             gu_sb[:, FE * m + P * c:FE * m + P * (c + 1)], fold, start=True, stop=True)
                ins.then_inc(s["folded"], 1)

            pairs = pe.value_load(tab[0:1, PAIRS:PAIRS + 1], min_val=EXPERTS // 2, max_val=MAX_PAIRS)

            def down(a, b, buf):
                for n in range(2):
                    w_hi, w_lo = bite(buf, n)
                    c, bank = b // 2, 2 * (b % 2) + n
                    ins = products(big[:, 512 * bank:512 * (bank + 1)], hid_hi[a][:, c, :], hid_lo[a][:, c, :],
                                   w_hi, w_lo, c == 0 and a == 0, c == FC - 1 and a == 1)
                ins.then_inc(bite_used, 1)

            def turn_weights(m):
                pe.wait_ge(s["pair_ready"], m)
                for t in range(TT):
                    ins = nc.tensor.transpose(acc[0][:, P * t:P * (t + 1)], sel_pair[:, t, :], ident)
                ins.then_inc(s["selT_ready"], 1)

            def combine(m, v):
                if v == 0:
                    pe.wait_ge(s["selT_out"], m)
                    pe.wait_ge(s["big_act"], m * 2 + DC // 2)
                if v == 2:
                    pe.wait_ge(s["big_dve"], m * 10 + (DC // 2 - 8))
                if v >= 4:
                    pe.wait_ge(s["big_dve"], m * 10 + (DC // 2 - 8 + v - 3))
                n, t = v // 2, v % 2
                mm(big[:, 512 * (v % 4):512 * (v % 4 + 1)], sel_T[:, t, :], y_sb[:, 512 * n:512 * (n + 1)],
                   start=True, stop=True).then_inc(s["big_filled"], 1)

            def pair(m, start, at, first):
                for a in range(2):
                    for q in range(GU if first and a == 0 else PASS):
                        if q == 0:
                            pe.wait_ge(s["win_ready"], m * 2 + (a + 1))
                            if a == 1 and not first:
                                pe.wait_ge(s["selT_out"], m)
                        if q == GU:
                            pe.wait_ge(s["hid_ready"], m * 2 + a)
                            if a == 1:
                                pe.wait_ge(s["big_act"], m * 2 + DC // 2)
                                pe.wait_ge(s["big_dve"], m * 10 + DC // 2)
                        pe.wait_ge(lo_ready, start + (at[a] + q + 1))
                        buf = (at[a] + q) % BUFS
                        if q < GU:
                            for n in range(2):
                                w_hi, w_lo = bite(buf, n)
                                j = 2 * (q % 8) + n
                                mm(acc[q // 8][:, :], win[a][:, j, :], w_hi, start=j == 0, stop=False)
                                ins = mm(acc[q // 8][:, :], win[a][:, j, :], w_lo, start=False, stop=j == DC - 1)
                            ins.then_inc(bite_used, 1)
                        else:
                            down(1 - a, q - GU, buf)
                        if q == AT_FOLD_G:
                            pe.wait_ge(s["gu_out"], m * 4 + (2 * a + 1))
                            folded(0)
                        if q == AT_FOLD_U and not (first and a == 0):
                            pe.wait_ge(s["gu_out"], m * 4 + (2 * a + 2))
                            folded(1)
                        if first and a == 1 and q == AT_FOLD_U - GU:
                            pe.wait_ge(s["gu_out"], 2)
                            folded(1)
                        if a == 0 and q == AT_SELT and not first:
                            turn_weights(m)
                        if a == 1 and not first and 0 <= q - AT_COMB < 8:
                            combine(m, q - AT_COMB)

            pair(0, DENSE, FIRST_AT, True)
            with pe.Fori(1, pairs) as m:
                pair(m, pair_start(m), PAIR_AT, False)
            pe.wait_ge(s["hid_ready"], pairs * 2)
            for b in range(DOWN):
                pe.wait_ge(lo_ready, pair_start(pairs) + (b + 1))
                down(1, b, b % BUFS)
                if b == 0:
                    turn_weights(pairs)
            for v in range(8):
                combine(pairs, v)

            pe.wait_ge(s["big_dve"], pairs * 10 + DC // 2)
            turn(2, hp_tok)
            pe.wait_ge(s["hT_out"], 3 * DC)
            pe.wait_ge(s["ple_in"], 32)
            for b in range(N_PLE * IN_BITES):
                i, k2 = b // IN_BITES, 2 * (b % IN_BITES)
                if k2 == 0:
                    for t in range(TT):
                        v = 2 * i + t
                        if v >= 4:
                            pe.wait_ge(s["p_out"], v - 3)
                        for k in range(2):
                            mm(big[:, 512 * (v % 4):512 * (v % 4 + 1)], p_T[:, k, P * t:P * (t + 1)],
                               proj_sb[:, k, 512 * i:512 * (i + 1)], start=k == 0, stop=k == 1)
                pe.wait_ge(lo_ready, pair_start(pairs) + (DOWN + b + 1))
                for t in range(TT):
                    for n in range(2):
                        k = k2 + n
                        w_hi, w_lo = bite(b % BUFS, n)
                        ins = products(p_bank(2 * i + t), hT_hi[:, k, P * t:P * (t + 1)],
                                       hT_lo[:, k, P * t:P * (t + 1)], w_hi, w_lo, k == 0, k == DC - 1)
                    if t:
                        ins.then_inc(bite_used, 1)
                    elif k == DC - 1:
                        ins.then_inc(s["p_first"], 1)


def shape_constants():
    half = P // 2
    inv = 10000.0 ** (-np.arange(half, dtype=np.float32) / half)
    ang = np.arange(TOK, dtype=np.float32)[None, :] * inv.astype(np.float32)[:, None]
    cos = np.concatenate([np.cos(ang), np.cos(ang)], 0)
    sin = np.concatenate([np.sin(ang), np.sin(ang)], 0)
    rot = np.zeros((P, P), np.float32)
    for d in range(half):
        rot[d + half, d] = -1.0
        rot[d, d + half] = 1.0
    i = np.arange(P)
    parts = dict(ident=np.eye(P), rot=rot, cos=cos, sin=sin,
                 causal=np.where(i[None, :] <= i[:, None], 0.0, -1e30),
                 before=(i[:, None] < i[None, :]), ones=np.ones((P, P)),
                 desc=np.tile(np.arange(8, 0, -1), (P, 1)),
                 fold=np.concatenate([np.eye(WIN), np.eye(WIN)], 0),
                 times=np.tile(np.arange(TIMES), (P, 1)), zeros=np.zeros((P, 64)))
    consts = np.concatenate([np.asarray(parts[n], np.float32) for n in CONSTS], 1)
    masks = np.zeros((P, 7, P), np.float32)
    for n in range(7):
        span = i >> n
        masks[:, n, :] = (span[:, None] % 2 == 0) & (span[None, :] == span[:, None] + 1)
    return np.ascontiguousarray(consts), masks.reshape(P, 7 * P), np.arange(SLOTS, dtype=np.float32)[None, :]


def kernel(x, p, norm_mix_g, w_in, hgrn_lb_raw, hgrn_norm_g, w_up_hgrn, w_up_moba, w_out, norm_ffn_g,
           w_router_group, w_router_expert, w_exp_gate, w_exp_up, w_exp_down, norm_ple_g, w_ple_gate,
           w_ple_proj, norm_final_g):
    import concourse.bacc as bacc
    from concourse.bass_utils import run_bass_kernel_spmd

    a = np.asarray
    split = lambda w, n: a(w).reshape(P, 2, 8, n, 512).transpose(3, 1, 0, 2, 4).reshape(2 * n, P, HALF)
    plain = lambda w, k, n: a(w).reshape(k, 8, P, n, 512).transpose(3, 0, 2, 1, 4).reshape(k * n, P, HALF)
    halves = np.concatenate([split(w_in[0], N_IN), plain(w_up_hgrn[0], 1, 4), plain(w_up_moba[0], 1, 4),
                             plain(w_out[0], 2, N_OUT), split(w_ple_gate[0], N_PLE)], 0)
    cols = lambda g: a(g).reshape(P, DC)
    learned = np.concatenate([cols(norm_mix_g), cols(norm_ffn_g), cols(norm_ple_g),
                              a(hgrn_norm_g).reshape(P, 1),
                              a(hgrn_lb_raw).reshape(2, HEADS, P).transpose(2, 0, 1).reshape(P, 16)], 1)
    router = np.concatenate([a(w_router_group[0]).reshape(P, DC, GROUPS),
                             a(w_router_expert[0]).reshape(P, DC, EXPERTS)], 2)
    pt = a(p).reshape(TOK, 2, P).transpose(2, 1, 0)
    proj = a(w_ple_proj[0]).reshape(2, P, D).transpose(1, 0, 2)
    consts, masks, iota_row = shape_constants()
    arrays = dict(x=a(x).reshape(TOK, D), pt=pt, halves=halves, ple_proj=proj, learned=learned, router=router,
                  consts=consts, iota_row=iota_row, masks=masks, w_gate=a(w_exp_gate[0]), w_up=a(w_exp_up[0]),
                  w_down=a(w_exp_down[0]), g_final=a(norm_final_g).reshape(1, D))
    nc = bacc.Bacc("TRN2", target_bir_lowering=False, num_devices=1)
    arrays = {n: np.ascontiguousarray(v) for n, v in arrays.items()}
    aps = [nc.dram_tensor("in_" + n, v.shape, mybir.dt.from_np(v.dtype), kind="ExternalInput").ap()
           for n, v in arrays.items()]
    out = nc.dram_tensor("out", (TOK, D), F32, kind="ExternalOutput").ap()
    build_layer(nc, *aps, out)
    r = run_bass_kernel_spmd(nc, [{"in_" + n: v for n, v in arrays.items()}], core_ids=[0])
    return r.results[0]["out"].reshape(1, TOK, D)
```

```python
from contextlib import ExitStack

import concourse.bass as bass
import numpy as np
from concourse import mybir

F32 = mybir.dt.float32
F32R = mybir.dt.float32r
I32 = mybir.dt.int32
U8 = mybir.dt.uint8
ALU = mybir.AluOpType
ACT = mybir.ActivationFunctionType
AX = mybir.AxisListType

P = 128
TOK = 256
TT = TOK // P
D = 2048
DC = D // P
HEADS = 8
HW = HEADS * P
EXPERTS, GROUPS = 32, 4
PER_GROUP = EXPERTS // GROUPS
FE = 512
FC = FE // P
SLOTS = 2 * TOK
WIN = 64
PLE = 256
EPS = 1e-6
SCALE = float(P) ** -0.5
RING = 3
HALF = 4096
BITE = 1024
PER_HALF = HALF // BITE
BUFS = 4
MAX_PASSES = EXPERTS + SLOTS // WIN
MAX_PAIRS = MAX_PASSES // 2
TIMES = MAX_PASSES + 2

N_IN, N_UP, N_OUT, N_PLE = 22, 8, 4, 4
IN_BITES, UP_BITES = DC // 2, HEADS // 2
FIRST_UP = N_IN * IN_BITES
FIRST_OUT = FIRST_UP + N_UP * UP_BITES
DENSE = FIRST_OUT + N_OUT * IN_BITES
PASS = 24
PAIR = 2 * PASS
assert DENSE % (PER_HALF * RING) == 0 and PASS % (PER_HALF * RING) == 0
DENSE_HALVES, PLE_HALVES = DENSE // PER_HALF, N_PLE * IN_BITES // PER_HALF
U_HF, U_HI, U_HOG, U_MQ, U_MV, U_GA, U_GB, U_UPH, U_UPM, U_OUT, U_END = (
    4, 8, 12, 16, 24, 28, 36, 44, 52, 60, 68)
LEVELS = 9
AT_LEVEL, LEVEL_STEP = 36, 6
AT_BOUND = 8
AT_O, AT_OT, AT_ATT = 104, 114, (122, 144)
GU, DOWN = 16, 8
FIRST_AT, PAIR_AT = (0, GU), (0, PASS)
AT_FOLD_G, AT_FOLD_U, AT_SELT = 12, 20, 16
AT_GATE_OUT, AT_SILU, AT_UP_OUT, AT_HID, AT_SELT_OUT = 11, 16, 19, 24, 21
AT_Y, AT_COMB = 2, 2
LAG = 3

CONSTS = dict(ident=128, rot=128, cos=256, sin=256, causal=128, before=128, ones=128, zeros=64, desc=8, fold=64, times=42)
LEARNED = dict(g_mix=16, g_ffn=16, g_ple=16, g_hgrn=1, lb_raw=16)


def last_bite(block):
    return block * IN_BITES + IN_BITES - 1 if block < N_IN else (
        FIRST_UP + (block - N_IN + 1) * UP_BITES - 1 if block < N_IN + N_UP
        else FIRST_OUT + (block - N_IN - N_UP + 1) * IN_BITES - 1)


def at_rotate(k):
    return last_bite(U_MQ // 2 + k // 2) + 4 + 2 * (k % 2)


def block_ending(g):
    for block in range(N_IN + N_UP + N_OUT):
        if last_bite(block) == g:
            return block
    return None


def columns(table):
    out, at = {}, 0
    for name, n in table.items():
        out[name] = (at, at + n)
        at += n
    return out, at


CONST_AT, N_CONST = columns(CONSTS)
LEARNED_AT, N_LEARNED = columns(LEARNED)


def build_layer(nc, x, pt, halves, ple_proj, learned, router, consts, iota_row, masks, w_gate, w_up,
                w_down, g_final, out):
    projected = nc.dram_tensor("projected", [TT, P, D], F32).ap()
    gate_v = w_gate.rearrange("e (p j) f -> e p (j f)", p=P).rearrange("e p (two f) -> two e p f", two=2)
    up_v = w_up.rearrange("e (p j) f -> e p (j f)", p=P).rearrange("e p (two f) -> two e p f", two=2)
    down_v = w_down.rearrange("e (two c p) d -> two e p c d", two=2, p=P)

    with ExitStack() as ctx:
        def sb(name, shape, dt=F32):
            return ctx.enter_context(nc.sbuf_tensor(name, shape, dt))

        def sem(name):
            return ctx.enter_context(nc.semaphore(name))

        ring = [sb(f"ring{n}", [P, HALF]) for n in range(RING)]
        bite_hi = sb("bite_hi", [P, BUFS * BITE], F32R)
        bite_lo = sb("bite_lo", [P, BUFS * BITE], F32R)
        xtok = sb("xtok", [P, TT * D])
        hT_all = sb("hT_all", [P, 2 * DC * TOK])
        hT_at = nc.sbuf_base - 4 * 2 * DC * TOK
        arena = sb("arena", [P, 16384])
        arena_at = nc.sbuf_base - 4 * 16384
        work = sb("work", [P, 2048])
        work_at = nc.sbuf_base - 4 * 2048

        def over(name, base, first, n, dt=F32R):
            return nc.alloc_sbuf_tensor_at(name, [P, n], dt, offset=base + 4 * first)
        cst = sb("cst", [P, N_CONST])
        lrn = sb("lrn", [P, N_LEARNED])
        mask = sb("mask", [P, 7, P], U8)
        stat = sb("stat", [P, 192])

        def const(name):
            a, b = CONST_AT[name]
            return cst[:, a:b]

        def learnt(name):
            a, b = LEARNED_AT[name]
            return lrn[:, a:b]

        ident, ones = const("ident"), const("ones")
        x_t = [xtok[:, t * D:(t + 1) * D] for t in range(TT)]
        chunks = lambda ap, n: ap.rearrange("p (j t) -> p j t", j=n)
        hT_hi = chunks(over("hT_hi", hT_at, 0, DC * TOK)[:, :], DC)
        hT_lo = chunks(over("hT_lo", hT_at, DC * TOK, DC * TOK)[:, :], DC)
        merged_hi, merged_lo = hT_hi, hT_lo
        hT = chunks(hT_all[:, 0:DC * TOK], DC)

        def slab(n, k=1):
            return arena[:, 2048 * n:2048 * (n + k)]

        q_T, k_T, f_T = slab(0), slab(1), slab(2)
        v_tok, og_tok, mq_T, mk_T, mv_tok = slab(3), slab(4), slab(5), slab(6), slab(7)
        by_head = lambda ap: ap.rearrange("p (h t) -> p h t", h=HEADS)
        gate_a, gate_b = slab(1, 2), slab(5, 2)
        oh_hi, oh_lo = over("oh_hi", arena_at, 0, 2048), over("oh_lo", arena_at, 3 * 2048, 2048)
        om_hi, om_lo = over("om_hi", arena_at, 4 * 2048, 2048), over("om_lo", arena_at, 7 * 2048, 2048)
        probs_T = og_tok[:, 0:4 * 384]
        sc_T = xtok[:, 0:2048].rearrange("p (h b t) -> p h b t", h=HEADS, b=2)
        sc_off = xtok[:, 2048:3072].rearrange("p (h t) -> p h t", h=HEADS)
        spans = [f_T, xtok[:, 3072:4096], f_T[:, 0:512], f_T[:, 512:768], f_T[:, 768:896],
                 f_T[:, 896:960], f_T[:, 960:992]]
        h_hi = over("h_hi", arena_at, 0, TT * D)
        h_lo = over("h_lo", hT_at, DC * TOK, TT * D)
        h_tok = arena[:, 4096:8192]
        XW = SLOTS + WIN
        steps = cst[:, CONST_AT["ones"][0] + WIN:CONST_AT["zeros"][0] + WIN]
        xg_T = arena[:, 4096:4096 + DC * XW].rearrange("p (j s) -> p j s", j=DC)
        wr = arena[:, 14336:14336 + DC * 36].rearrange("p (j e) -> p j e", j=DC)
        rt = arena[:, 15360:16384]
        win = [over(f"win{a}", *at, DC * P)[:, :].rearrange("p (j s) -> p j s", j=DC)
               for a, at in enumerate(((arena_at, 0), (hT_at, 2048)))]
        gu_sb = arena[:, 2048:3072]
        hid_hi = [over(f"hid_hi{a}", *at, FC * P)[:, :].rearrange("p (c s) -> p c s", c=FC)
                  for a, at in enumerate(((arena_at, 3072), (hT_at, 0)))]
        hid_lo = [over(f"hid_lo{a}", *at, FC * P)[:, :].rearrange("p (c s) -> p c s", c=FC)
                  for a, at in enumerate(((arena_at, 3584), (hT_at, 512)))]
        rows_of = [slice(WIN * a, WIN * (a + 1)) for a in range(2)]
        silu_g = arena[:, 14336:14592]
        hid = arena[:, 14592:14848]
        table, table_2 = [hT_all[0:1, n:n + TIMES * EXPERTS].rearrange("p (n e) -> p n e", e=EXPERTS)
                          for n in (1024, 1024 + TIMES * EXPERTS)]
        sel = over("sel", work_at, SLOTS, TT * SLOTS)[:, :].rearrange("p (t s) -> p t s", t=TT)
        selw = hT_all[:, 5120:5120 + TT * XW].rearrange("p (t s) -> p t s", t=TT)
        part0 = 5120 + TT * XW
        sel_cols = hT_all[:, part0:part0 + 256].rearrange("p (t s) -> p t s", t=TT)
        own = hT_all[:, part0 + 256:part0 + 384]
        sel_pair = hT_all[:, part0 + 384:part0 + 640].rearrange("p (t s) -> p t s", t=TT)
        sel_T = hT_all[:, part0 + 640:part0 + 896].rearrange("p (t s) -> p t s", t=TT)
        iota = work[:, 0:SLOTS]
        sel_cols_2 = hT_all[:, part0 + 900:part0 + 900 + 512]
        wait_taker = hT_all[0:1, part0 + 896:part0 + 897]
        y_sb = work[:, :]
        squares_of = [arena[:, 2048:4096], arena[:, 12288:14336]]
        times_g = arena[:, 8192:12288]
        proj_sb = arena[:, 8192:12288].rearrange("p (c d) -> p c d", c=2)
        p_T = work[:, 1536:2048].rearrange("p (c t) -> p c t", c=2)
        stage = arena[:, 12288:14336].rearrange("p (b d) -> p b d", b=4)
        proj_back = arena[:, 4096:8192].rearrange("p (t d) -> p t d", t=TT)
        sig_p = work[:, 512:1536].rearrange("p (b d) -> p b d", b=2)
        g_fin = arena[:, 0:2048]
        diag = arena[:, 14912:15168].rearrange("p (t s) -> p t s", t=TT)

        tab = sb("tab", [1, 3 * TIMES + 2], I32)
        BIG_ACT, BIG_DVE = DC, DC
        EXPERT_OF, SLOT_OF, OFF_OF, PASSES, PAIRS = 0, TIMES, 2 * TIMES, 3 * TIMES, 3 * TIMES + 1

        acc = [ctx.enter_context(nc.psum_tensor(f"acc{b}", [P, 512], F32)) for b in range(2)]
        mid = ctx.enter_context(nc.psum_tensor("mid", [P, 1024], F32))
        big = ctx.enter_context(nc.psum_tensor("big", [P, 2048], F32))

        raw_in = [sem(f"raw_in{n}") for n in range(RING)]
        x_in = [sem(f"x_in{t}") for t in range(TT)]
        consts_in, masks_in = sem("consts_in"), sem("masks_in")
        hi_ready, lo_ready = sem("hi_ready"), sem("lo_ready")
        bite_used = sem("bite_used")
        first_ready = sem("first_ready")
        bank_free = [sem(f"bank_free{b}") for b in range(2)]
        proj_saved = [sem(f"proj_saved{b}") for b in range(4)]
        dve_step = sem("dve_step")
        act_step = sem("act_step")
        names = ("sq_done ms_ready root_ready h_ready hT_bank hT_hi_out hT_out rot_ready roped "
                 "fk_sig lvl_ready lvl_done off_copied o_ready osq_done oms_ready oroot_ready on_ready oT_ready "
                 "oh_hi_out oh_done s_ready mx_ready exp_done pn_ready pT_ready pT_out pv_ready om_out om_hi_out "
                 "om_done lb_exp lb_max sum_ready merged_hi_out merged_ready x_again router_in logits_ready "
                 "gexp_in gexp_out wexp_in wexp_out onehot_ready counts_ready sel_ready big_filled "
                 "big_act big_dve padded tab_ready win_hi_out win_ready cols_ready pair_ready selT_ready selT_out gu_out folded "
                 "silu_done hid_hi_out hid_ready iota_in proj_in proj_done proj_out proj_again p_first "
                 "p_out_act p_out g_fin_in fin_act fin_dve r_ready times_g_ready h_split h_lo_ready win0_hi stored").split()
        s = {n: sem(n) for n in names}

        block = ctx.enter_context(nc.Block())

        def p_bank(v):
            return acc[v % 2][:, :] if v // 2 % 2 == 0 else mid[:, 512 * (v % 2):512 * (v % 2 + 1)]

        def proj_bank(v):
            return big[:, 512 * v:512 * (v + 1)] if v < 2 else acc[v % 2][:, :]

        def unit_stands(engine, u):
            if u % 2:
                engine.wait_ge(bite_used, last_bite(u // 2) + 1)
            else:
                engine.wait_ge(first_ready, u // 2 + 1)

        def pair_start(m):
            return m * PAIR + (DENSE - DOWN)

        def later(m, b):
            h = (DENSE - DOWN + b) // PER_HALF
            return (h % RING, b % PER_HALF, b % BUFS, m * (16 * PAIR // PER_HALF // RING) + landed(h),
                    m * PAIR + (DENSE - DOWN + b))

        def landed(half):
            return 16 * (half // RING + 1)

        @block.sync
        def _(sp):
            xv = x.rearrange("(t p) d -> t p d", p=P)
            for t in range(TT):
                sp.dma_start(x_t[t], xv[t]).then_inc(x_in[t], 16)
            sp.dma_start(cst[:, :], consts).then_inc(consts_in, 16)
            sp.dma_start(lrn[:, :], learned).then_inc(consts_in, 16)

            def load_dense(i, slot):
                sp.dma_start(ring[slot][:, :], halves[i]).then_inc(raw_in[slot], 16)

            def load_expert(e, i, slot):
                if i < 4:
                    src = (gate_v, up_v)[i // 2][i % 2][bass.ds(e, 1)].rearrange("e p f -> (e p) f")
                    sp.dma_start(ring[slot][:, :], src).then_inc(raw_in[slot], 16)
                else:
                    src = down_v[i % 2][bass.ds(e, 1)].rearrange("e p c d -> (e p) c d")
                    sp.dma_start(ring[slot][:, :].rearrange("p (c d) -> p c d", c=2), src)\
                      .then_inc(raw_in[slot], 16)

            for h in range(DENSE_HALVES):
                if h >= RING:
                    sp.wait_ge(lo_ready, PER_HALF * (h - RING + 1))
                load_dense(h, h % RING)
                if h == 0:
                    sp.dma_start(work[:, 0:7 * P], masks).then_inc(masks_in, 16)
                if h == FIRST_OUT // PER_HALF + 4:
                    sp.wait_ge(bite_used, FIRST_OUT)
                    sp.wait_ge(s["sum_ready"], 8)
                    sp.dma_start(proj_sb, ple_proj).then_inc(s["proj_in"], 16)
                    sp.wait_ge(s["om_done"], 1)
                    sp.dma_start(p_T, pt).then_inc(s["proj_in"], 16)
                if h == (AT_ATT[1] + 20) // PER_HALF + 2:
                    sp.wait_ge(s["pT_ready"], 2)
                    for t in range(TT):
                        sp.dma_start(x_t[t], xv[t]).then_inc(s["x_again"], 16)
            for i in range(4):
                if i == RING:
                    sp.wait_ge(bite_used, FIRST_OUT)
                    sp.dma_start(wr, router).then_inc(s["router_in"], 16)
                    for b in range(2):
                        sp.wait_ge(bank_free[b], U_END // 2)
                    sp.dma_start(iota, iota_row.partition_broadcast(P)).then_inc(s["iota_in"], 16)
                    for v in range(8):
                        sp.wait_ge(s["proj_out"], v + 1)
                        sp.dma_start(projected[v % 2][:, 512 * (v // 2):512 * (v // 2 + 1)], stage[:, v % 4, :])\
                          .then_inc(proj_saved[v % 4], 16)
                sp.wait_ge(lo_ready, DENSE + PER_HALF * (i - RING + 1))
                load_expert(0, i, i % RING)
            sp.wait_ge(s["tab_ready"], 1)
            passes = sp.value_load(tab[0:1, PASSES:PASSES + 1], min_val=EXPERTS, max_val=MAX_PASSES)

            def load_pass(n, part):
                e = sp.value_load(tab[0:1, bass.ds(n + (EXPERT_OF - (part[0] >= 4)), 1)], min_val=0,
                                  max_val=EXPERTS - 1)
                for i in part:
                    sp.wait_ge(lo_ready, n * PASS + (DENSE - DOWN + PER_HALF * (i - RING + 1)))
                    load_expert(e, i, (i + 1) % RING)

            with sp.Fori(1, passes) as n:
                load_pass(n, range(4))
                load_pass(n, range(4, 6))
            e = sp.value_load(tab[0:1, bass.ds(passes + (EXPERT_OF - 1), 1)], min_val=0, max_val=EXPERTS - 1)
            for i in range(2):
                sp.wait_ge(lo_ready, passes * PASS + (DENSE - DOWN + PER_HALF * (i - RING + 1)))
                load_expert(e, 4 + i, (i + 1) % RING)

            def load_ple(i):
                sp.wait_ge(lo_ready, passes * PASS + (DENSE + PER_HALF * (i - RING + 1)))
                load_dense(DENSE_HALVES + i, i % RING)

            load_ple(0)
            sp.wait_ge(s["win_ready"], passes + 2)
            for b in range(4):
                sp.wait_ge(proj_saved[b], 32)
            sp.dma_start(proj_back, projected.rearrange("t p d -> p t d")).then_inc(s["proj_again"], 16)
            load_ple(1)
            load_ple(2)
            pairs = sp.value_load(tab[0:1, PAIRS:PAIRS + 1], min_val=EXPERTS // 2, max_val=MAX_PAIRS)
            sp.wait_ge(s["big_filled"], pairs * 8 + DC)
            sp.dma_start(g_fin, g_final.partition_broadcast(P)).then_inc(s["g_fin_in"], 16)
            for i in range(RING, PLE_HALVES):
                load_ple(i)
            ov = out.rearrange("(t p) d -> t p d", p=P)
            for t in range(TT):
                sp.wait_ge(s[("fin_dve", "fin_act")[t]], 1)
                sp.dma_start(ov[t], times_g[:, t * D:(t + 1) * D]).then_inc(s["stored"], 16)
            sp.wait_ge(s["stored"], 16 * TT)

        @block.gpsimd
        def _(pool):
            tt, copy = nc.gpsimd.tensor_tensor, nc.gpsimd.tensor_copy
            pool.wait_ge(s["om_out"], 2)
            copy(om_hi[:, :], work[:, :]).then_inc(s["om_hi_out"], 1)
            pool.wait_ge(s["om_hi_out"], 1)
            tt(om_lo[:, :], work[:, :], om_hi[:, :].bitcast(F32), ALU.subtract).then_inc(s["om_done"], 1)
            for i in range(8):
                pool.wait_ge(s["sum_ready"], i + 1)
                part = gate_a[:, 512 * i:512 * (i + 1)].rearrange("p (c t) -> p c t", c=2)
                hi, lo = merged_hi[:, 2 * i:2 * i + 2, :], merged_lo[:, 2 * i:2 * i + 2, :]
                copy(hi, part).then_inc(s["merged_hi_out"], 1)
                pool.wait_ge(s["merged_hi_out"], i + 1)
                tt(lo, part, hi.bitcast(F32), ALU.subtract).then_inc(s["merged_ready"], 1)

            def window(a, slot, hi_count):
                src = xg_T[:, :, bass.ds(slot, WIN)]
                copy(win[a][:, :, 0:WIN], src).then_inc(s["win_hi_out"], 1)
                pool.wait_ge(s["win_hi_out"], hi_count)
                tt(wait_taker, ident[0:1, 0:1], ident[0:1, 0:1], ALU.mult).then_inc(s["win_hi_out"], 1)
                tt(win[a][:, :, WIN:P], src, win[a][:, :, 0:WIN].bitcast(F32), ALU.subtract)\
                    .then_inc(s["win_ready"], 1)

            pool.wait_ge(s["h_split"], 4)
            tt(h_lo[:, :], h_tok, h_hi[:, :].bitcast(F32), ALU.subtract).then_inc(s["h_lo_ready"], 1)

            pool.wait_ge(s["big_act"], DC)
            nc.gpsimd.memset(xg_T[:, :, SLOTS:XW], 0.0).then_inc(s["padded"], 1)
            for a in range(2):
                other = rows_of[1 - a]
                nc.gpsimd.memset(hid_hi[a][:, :, other].bitcast(F32), 0.0).then_inc(s["padded"], 1)
                nc.gpsimd.memset(hid_lo[a][:, :, other].bitcast(F32), 0.0).then_inc(s["padded"], 1)
            pool.wait_ge(s["padded"], 5)

            def index(first, n, top):
                return pool.value_load(tab[0:1, bass.ds(n + first, 1)], min_val=0, max_val=top)

            def pair_part(n, count, turned=None):
                slots = [index(SLOT_OF + a, n, SLOTS) for a in range(2)]
                offs = [index(OFF_OF + a, n, WIN) for a in range(2)]
                if turned is not None:
                    pool.wait_ge(s["selT_ready"], turned)
                for a in range(2):
                    copy(sel_cols[:, :, rows_of[a]], selw[:, :, bass.ds(slots[a], WIN)]).then_inc(s["cols_ready"], 1)
                for a in range(2):
                    copy(own[:, rows_of[a]], steps[:, bass.ds(offs[a], WIN)]).then_inc(s["cols_ready"], 1)
                pool.wait_ge(s["cols_ready"], count)
                tt(sel_pair, sel_cols, own.unsqueeze(1).broadcast_to([P, TT, P]), ALU.mult)\
                    .then_inc(s["pair_ready"], 1)

            pool.wait_ge(s["tab_ready"], 1)
            pool.wait_ge(s["win_ready"], 1)
            window(1, index(SLOT_OF + 1, 0, SLOTS), 1)
            pool.wait_ge(s["sel_ready"], 2 * TT)
            pair_part(0, 4)
            pairs = pool.value_load(tab[0:1, PAIRS:PAIRS + 1], min_val=EXPERTS // 2, max_val=MAX_PAIRS)

            def next_pair(m, start, at):
                for a in range(2):
                    slot = index(SLOT_OF + a + 2, m * 2, SLOTS)
                    pool.wait_ge(bite_used, start + (at[a] + GU))
                    window(a, slot, m * 4 + (2 * a + 3))
                pair_part(m * 2 + 2, m * 4 + 8, m + 1)

            next_pair(0, DENSE, FIRST_AT)
            with pool.Fori(1, pairs) as m:
                next_pair(m, pair_start(m), PAIR_AT)

        @block.scalar
        def _(act):
            count = [0]

            def then(ins):
                count[0] += 1
                ins.then_inc(act_step, 1)
                act.wait_ge(act_step, count[0])

            def squares(n, into, src):
                for t in range(TT):
                    if n == 0:
                        act.wait_ge(x_in[t], 16)
                    nc.scalar.activation(into[:, t * D:(t + 1) * D], src[t], ACT.Square,
                                         accum_out=stat[:, 2 * n + t:2 * n + t + 1]).then_inc(s["sq_done"], 1)

            def root_table():
                nc.scalar.activation(stat[:, 190:191], stat[:, 8:9], ACT.Sqrt)

            def part_squares(v):
                c, t = v // 2, v % 2
                w = slice(512 * c, 512 * (c + 1))
                nc.scalar.activation(squares_of[t][:, w], x_t[t][:, w], ACT.Square,
                                     accum_out=stat[:, 16 + 4 * t + c:17 + 4 * t + c]).then_inc(s["sq_done"], 1)

            def root(n):
                act.wait_ge(s["ms_ready"], n + 1)
                nc.scalar.activation(stat[:, 8 + 2 * n:10 + 2 * n], stat[:, 8 + 2 * n:10 + 2 * n],
                                     ACT.Sqrt).then_inc(s["root_ready"], 1)

            def hi(slot, quarter, buf, fallen, used):
                if fallen is not None:
                    act.wait_ge(raw_in[slot], fallen)
                if used is not None:
                    act.wait_ge(bite_used, used)
                nc.scalar.activation(bite_hi[:, BITE * buf:BITE * (buf + 1)],
                                     ring[slot][:, BITE * quarter:BITE * (quarter + 1)], ACT.Copy)\
                    .then_inc(hi_ready, 1)

            def hi_dense(g):
                h = g // PER_HALF
                hi(h % RING, g % PER_HALF, g % BUFS, landed(h) if g % PER_HALF == 0 else None,
                   g - BUFS + 1 if g >= BUFS else None)

            def hi_later(m, b):
                slot, quarter, buf, fallen, number = later(m, b)
                hi(slot, quarter, buf, fallen if quarter == 0 else None, number - (BUFS - 1))

            def turned_hi(n, k, gain):
                for j in range(DC):
                    act.wait_ge(s["hT_bank"], DC * n + 2 * (j // 2) + 2)
                    q = (j // 2 % 4) * 512 + 256 * (j % 2)
                    nc.scalar.activation(hT_hi[:, j, :], big[:, q:q + 256], ACT.Copy, scale=gain[:, j:j + 1])\
                        .then_inc(s["hT_hi_out"], 1)
                    if n == 0 and j in (3, 7):
                        hi_dense(j // 2 - 1)
                        hi_dense(j // 2)

            squares(0, arena[:, 0:4096], x_t)
            root(0)
            act.wait_ge(consts_in, 32)
            turned_hi(0, 0, learnt("g_mix"))

            lb = stat[:, 32:48]

            def evacuate(u):
                bank = acc[u % 2]
                unit_stands(act, u)
                free = bank_free[u % 2]
                if u < U_HF:
                    nc.scalar.activation(q_T[:, 512 * u:512 * (u + 1)], bank[:, :], ACT.Silu).then_inc(free, 1)
                elif u < U_HI:
                    w = slice(512 * (u - U_HF), 512 * (u - U_HF + 1))
                    nc.scalar.activation(f_T[:, w], bank[:, :], ACT.Sigmoid).then_inc(s["fk_sig"], 1)
                    nc.scalar.activation(k_T[:, w], bank[:, :], ACT.Sigmoid, scale=-1.0).then_inc(free, 1)
                elif u < U_MQ:
                    base, dst = (U_HI, v_tok) if u < U_HOG else (U_HOG, og_tok)
                    c, t = (u - base) // 2, (u - base) % 2
                    nc.scalar.activation(dst[:, t * HW + 512 * c:t * HW + 512 * (c + 1)], bank[:, :],
                                         ACT.Copy if dst is v_tok else ACT.Silu).then_inc(free, 1)
                elif u < U_MV:
                    k = u - U_MQ
                    dst = (mq_T, mk_T)[k // 4][:, 512 * (k % 4):512 * (k % 4 + 1)]
                    nc.scalar.activation(dst, bank[:, :], ACT.Copy).then_inc(free, 1)
                elif u < U_GA:
                    c, t = (u - U_MV) // 2, (u - U_MV) % 2
                    nc.scalar.activation(mv_tok[:, t * HW + 512 * c:t * HW + 512 * (c + 1)], bank[:, :],
                                         ACT.Copy).then_inc(free, 1)
                elif u < U_UPH:
                    if u == U_GA:
                        act.wait_ge(s["lvl_done"], LEVELS)
                        act.wait_ge(s["off_copied"], 1)
                    if u == U_GB:
                        act.wait_ge(s["s_ready"], 2)
                    dst, base = (gate_a, U_GA) if u < U_GB else (gate_b, U_GB)
                    w = slice(512 * (u - base), 512 * (u - base + 1))
                    nc.scalar.activation(dst[:, w], bank[:, :], ACT.Sigmoid).then_inc(free, 1)

            def softmax(r):
                act.wait_ge(s["mx_ready"], r + 1)
                sm = xtok[:, 1536 * r:1536 * (r + 1)].rearrange("p (h s) -> p h s", h=4)
                for h in range(4):
                    for t, (a, b) in enumerate(((0, 128), (128, 384))):
                        k = 4 * t + h
                        nc.scalar.activation(sm[:, h, a:b], sm[:, h, a:b], ACT.Exp,
                                             bias=stat[:, 112 + k:113 + k], scale=SCALE,
                                             accum_out=stat[:, 120 + k:121 + k]).then_inc(s["exp_done"], 1)

            for g in range(LAG, DENSE + LAG):
                if g >= BUFS:
                    hi_dense(g)
                block = block_ending(g - LAG)
                if block is not None and block < U_UPH // 2:
                    evacuate(2 * block)
                    evacuate(2 * block + 1)
                if block == U_END // 2 - 1:
                    root_table()
                if block is not None and block >= U_OUT // 2:
                    for u in (2 * block, 2 * block + 1):
                        act.wait_ge(bank_free[u % 2], u // 2 + 1)
                        part_squares(u - U_OUT)
                if g == AT_BOUND:
                    act.wait_ge(s["lb_max"], 1)
                    nc.scalar.activation(lb, lb, ACT.Exp).then_inc(s["lb_exp"], 1)
                if g == AT_LEVEL + LEVEL_STEP * (LEVELS - 1) + LAG:
                    act.wait_ge(s["lvl_done"], LEVELS)
                    nc.scalar.activation(sc_off, big[:, 0:1024].rearrange("p (h t) -> p h t", h=HEADS),
                                         ACT.Copy).then_inc(s["off_copied"], 1)
                if g == AT_O + LAG:
                    act.wait_ge(s["o_ready"], 1)
                    act.wait_ge(s["roped"], 8)
                    nc.scalar.activation(work[:, :], big[:, :], ACT.Square).then_inc(s["osq_done"], 1)
                if g == AT_O + LAG + 2:
                    act.wait_ge(s["oms_ready"], 1)
                    nc.scalar.activation(stat[:, 48:64], stat[:, 48:64], ACT.Sqrt).then_inc(s["oroot_ready"], 1)
                if g == AT_OT + LAG:
                    act.wait_ge(s["oT_ready"], 1)
                    act.wait_ge(s["lvl_done"], LEVELS)
                    nc.scalar.activation(oh_hi[:, :], big[:, :], ACT.Copy, scale=learnt("g_hgrn"))\
                      .then_inc(s["oh_hi_out"], 1)
                for r, at in enumerate(AT_ATT):
                    if g == at + LAG + 2:
                        softmax(r)
                    if g == at + 20:
                        act.wait_ge(s["pv_ready"], r + 1)
                        nc.scalar.activation(work[:, 1024 * r:1024 * (r + 1)], mid[:, :], ACT.Copy)\
                          .then_inc(s["om_out"], 1)

            root(1)

            def projected_out(v):
                act.wait_ge(s["proj_done"], v + 1)
                if v >= 4:
                    act.wait_ge(proj_saved[v % 4], 16)
                nc.scalar.activation(stage[:, v % 4, :], proj_bank(v), ACT.Copy).then_inc(s["proj_out"], 1)

            projected_out(0)
            projected_out(1)
            act.wait_ge(s["h_ready"], 2 * TT)
            for t in range(TT):
                w = slice(t * D, (t + 1) * D)
                for dst in (h_hi, h_tok):
                    nc.scalar.activation(dst[:, w], x_t[t], ACT.Copy, scale=stat[:, 10 + t:11 + t])\
                        .then_inc(s["h_split"], 1)
            act.wait_ge(s["gexp_in"], 1)
            ge = rt[:, 72:80]
            nc.scalar.activation(ge, ge, ACT.Exp).then_inc(s["gexp_out"], 1)
            projected_out(2)
            projected_out(3)
            act.wait_ge(s["wexp_in"], 1)
            we = rt[:, 200:202]
            nc.scalar.activation(we, we, ACT.Exp).then_inc(s["wexp_out"], 1)
            for v in range(4, 8):
                projected_out(v)

            act.wait_ge(s["h_lo_ready"], 1)
            for j in range(DC):
                act.wait_ge(s["big_filled"], j + 1)
                if j == 14:
                    for b in range(4):
                        act.wait_ge(proj_saved[b], 32)
                nc.scalar.activation(xg_T[:, j, 0:SLOTS], big[:, 512 * (j % 4):512 * (j % 4 + 1)], ACT.Copy,
                                     scale=learnt("g_ffn")[:, j:j + 1]).then_inc(s["big_act"], 1)
            act.wait_ge(s["big_act"], DC)
            nc.scalar.activation(win[0][:, :, 0:WIN], xg_T[:, :, 0:WIN], ACT.Copy).then_inc(s["win0_hi"], 1)


            def beside(m, start, at, b):
                for a in range(2):
                    if b == at[a] + AT_GATE_OUT:
                        act.wait_ge(bite_used, start + (at[a] + GU // 2))
                        nc.scalar.activation(gu_sb[:, 0:FE], acc[0][:, :], ACT.Copy).then_inc(s["gu_out"], 1)
                    if b == at[a] + AT_UP_OUT:
                        act.wait_ge(bite_used, start + (at[a] + GU))
                        nc.scalar.activation(gu_sb[:, FE:2 * FE], acc[1][:, :], ACT.Copy).then_inc(s["gu_out"], 1)
                    if b == at[a] + AT_SILU:
                        act.wait_ge(s["folded"], m * 4 + (2 * a + 1))
                        nc.scalar.activation(silu_g, mid[:, 0:FC * WIN], ACT.Silu).then_inc(s["silu_done"], 1)

            def turned_weights(m):
                act.wait_ge(s["selT_ready"], m)
                nc.scalar.activation(sel_T, acc[0][:, 0:TOK].rearrange("p (t s) -> p t s", t=TT),
                                     ACT.Copy).then_inc(s["selT_out"], 1)

            def rows_out(stands):
                act.wait_ge(bite_used, stands)
                for k in range(2):
                    nc.scalar.activation(y_sb[:, 512 * k:512 * (k + 1)], big[:, 512 * k:512 * (k + 1)],
                                         ACT.Copy).then_inc(s["big_act"], 1)

            for b in range(LAG, PAIR - DOWN + LAG):
                hi_dense(DENSE + b)
                beside(0, DENSE, FIRST_AT, b)
            act.wait_ge(s["tab_ready"], 1)
            pairs = act.value_load(tab[0:1, PAIRS:PAIRS + 1], min_val=EXPERTS // 2, max_val=MAX_PAIRS)
            with act.Fori(1, pairs) as m:
                for b in range(LAG, PAIR + LAG):
                    hi_later(m, b)
                    beside(m, pair_start(m), PAIR_AT, b)
                    if b == AT_SELT_OUT:
                        turned_weights(m)
                    if b == PASS + AT_Y:
                        rows_out(pair_start(m) + PASS)
            for b in range(LAG, DOWN + LAG + 1):
                hi_later(pairs, b)
                if b == LAG:
                    turned_weights(pairs)
                if b == DOWN + AT_Y:
                    rows_out(pair_start(pairs) + DOWN)

            act.wait_ge(s["win_ready"], pairs * 2 + 2)
            root_table()
            for v in range(8):
                act.wait_ge(s["big_dve"], pairs * 10 + (BIG_DVE + v - 7))
                part_squares(v)
            root(2)
            act.wait_ge(s["pair_ready"], pairs + 1)
            turned_hi(2, 1, learnt("g_ple"))

            def part_of_x4(c):
                for v in (2 * c, 2 * c + 1):
                    act.wait_ge(s["p_out"], v + 1)
                    part_squares(v)

            for b in range(LAG + 1, N_PLE * IN_BITES + LAG):
                if b < N_PLE * IN_BITES:
                    hi_later(pairs, DOWN + b)
                if (b - LAG) % IN_BITES == 1 and b - LAG > IN_BITES:
                    part_of_x4((b - LAG) // IN_BITES - 1)
                if (b - LAG) % IN_BITES == IN_BITES - 1:
                    for t in range(TT):
                        v = 2 * ((b - LAG) // IN_BITES) + t
                        if t == 0:
                            act.wait_ge(s["p_first"], v // 2 + 1)
                        else:
                            act.wait_ge(bite_used, pair_start(pairs) + (DOWN + b - LAG + 1))
                        if v >= 2:
                            act.wait_ge(s["p_out"], v - 1)
                        nc.scalar.activation(sig_p[:, v % 2, :], p_bank(v), ACT.Sigmoid).then_inc(s["p_out_act"], 1)
            root_table()
            part_of_x4(N_PLE - 1)
            root(3)
            act.wait_ge(s["r_ready"], 1)
            act.wait_ge(s["times_g_ready"], 8)
            nc.scalar.activation(times_g[:, D:2 * D], times_g[:, D:2 * D], ACT.Copy, scale=stat[:, 15:16])\
                .then_inc(s["fin_act"], 1)

        @block.vector
        def _(dve):
            count = [0]
            tt, ts, stt = nc.vector.tensor_tensor, nc.vector.tensor_scalar, nc.vector.scalar_tensor_tensor

            def then(ins):
                count[0] += 1
                ins.then_inc(dve_step, 1)
                dve.wait_ge(dve_step, count[0])

            def factors(n):
                parts = n > 0
                dve.wait_ge(s["sq_done"], 8 * n + 2)
                r = stat[:, 8 + 2 * n:10 + 2 * n]
                if parts:
                    then(nc.vector.tensor_reduce(r, stat[:, 16:24].rearrange("p (t c) -> p t c", t=TT), AX.X, ALU.add))
                ts(r, r if parts else stat[:, 0:2], 1.0 / D, EPS, ALU.mult, ALU.add).then_inc(s["ms_ready"], 1)
                dve.wait_ge(s["root_ready"], n + 1)
                if n == 3:
                    nc.vector.reciprocal(r, r).then_inc(s["r_ready"], 1)
                    dve.wait_ge(s["r_ready"], 1)
                    return r
                then(nc.vector.reciprocal(r, r))
                if n == 0:
                    dve.wait_ge(consts_in, 32)
                for t in range(TT):
                    ts(diag[:, t, :], ident, r[:, t:t + 1], None, ALU.mult).then_inc(s["h_ready"], 1)

            def turned(n, gain):
                for j in range(DC):
                    dve.wait_ge(s["hT_bank"], DC * n + 2 * (j // 2) + 2)
                    q = (j // 2 % 4) * 512 + 256 * (j % 2)
                    ts(hT[:, j, :], big[:, q:q + 256], gain[:, j:j + 1], None, ALU.mult)\
                        .then_inc(s["big_dve"], 1)

            def turned_lo(k, gain):
                for j in range(DC):
                    dve.wait_ge(s["hT_hi_out"], DC * k + 2 * (j // 2) + 2)
                    q = (j // 2 % 4) * 512 + 256 * (j % 2)
                    stt(hT_lo[:, j, :], big[:, q:q + 256], gain[:, j:j + 1], hT_hi[:, j, :].bitcast(F32),
                        ALU.mult, ALU.subtract).then_inc(s["hT_out"], 1)
                    if k == 0 and j in (3, 7):
                        lo_dense(j // 2 - 1)
                        lo_dense(j // 2)

            def lo(slot, quarter, buf, ready):
                at = slice(BITE * buf, BITE * (buf + 1))
                dve.wait_ge(hi_ready, ready)
                tt(bite_lo[:, at], ring[slot][:, BITE * quarter:BITE * (quarter + 1)], bite_hi[:, at].bitcast(F32),
                   ALU.subtract).then_inc(lo_ready, 1)

            def lo_dense(g):
                lo(g // PER_HALF % RING, g % PER_HALF, g % BUFS, g + 1)

            def lo_later(m, b):
                slot, quarter, buf, _, number = later(m, b)
                lo(slot, quarter, buf, number + 1)

            factors(0)
            turned_lo(0, learnt("g_mix"))
            dve.wait_ge(masks_in, 16)
            then(nc.vector.tensor_copy(mask[:, :, :], work[:, 0:7 * P].rearrange("p (n t) -> p n t", n=7)))

            lb = stat[:, 32:48]
            raw = learnt("lb_raw")
            then(tt(stat[:, 64:72], raw[:, 0:8], raw[:, 8:16], ALU.max))
            then(tt(lb[:, 0:8], raw[:, 0:8], stat[:, 64:72], ALU.subtract))
            tt(lb[:, 8:16], raw[:, 8:16], stat[:, 64:72], ALU.subtract).then_inc(s["lb_max"], 1)
            lbv, lbc = stat[:, 72:80], stat[:, 80:88]

            def bound():
                dve.wait_ge(s["lb_exp"], 1)
                then(tt(stat[:, 64:72], lb[:, 0:8], lb[:, 8:16], ALU.add))
                then(nc.vector.reciprocal(stat[:, 64:72], stat[:, 64:72]))
                then(tt(stat[:, 72:80], lb[:, 0:8], stat[:, 64:72], ALU.mult))
                then(tt(stat[:, 80:88], lb[:, 8:16], stat[:, 64:72], ALU.mult))

            def forget(u):
                dve.wait_ge(s["fk_sig"], u - U_HF + 1)
                dve.wait_ge(bank_free[u % 2], u // 2 + 1)
                for h in range(2 * (u - U_HF), 2 * (u - U_HF) + 2):
                    w = slice(TOK * h, TOK * (h + 1))
                    ts(f_T[:, w], f_T[:, w], lbc[:, h:h + 1], lbv[:, h:h + 1], ALU.mult, ALU.add)
                    ins = ts(k_T[:, w], k_T[:, w], lbc[:, h:h + 1], None, ALU.mult)
                then(ins)

            def rope(k):
                raw_u = (mq_T, mk_T)[k // 4][:, 512 * (k % 4):512 * (k % 4 + 1)].rearrange("p (h t) -> p h t", h=2)
                tmp = work[:, 0:512].rearrange("p (h t) -> p h t", h=2)
                wide = lambda n: const(n).unsqueeze(1).broadcast_to([P, 2, TOK])
                dve.wait_ge(s["rot_ready"], k + 1)
                rot_ps = mid[:, 0:512].rearrange("p (h t) -> p h t", h=2)
                then(tt(tmp, rot_ps, wide("sin"), ALU.mult))
                then(tt(raw_u, raw_u, wide("cos"), ALU.mult))
                ins = tt(raw_u, raw_u, tmp, ALU.add)
                ins.then_inc(s["roped"], 1)
                dve.wait_ge(s["roped"], k + 1)

            def level(n):
                dve.wait_ge(s["lvl_done"], n + 1)
                sc = xtok[:, 0:2048].rearrange("p (m t) -> p m t", m=16)
                ps = big[:, :].rearrange("p (m t) -> p m t", m=16)
                if n == 0:
                    then(tt(sc, ps, ident.unsqueeze(1).broadcast_to([P, 16, P]), ALU.mult))
                    tt(q_T, q_T, f_T, ALU.mult).then_inc(s["lvl_ready"], 1)
                    dve.wait_ge(s["lvl_ready"], n + 2)
                    return
                if n < LEVELS - 1:
                    L = 1 << (n - 1)
                    then(nc.vector.copy_predicated(sc, mask[:, n - 1, :].unsqueeze(1).broadcast_to([P, 16, P]), ps))
                    m = HEADS * TOK // (2 * L)
                    two = lambda ap: ap.rearrange("p (m two l) -> p m two l", m=m, two=2)
                    qv, kv = two(q_T), two(k_T)
                    tot = spans[n - 1][:, 0:2 * m].rearrange("p (m two) -> p m two", two=2)
                    wide = lambda k: tot[:, :, k:k + 1].broadcast_to([P, m, L])
                    then(tt(qv[:, :, 1, :], qv[:, :, 1, :], wide(0), ALU.mult))
                    then(tt(kv[:, :, 0, :], kv[:, :, 0, :], wide(1), ALU.mult))
                    if n < LEVELS - 2:
                        then(tt(spans[n][:, 0:m], tot[:, :, 0], tot[:, :, 1], ALU.mult))
                    ts(stat[:, 188:189], lbv[:, 0:1], 1.0, None, ALU.mult).then_inc(s["lvl_ready"], 1)

            def hgrn_mean():
                dve.wait_ge(s["osq_done"], 1)
                r = stat[:, 48:64]
                then(nc.vector.tensor_reduce(r, work[:, :].rearrange("p (m v) -> p m v", m=16), AX.X, ALU.add))
                ts(r, r, 1.0 / P, EPS, ALU.mult, ALU.add).then_inc(s["oms_ready"], 1)

            def hgrn_norm():
                r = stat[:, 48:64]
                dve.wait_ge(s["oroot_ready"], 1)
                then(nc.vector.reciprocal(r, r))
                wv = work[:, :].rearrange("p (m v) -> p m v", m=16)
                then(tt(wv, big[:, :].rearrange("p (m v) -> p m v", m=16),
                        r.unsqueeze(2).broadcast_to([P, 16, P]), ALU.mult))
                tt(work[:, :], work[:, :], og_tok, ALU.mult).then_inc(s["on_ready"], 1)

            def scores(r):
                dve.wait_ge(s["s_ready"], r + 1)
                sm = xtok[:, 1536 * r:1536 * (r + 1)].rearrange("p (h b s) -> p h b s", h=4, b=3)
                ps = big[:, :].rearrange("p (h b s) -> p h b s", h=4, b=4)
                bias = const("causal").unsqueeze(1).unsqueeze(1).broadcast_to([P, 4, 2, P])
                tt(sm[:, :, 0:3:2, :], ps[:, :, 0:3:2, :], bias, ALU.add)
                then(nc.vector.tensor_copy(sm[:, :, 1, :], ps[:, :, 1, :]))
                flat = xtok[:, 1536 * r:1536 * (r + 1)].rearrange("p (h s) -> p h s", h=4)
                mx = stat[:, 112:120]
                nc.vector.tensor_reduce(mx[:, 0:4], flat[:, :, 0:128], AX.X, ALU.max)
                then(nc.vector.tensor_reduce(mx[:, 4:8], flat[:, :, 128:384], AX.X, ALU.max))
                ts(mx, mx, -SCALE, None, ALU.mult).then_inc(s["mx_ready"], 1)

            def probabilities(r):
                flat = xtok[:, 1536 * r:1536 * (r + 1)].rearrange("p (h s) -> p h s", h=4)
                dve.wait_ge(s["exp_done"], 8 * (r + 1))
                rs = stat[:, 120:128]
                then(nc.vector.reciprocal(rs, rs))
                then(tt(flat[:, :, 0:128], flat[:, :, 0:128], rs[:, 0:4].unsqueeze(2).broadcast_to([P, 4, 128]), ALU.mult))
                tt(flat[:, :, 128:384], flat[:, :, 128:384], rs[:, 4:8].unsqueeze(2).broadcast_to([P, 4, 256]),
                   ALU.mult).then_inc(s["pn_ready"], 1)

            def probs_out(r):
                dve.wait_ge(s["pT_ready"], r + 1)
                if r:
                    dve.wait_ge(s["pv_ready"], r)
                nc.vector.tensor_copy(probs_T.rearrange("p (h s) -> p h s", h=4),
                                      big[:, :].rearrange("p (h s) -> p h s", h=4)[:, :, 0:384])\
                    .then_inc(s["pT_out"], 1)

            def gated(u):
                unit_stands(dve, u)
                if u == U_UPH:
                    dve.wait_ge(bank_free[1], U_UPH // 2)
                    dve.wait_ge(bank_free[0], U_UPH // 2)
                w = slice(512 * ((u - U_UPH) % 8), 512 * ((u - U_UPH) % 8 + 1))
                gate = gate_a if u < U_UPM else gate_b
                tt(gate[:, w], gate[:, w], acc[u % 2][:, :], ALU.mult).then_inc(bank_free[u % 2], 1)
                dve.wait_ge(bank_free[u % 2], u // 2 + 1)
                if u >= U_UPM:
                    tt(gate_a[:, w], gate_a[:, w], gate_b[:, w], ALU.add).then_inc(s["sum_ready"], 1)

            def added(u):
                if u == U_OUT:
                    dve.wait_ge(s["x_again"], 16 * TT)
                unit_stands(dve, u)
                c, t = (u - U_OUT) // 2, (u - U_OUT) % 2
                xs = x_t[t][:, 512 * c:512 * (c + 1)]
                tt(xs, xs, acc[u % 2][:, :], ALU.add).then_inc(bank_free[u % 2], 1)

            for g in range(LAG + 1, DENSE + LAG):
                lo_dense(g)
                if g == AT_BOUND:
                    bound()
                block = block_ending(g - LAG)
                if block is not None and U_HF // 2 <= block < U_HI // 2:
                    forget(2 * block)
                    forget(2 * block + 1)
                    if block == U_HI // 2 - 1:
                        ts(stat[:, 188:189], lbv[:, 0:1], 1.0, None, ALU.mult).then_inc(s["lvl_ready"], 1)
                n, rest = divmod(g - LAG - AT_LEVEL, LEVEL_STEP)
                if rest == 0 and 0 <= n < LEVELS - 1:
                    level(n)
                for k in range(U_MV - U_MQ):
                    if g == at_rotate(k) + 2:
                        rope(k)
                if g == AT_O + LAG + 1:
                    hgrn_mean()
                if g == AT_O + LAG + 3:
                    hgrn_norm()
                if g == AT_OT + LAG + 1:
                    dve.wait_ge(s["oh_hi_out"], 1)
                    stt(oh_lo[:, :], big[:, :], learnt("g_hgrn"), oh_hi[:, :].bitcast(F32), ALU.mult,
                        ALU.subtract).then_inc(s["oh_done"], 1)
                for r, at in enumerate(AT_ATT):
                    if g == at + LAG:
                        scores(r)
                    if g == at + LAG + 5:
                        probabilities(r)
                    if g == at + 14:
                        probs_out(r)
                block = block_ending(g - LAG + 1)
                if block is not None and block >= U_UPH // 2:
                    for u in (2 * block, 2 * block + 1):
                        gated(u) if u < U_OUT else added(u)

            factors(1)
            turned(1, learnt("g_ffn"))

            dve.wait_ge(s["logits_ready"], 1)
            lg = rt[:, 0:72].rearrange("p (t e) -> p t e", t=TT)
            then(nc.vector.tensor_copy(lg, mid[:, :].rearrange("p (t e) -> p t e", t=TT)[:, :, 0:36]))
            g_l, e_l = lg[:, :, 0:GROUPS], lg[:, :, GROUPS:36]
            ge = rt[:, 72:80].rearrange("p (t g) -> p t g", t=TT)
            gmax, pg = rt[:, 80:82], rt[:, 82:84]
            wide = lambda ap, n: ap.unsqueeze(2).broadcast_to([P, TT, n])
            desc = const("desc")

            def first_max(vals, top, onehot, n):
                down_counting = desc[:, 8 - n:8].unsqueeze(1).broadcast_to([P, TT, n])
                then(nc.vector.tensor_reduce(top, vals, AX.X, ALU.max))
                then(tt(onehot, vals, wide(top, n), ALU.is_equal))
                then(tt(onehot, onehot, down_counting, ALU.mult))
                then(nc.vector.tensor_reduce(rt[:, 84:86], onehot, AX.X, ALU.max))
                then(tt(onehot, onehot, wide(rt[:, 84:86], n), ALU.is_equal))

            goh = rt[:, 86:94].rearrange("p (t g) -> p t g", t=TT)
            first_max(g_l, gmax, goh, GROUPS)
            tt(ge, g_l, wide(gmax, GROUPS), ALU.subtract).then_inc(s["gexp_in"], 1)
            dve.wait_ge(s["gexp_out"], 1)
            then(nc.vector.tensor_reduce(pg, ge, AX.X, ALU.add))
            then(nc.vector.reciprocal(pg, pg))
            grid = [P, TT, GROUPS, PER_GROUP]
            prod = rt[:, 96:160].rearrange("p (t g i) -> p t g i", t=TT, g=GROUPS)
            for t in range(TT):
                then(tt(prod[:, t], e_l[:, t, :].rearrange("p (g i) -> p g i", g=GROUPS),
                        goh[:, t, :].unsqueeze(2).broadcast_to([P, GROUPS, PER_GROUP]), ALU.mult))
            e8 = rt[:, 160:176].rearrange("p (t i) -> p t i", t=TT)
            for t in range(TT):
                then(nc.vector.tensor_reduce(e8[:, t, :], prod[:, t].rearrange("p g i -> p i g"), AX.X, ALU.add))
            oh = [rt[:, 208 + 16 * k:224 + 16 * k].rearrange("p (t i) -> p t i", t=TT) for k in range(2)]
            tops = [rt[:, 196 + 2 * k:198 + 2 * k] for k in range(2)]
            first_max(e8, tops[0], oh[0], PER_GROUP)
            e8b = rt[:, 176:192].rearrange("p (t i) -> p t i", t=TT)
            then(stt(e8b, oh[0], -1e30, e8, ALU.mult, ALU.add))
            first_max(e8b, tops[1], oh[1], PER_GROUP)
            we = rt[:, 200:202]
            tt(we, tops[1], tops[0], ALU.subtract).then_inc(s["wexp_in"], 1)
            dve.wait_ge(s["wexp_out"], 1)
            w_k = [rt[:, 202 + 2 * k:204 + 2 * k] for k in range(2)]
            then(ts(w_k[0], we, 1.0, None, ALU.add))
            then(nc.vector.reciprocal(w_k[0], w_k[0]))
            then(tt(w_k[0], w_k[0], pg, ALU.mult))
            then(tt(w_k[1], w_k[0], we, ALU.mult))
            OH = [rt[:, 256 + 64 * k:320 + 64 * k].rearrange("p (t e) -> p t e", t=TT) for k in range(2)]
            both = rt[:, 384:448].rearrange("p (t e) -> p t e", t=TT)
            for k in range(2):
                for t in range(TT):
                    then(tt(OH[k][:, t, :].rearrange("p (g i) -> p g i", g=GROUPS),
                            goh[:, t, :].unsqueeze(2).broadcast_to([P, GROUPS, PER_GROUP]),
                            oh[k][:, t, :].unsqueeze(1).broadcast_to([P, GROUPS, PER_GROUP]), ALU.mult))
            tt(both, OH[0], OH[1], ALU.add).then_inc(s["onehot_ready"], 1)

            dve.wait_ge(s["counts_ready"], 1)
            cnt, incl, slot0 = rt[:, 448:480], rt[:, 480:512], rt[:, 512:544]
            pos = rt[:, 544:608].rearrange("p (t e) -> p t e", t=TT)
            then(nc.vector.tensor_copy(cnt, mid[:, 256:288]))
            then(nc.vector.tensor_tensor_scan(incl, ones[:, 0:EXPERTS], cnt, 0.0, ALU.mult, ALU.add))
            then(tt(slot0, incl, cnt, ALU.subtract))
            then(tt(pos, mid[:, 288:352].rearrange("p (t e) -> p t e", t=TT),
                    slot0.unsqueeze(1).broadcast_to([P, TT, EXPERTS]), ALU.add))
            slot_k = [rt[:, 608 + 2 * k:610 + 2 * k] for k in range(2)]
            tmp = rt[:, 612:676].rearrange("p (t e) -> p t e", t=TT)
            for k in range(2):
                then(tt(tmp, pos, OH[k], ALU.mult))
                then(nc.vector.tensor_reduce(slot_k[k], tmp, AX.X, ALU.add))
            dve.wait_ge(s["iota_in"], 16)
            at = [[slot_k[k][:, t:t + 1] for k in range(2)] for t in range(TT)]
            wt = [[w_k[k][:, t:t + 1] for k in range(2)] for t in range(TT)]
            for t in range(TT):
                then(ts(sel[:, t, :], iota, at[t][0], None, ALU.is_equal))
                stt(sel[:, t, :], iota, at[t][1], sel[:, t, :].bitcast(F32), ALU.is_equal, ALU.add)\
                    .then_inc(s["sel_ready"], 1)
            npass, many = rt[:, 676:708], rt[:, 708:740]
            then(ts(npass, cnt, float(WIN), 1.0, ALU.is_gt, ALU.add))
            for m in range(2, TOK // WIN):
                then(stt(npass, cnt, float(WIN * m), npass, ALU.is_gt, ALU.add))
            then(nc.vector.tensor_tensor_scan(many, ones[:, 0:EXPERTS], npass, 0.0, ALU.mult, ALU.add))
            then(tt(npass, many, npass, ALU.subtract))
            a_e, d_e = rt[:, 740:772], rt[:, 772:804]
            then(stt(a_e, npass, -float(WIN), slot0, ALU.mult, ALU.add))
            then(nc.vector.tensor_copy(d_e[:, 0:1], a_e[:, 0:1]))
            then(tt(d_e[:, 1:EXPERTS], a_e[:, 1:EXPERTS], a_e[:, 0:EXPERTS - 1], ALU.subtract))
            row = lambda v: v[0:1].unsqueeze(1).broadcast_to([1, TIMES, EXPERTS])
            times = const("times")[0:1]
            e_of, s_of, o_of = [rt[0:1, 804 + 44 * k:804 + 44 * k + TIMES] for k in range(3)]
            then(tt(table, row(npass), times.unsqueeze(2).broadcast_to([1, TIMES, EXPERTS]), ALU.is_le))
            then(nc.vector.tensor_reduce(e_of, table, AX.X, ALU.add))
            then(ts(e_of, e_of, -1.0, None, ALU.add))
            then(tt(table_2, table, row(cnt), ALU.mult))
            then(nc.vector.tensor_reduce(o_of, table_2, AX.X, ALU.add))
            then(tt(table, table, row(d_e), ALU.mult))
            then(nc.vector.tensor_reduce(s_of, table, AX.X, ALU.add))
            then(stt(s_of, times, float(WIN), s_of, ALU.mult, ALU.add))
            then(tt(o_of, s_of, o_of, ALU.subtract))
            then(ts(o_of, o_of, float(WIN), 0.0, ALU.add, ALU.max))
            then(ts(o_of, o_of, float(WIN), None, ALU.min))
            then(ts(s_of, s_of, float(SLOTS), None, ALU.min))
            then(nc.vector.tensor_copy(tab[0:1, EXPERT_OF:EXPERT_OF + TIMES], e_of))
            then(nc.vector.tensor_copy(tab[0:1, SLOT_OF:SLOT_OF + TIMES], s_of))
            then(nc.vector.tensor_copy(tab[0:1, OFF_OF:OFF_OF + TIMES], o_of))
            then(ts(e_of, times, 2.0, many[0:1, EXPERTS - 1:EXPERTS], ALU.mult, ALU.is_lt))
            then(nc.vector.tensor_reduce(rt[0:1, 936:937], e_of, AX.X, ALU.add))
            then(ts(rt[0:1, 937:938], rt[0:1, 936:937], 2.0, None, ALU.mult))
            then(nc.vector.tensor_copy(tab[0:1, PAIRS:PAIRS + 1], rt[0:1, 936:937]))
            nc.vector.tensor_copy(tab[0:1, PASSES:PASSES + 1], rt[0:1, 937:938]).then_inc(s["tab_ready"], 1)
            dve.wait_ge(s["win0_hi"], 1)
            tt(win[0][:, :, WIN:P], xg_T[:, :, 0:WIN], win[0][:, :, 0:WIN].bitcast(F32), ALU.subtract)\
                .then_inc(s["win_ready"], 1)

            silu_v = silu_g.rearrange("p (c s) -> p c s", c=FC)
            hid_v = hid.rearrange("p (c s) -> p c s", c=FC)
            up_T = mid[:, 512:512 + FC * WIN].rearrange("p (c s) -> p c s", c=FC)

            def hidden(m, a):
                dve.wait_ge(s["folded"], m * 4 + (2 * a + 2))
                dve.wait_ge(s["silu_done"], m * 2 + (a + 1))
                tt(hid_hi[a][:, :, rows_of[a]], silu_v, up_T, ALU.mult).then_inc(s["hid_hi_out"], 1)
                tt(hid_v, silu_v, up_T, ALU.mult).then_inc(s["hid_hi_out"], 1)
                dve.wait_ge(s["hid_hi_out"], m * 4 + (2 * a + 2))
                tt(hid_lo[a][:, :, rows_of[a]], hid_v, hid_hi[a][:, :, rows_of[a]].bitcast(F32),
                   ALU.subtract).then_inc(s["hid_ready"], 1)

            def rows_out(stands):
                dve.wait_ge(bite_used, stands)
                for k in range(2, 4):
                    nc.vector.tensor_copy(y_sb[:, 512 * k:512 * (k + 1)], big[:, 512 * k:512 * (k + 1)])\
                        .then_inc(s["big_dve"], 1)

            def add(m, v):
                dve.wait_ge(s["big_filled"], m * 8 + (DC + v - 7))
                xs = x_t[v % 2][:, 512 * (v // 2):512 * (v // 2 + 1)]
                tt(xs, xs, big[:, 512 * (v % 4):512 * (v % 4 + 1)], ALU.add).then_inc(s["big_dve"], 1)

            def weights_by_slot():
                dve.wait_ge(s["big_act"], DC)
                then(nc.vector.memset(selw[:, :, SLOTS:XW], 0.0))
                for t in range(TT):
                    then(ts(selw[:, t, 0:SLOTS], iota, at[t][0], wt[t][0], ALU.is_equal, ALU.mult))
                    then(ts(sel_cols_2, iota, at[t][1], wt[t][1], ALU.is_equal, ALU.mult))
                    tt(selw[:, t, 0:SLOTS], selw[:, t, 0:SLOTS], sel_cols_2, ALU.add)\
                        .then_inc(s["sel_ready"], 1)

            for b in range(LAG, PAIR - DOWN + LAG):
                lo_dense(DENSE + b)
                if b == 20:
                    weights_by_slot()
                for a in range(2):
                    if b == FIRST_AT[a] + AT_HID:
                        hidden(0, a)
            dve.wait_ge(s["tab_ready"], 1)
            pairs = dve.value_load(tab[0:1, PAIRS:PAIRS + 1], min_val=EXPERTS // 2, max_val=MAX_PAIRS)
            with dve.Fori(1, pairs) as m:
                for b in range(LAG, PAIR + LAG):
                    lo_later(m, b)
                    for a in range(2):
                        if b == PAIR_AT[a] + AT_HID:
                            hidden(m, a)
                    if b == PASS + AT_Y:
                        rows_out(pair_start(m) + PASS)
                    if 0 <= b - (PASS + AT_COMB + LAG) < 8:
                        add(m, b - (PASS + AT_COMB + LAG))
            for b in range(LAG, DOWN + LAG + 1):
                lo_later(pairs, b)
                if b == DOWN + AT_Y:
                    rows_out(pair_start(pairs) + DOWN)
            for v in range(8):
                add(pairs, v)

            factors(2)
            turned_lo(1, learnt("g_ple"))
            for b in range(LAG + 1, N_PLE * IN_BITES + LAG):
                if b < N_PLE * IN_BITES:
                    lo_later(pairs, DOWN + b)
                if (b - LAG) % IN_BITES == IN_BITES - 1:
                    for t in range(TT):
                        n = (b - LAG) // IN_BITES
                        v = 2 * n + t
                        dve.wait_ge(s["p_out_act"], v + 1)
                        if v == 0:
                            dve.wait_ge(s["proj_again"], 16)
                        xs = x_t[t][:, 512 * n:512 * (n + 1)]
                        then(tt(sig_p[:, v % 2, :], sig_p[:, v % 2, :], proj_back[:, t, 512 * n:512 * (n + 1)],
                                ALU.mult))
                        tt(xs, xs, sig_p[:, v % 2, :], ALU.add).then_inc(s["p_out"], 1)
                        if v == 0:
                            dve.wait_ge(s["g_fin_in"], 16)
                        dve.wait_ge(s["p_out"], v + 1)
                        at = t * D + 512 * n
                        tt(times_g[:, at:at + 512], xs, g_fin[:, 512 * n:512 * (n + 1)], ALU.mult)\
                            .then_inc(s["times_g_ready"], 1)
            r = factors(3)
            dve.wait_ge(s["times_g_ready"], 8)
            ts(times_g[:, 0:D], times_g[:, 0:D], r[:, 0:1], None, ALU.mult).then_inc(s["fin_dve"], 1)

        @block.tensor
        def _(pe):
            mm = nc.tensor.matmul

            def turn(n, part=(0, DC)):
                if part[0] == 0:
                    if n == 0:
                        for t in range(TT):
                            pe.wait_ge(x_in[t], 16)
                    pe.wait_ge(s["h_ready"], TT * (n + 1))
                out, before = ("big_dve", 0) if n == 1 else ("hT_out", DC * (n // 2))
                for j in range(*part):
                    if j >= 8:
                        pe.wait_ge(s[out], before + 2 * (j // 2) - 6)
                    for t in range(TT):
                        rows = x_t[t].rearrange("p (c j) -> p j c", j=DC)[:, j, :]
                        q = (j // 2 % 4) * 512 + 256 * (j % 2) + P * t
                        ins = mm(big[:, q:q + P], rows, diag[:, t, :], start=True, stop=True)
                    ins.then_inc(s["hT_bank"], 1)
                    if n == 1 and j % 2 and j > 4:
                        logits(j - 5)
                        logits(j - 4)

            def logits(j):
                pe.wait_ge(s["big_dve"], j + 1)
                for t in range(TT):
                    ins = mm(mid[:, 512 * t:512 * t + 36], hT[:, j, P * t:P * (t + 1)], wr[:, j, :],
                             start=j == 0, stop=j == DC - 1)
                if j == DC - 1:
                    ins.then_inc(s["logits_ready"], 1)

            def products(dst, x_hi, x_lo, y_hi, y_lo, start, stop, beside=False):
                mm(dst, x_hi, y_hi, start=start, stop=False, skip_group_check=beside)
                mm(dst, x_lo, y_hi, start=False, stop=False, skip_group_check=beside)
                return mm(dst, x_hi, y_lo, start=False, stop=stop, skip_group_check=beside)

            def bite(buf, n, chunk=None):
                a = BITE * buf + 512 * n + (P * chunk if chunk is not None else 0)
                w = slice(a, a + (512 if chunk is None else P))
                return bite_hi[:, w], bite_lo[:, w]

            def open_bank(u):
                if u >= 2:
                    pe.wait_ge(bank_free[u % 2], u // 2)

            def extras(g):
                n, rest = divmod(g - AT_LEVEL, LEVEL_STEP)
                if rest == 0 and 0 <= n < LEVELS:
                    level(n)
                for k in range(U_MV - U_MQ):
                    if g == at_rotate(k):
                        raw_u = (mq_T, mk_T)[k // 4][:, 512 * (k % 4):512 * (k % 4 + 1)]
                        pe.wait_ge(bank_free[k % 2], (U_MQ + k) // 2 + 1)
                        if k:
                            pe.wait_ge(s["roped"], k)
                        mm(mid[:, 0:512], const("rot"), raw_u, start=True, stop=True).then_inc(s["rot_ready"], 1)
                if g == AT_O:
                    hgrn_out()
                if g == AT_OT:
                    pe.wait_ge(s["on_ready"], 1)
                    ov = big[:, :].rearrange("p (h t k) -> p h t k", h=HEADS, t=TT)
                    for h in range(HEADS):
                        for t in range(TT):
                            ins = nc.tensor.transpose(ov[:, h, t, :], work[:, t * HW + P * h:t * HW + P * (h + 1)], ident)
                    ins.then_inc(s["oT_ready"], 1)
                for r, at in enumerate(AT_ATT):
                    if g == at:
                        att_scores(r)
                    if g == at + 11:
                        att_turn(r)
                    if g == at + 17:
                        att_values(r)

            def level(n):
                pe.wait_ge(s["lvl_ready"], n + 1)
                if n == 0:
                    pe.wait_ge(bank_free[1], U_HI // 2)
                q_h, k_h = by_head(q_T), by_head(k_T)
                if n < LEVELS - 1:
                    for h in range(HEADS):
                        for b in range(2):
                            m = 2 * h + b
                            ins = mm(big[:, P * m:P * (m + 1)], k_h[:, h, P * b:P * (b + 1)],
                                     q_h[:, h, P * b:P * (b + 1)], start=True, stop=True)
                else:
                    for h in range(HEADS):
                        ins = mm(big[:, P * h:P * (h + 1)], k_h[:, h, 0:P], q_h[:, h, P:2 * P], start=True, stop=True)
                ins.then_inc(s["lvl_done"], 1)

            def hgrn_out():
                pe.wait_ge(s["off_copied"], 1)
                v = v_tok.rearrange("p (t c) -> p t c", t=TT)
                for t in range(TT):
                    for h in range(HEADS):
                        dst = big[:, t * HW + P * h:t * HW + P * (h + 1)]
                        if t:
                            mm(dst, sc_off[:, h, :], v[:, 0, P * h:P * (h + 1)], start=True, stop=False)
                        ins = mm(dst, sc_T[:, h, t, :], v[:, t, P * h:P * (h + 1)], start=not t, stop=True)
                ins.then_inc(s["o_ready"], 1)

            def att_scores(r):
                pe.wait_ge(s["roped"], 8)
                pe.wait_ge(s["oh_done"], 1) if r == 0 else pe.wait_ge(s["pT_out"], r)
                q_h, k_h = by_head(mq_T), by_head(mk_T)
                for i in range(4):
                    h, at = 4 * r + i, 512 * i
                    mm(big[:, at:at + 128], q_h[:, h, 0:P], k_h[:, h, 0:P], start=True, stop=True)
                    ins = mm(big[:, at + 128:at + 384], q_h[:, h, P:TOK], k_h[:, h, :], start=True, stop=True)
                ins.then_inc(s["s_ready"], 1)

            def att_turn(r):
                pe.wait_ge(s["pn_ready"], r + 1)
                pv = xtok[:, 1536 * r:1536 * (r + 1)].rearrange("p (h b s) -> p h b s", h=4, b=3)
                for i in range(4):
                    for b in range(3):
                        at = 512 * i + P * b
                        ins = nc.tensor.transpose(big[:, at:at + P], pv[:, i, b, :], ident)
                ins.then_inc(s["pT_ready"], 1)

            def att_values(r):
                pe.wait_ge(s["pT_out"], r + 1)
                if r == 0:
                    pe.wait_ge(bank_free[1], U_GA // 2)
                    pe.wait_ge(bank_free[0], U_GA // 2)
                else:
                    pe.wait_ge(s["om_out"], r)
                v = mv_tok.rearrange("p (t c) -> p t c", t=TT)
                pt_v = probs_T.rearrange("p (h s) -> p h s", h=4)
                for i in range(4):
                    h, at = 4 * r + i, TOK * i
                    mm(mid[:, at:at + TOK], v[:, 0, P * h:P * (h + 1)], pt_v[:, i, 0:TOK], start=True, stop=False)
                    ins = mm(mid[:, at + P:at + TOK], v[:, 1, P * h:P * (h + 1)], pt_v[:, i, TOK:384],
                             start=False, stop=True)
                ins.then_inc(s["pv_ready"], 1)

            turn(0, (0, 8))
            g = 0
            for block in range(N_IN + N_UP + N_OUT):
                up = N_IN <= block < N_IN + N_UP
                if block < N_IN:
                    x_hi, x_lo = hT_hi, hT_lo
                elif up:
                    hgrn = block < N_IN + N_UP // 2
                    x_hi, x_lo = [by_head(v[:, :]) for v in ((oh_hi, oh_lo) if hgrn else (om_hi, om_lo))]
                    pe.wait_ge(s["oh_done" if hgrn else "om_done"], 1)
                else:
                    x_hi, x_lo = merged_hi, merged_lo
                tokens_out = block in (4, 5, 6, 7, 12, 13) or block >= N_IN + N_UP
                bites = UP_BITES if up else IN_BITES
                for i in range(bites):
                    pe.wait_ge(lo_ready, g + 1)
                    if block == 0:
                        pe.wait_ge(s["hT_out"], 2 * i + 2)
                    if block == N_IN + N_UP:
                        pe.wait_ge(s["merged_ready"], i + 1)
                    for half in range(2):
                        u = 2 * block + half
                        if i == 0:
                            open_bank(u)
                        for n in range(2):
                            k = 2 * i + n
                            first, last = k == 0, k == 2 * bites - 1
                            if tokens_out:
                                w_hi, w_lo = bite(g % BUFS, n)
                                toks = slice(P * half, P * (half + 1))
                                ins = products(acc[half][:, :], x_hi[:, k, toks], x_lo[:, k, toks], w_hi, w_lo,
                                               first, last)
                            else:
                                for c in range(2):
                                    w_hi, w_lo = bite(g % BUFS, n, 2 * half + c)
                                    ins = products(acc[half][:, TOK * c:TOK * (c + 1)], w_hi, w_lo,
                                                   x_hi[:, k, :], x_lo[:, k, :], first and c == 0, last and c == 0, c == 1)
                        if half:
                            ins.then_inc(bite_used, 1)
                        elif last:
                            ins.then_inc(first_ready, 1)
                    if block == 0 and i < 2:
                        turn(0, (4 * i + 8, 4 * i + 12))
                    if block < N_IN:
                        extras(g)
                    g += 1
            assert g == DENSE

            def project(v):
                if v == 2:
                    for b in range(2):
                        pe.wait_ge(bank_free[b], U_END // 2)
                if v >= 4:
                    pe.wait_ge(s["proj_out"], v - 1)
                for k in range(2):
                    ins = mm(proj_bank(v), p_T[:, k, P * (v % 2):P * (v % 2 + 1)],
                             proj_sb[:, k, 512 * (v // 2):512 * (v // 2 + 1)], start=k == 0, stop=k == 1)
                ins.then_inc(s["proj_done"], 1)

            pe.wait_ge(s["proj_in"], 32)
            project(0)
            project(1)
            pe.wait_ge(s["router_in"], 16)
            pe.wait_ge(s["proj_out"], 2)
            turn(1)
            for j in range(DC - 4, DC):
                logits(j)
            for v in range(2, 6):
                project(v)
            pe.wait_ge(s["onehot_ready"], 1)
            both = rt[:, 384:448].rearrange("p (t e) -> p t e", t=TT)
            before = const("before")
            mm(mid[:, 256:288], ones, both[:, 0, :], start=True, stop=False)
            mm(mid[:, 256:288], ones, both[:, 1, :], start=False, stop=True)
            mm(mid[:, 288:320], before, both[:, 0, :], start=True, stop=True)
            mm(mid[:, 320:352], before, both[:, 1, :], start=True, stop=False)
            mm(mid[:, 320:352], ones, both[:, 0, :], start=False, stop=True).then_inc(s["counts_ready"], 1)
            project(6)
            project(7)
            pe.wait_ge(s["sel_ready"], TT)
            pe.wait_ge(s["h_lo_ready"], 1)
            for j in range(DC):
                if j >= 4:
                    pe.wait_ge(s["big_act"], j - 3)
                for part in (h_hi, h_lo):
                    for t in range(TT):
                        rows = part[:, t * D:(t + 1) * D].rearrange("p (c j) -> p j c", j=DC)[:, j, :]
                        ins = mm(big[:, 512 * (j % 4):512 * (j % 4 + 1)], rows, sel[:, t, :],
                                 start=t == 0 and part is h_hi, stop=t == 1 and part is h_lo)
                ins.then_inc(s["big_filled"], 1)
            fold = const("fold")

            def folded(m):
                for c in range(FC):
                    ins = mm(mid[:, 512 * m + WIN * c:512 * m + WIN * (c + 1)],
                             gu_sb[:, FE * m + P * c:FE * m + P * (c + 1)], fold, start=True, stop=True)
                ins.then_inc(s["folded"], 1)


            def down(a, b, buf):
                for n in range(2):
                    w_hi, w_lo = bite(buf, n)
                    c, bank = b // 2, 2 * (b % 2) + n
                    ins = products(big[:, 512 * bank:512 * (bank + 1)], hid_hi[a][:, c, :], hid_lo[a][:, c, :],
                                   w_hi, w_lo, c == 0 and a == 0, c == FC - 1 and a == 1)
                ins.then_inc(bite_used, 1)

            def turn_weights(m):
                pe.wait_ge(s["pair_ready"], m)
                for t in range(TT):
                    ins = nc.tensor.transpose(acc[0][:, P * t:P * (t + 1)], sel_pair[:, t, :], ident)
                ins.then_inc(s["selT_ready"], 1)

            def combine(m, v):
                if v == 0:
                    pe.wait_ge(s["selT_out"], m)
                    pe.wait_ge(s["big_act"], m * 2 + BIG_ACT)
                if v == 2:
                    pe.wait_ge(s["big_dve"], m * 10 + (BIG_DVE - 8))
                if v >= 4:
                    pe.wait_ge(s["big_dve"], m * 10 + (BIG_DVE - 8 + v - 3))
                n, t = v // 2, v % 2
                mm(big[:, 512 * (v % 4):512 * (v % 4 + 1)], sel_T[:, t, :], y_sb[:, 512 * n:512 * (n + 1)],
                   start=True, stop=True).then_inc(s["big_filled"], 1)

            def pair(m, start, at, first):
                for a in range(2):
                    for q in range(GU if first and a == 0 else PASS):
                        if q == 0:
                            pe.wait_ge(s["win_ready"], m * 2 + (a + 1))
                            if a == 1 and not first:
                                pe.wait_ge(s["selT_out"], m)
                        if q == GU:
                            pe.wait_ge(s["hid_ready"], m * 2 + a)
                            if first:
                                pe.wait_ge(s["padded"], 5)
                            if a == 1:
                                pe.wait_ge(s["big_act"], m * 2 + BIG_ACT)
                                pe.wait_ge(s["big_dve"], m * 10 + BIG_DVE)
                        pe.wait_ge(lo_ready, start + (at[a] + q + 1))
                        buf = (at[a] + q) % BUFS
                        if q < GU:
                            for n in range(2):
                                w_hi, w_lo = bite(buf, n)
                                j = 2 * (q % 8) + n
                                mm(acc[q // 8][:, :], win[a][:, j, :], w_hi, start=j == 0, stop=False)
                                ins = mm(acc[q // 8][:, :], win[a][:, j, :], w_lo, start=False, stop=j == DC - 1)
                            ins.then_inc(bite_used, 1)
                        else:
                            down(1 - a, q - GU, buf)
                        if q == AT_FOLD_G:
                            pe.wait_ge(s["gu_out"], m * 4 + (2 * a + 1))
                            folded(0)
                        if q == AT_FOLD_U and not (first and a == 0):
                            pe.wait_ge(s["gu_out"], m * 4 + (2 * a + 2))
                            folded(1)
                        if first and a == 1 and q == AT_FOLD_U - GU:
                            pe.wait_ge(s["gu_out"], 2)
                            folded(1)
                        if a == 0 and q == AT_SELT and not first:
                            turn_weights(m)
                        if a == 1 and not first and 0 <= q - AT_COMB < 8:
                            combine(m, q - AT_COMB)

            pair(0, DENSE, FIRST_AT, True)
            pe.wait_ge(s["tab_ready"], 1)
            pairs = pe.value_load(tab[0:1, PAIRS:PAIRS + 1], min_val=EXPERTS // 2, max_val=MAX_PAIRS)
            with pe.Fori(1, pairs) as m:
                pair(m, pair_start(m), PAIR_AT, False)
            pe.wait_ge(s["hid_ready"], pairs * 2)
            for b in range(DOWN):
                pe.wait_ge(lo_ready, pair_start(pairs) + (b + 1))
                down(1, b, b % BUFS)
                if b == 0:
                    turn_weights(pairs)
            for v in range(8):
                combine(pairs, v)

            pe.wait_ge(s["big_dve"], pairs * 10 + BIG_DVE)
            turn(2, (0, 8))
            for b in range(N_PLE * IN_BITES):
                i, k2 = b // IN_BITES, 2 * (b % IN_BITES)
                if i == 0:
                    pe.wait_ge(s["hT_out"], DC + k2 + 2)
                pe.wait_ge(lo_ready, pair_start(pairs) + (DOWN + b + 1))
                for t in range(TT):
                    for n in range(2):
                        k = k2 + n
                        if b >= 2 * IN_BITES and k == 0:
                            pe.wait_ge(s["p_out_act"], 2 * i + t - 3)
                        w_hi, w_lo = bite(b % BUFS, n)
                        ins = products(p_bank(2 * i + t), hT_hi[:, k, P * t:P * (t + 1)],
                                       hT_lo[:, k, P * t:P * (t + 1)], w_hi, w_lo, k == 0, k == DC - 1)
                    if t:
                        ins.then_inc(bite_used, 1)
                    elif k == DC - 1:
                        ins.then_inc(s["p_first"], 1)
                if b < 2:
                    turn(2, (4 * b + 8, 4 * b + 12))


def shape_constants():
    half = P // 2
    inv = 10000.0 ** (-np.arange(half, dtype=np.float32) / half)
    ang = np.arange(TOK, dtype=np.float32)[None, :] * inv.astype(np.float32)[:, None]
    cos = np.concatenate([np.cos(ang), np.cos(ang)], 0)
    sin = np.concatenate([np.sin(ang), np.sin(ang)], 0)
    rot = np.zeros((P, P), np.float32)
    for d in range(half):
        rot[d + half, d] = -1.0
        rot[d, d + half] = 1.0
    i = np.arange(P)
    parts = dict(ident=np.eye(P), rot=rot, cos=cos, sin=sin,
                 causal=np.where(i[None, :] <= i[:, None], 0.0, -1e30),
                 before=(i[:, None] < i[None, :]), ones=np.ones((P, P)),
                 desc=np.tile(np.arange(8, 0, -1), (P, 1)),
                 fold=np.concatenate([np.eye(WIN), np.eye(WIN)], 0),
                 times=np.tile(np.arange(TIMES), (P, 1)), zeros=np.zeros((P, 64)))
    consts = np.concatenate([np.asarray(parts[n], np.float32) for n in CONSTS], 1)
    masks = np.zeros((P, 7, P), np.float32)
    for n in range(7):
        span = i >> n
        masks[:, n, :] = (span[:, None] % 2 == 0) & (span[None, :] == span[:, None] + 1)
    return np.ascontiguousarray(consts), masks.reshape(P, 7 * P), np.arange(SLOTS, dtype=np.float32)[None, :]


def kernel(x, p, norm_mix_g, w_in, hgrn_lb_raw, hgrn_norm_g, w_up_hgrn, w_up_moba, w_out, norm_ffn_g,
           w_router_group, w_router_expert, w_exp_gate, w_exp_up, w_exp_down, norm_ple_g, w_ple_gate,
           w_ple_proj, norm_final_g):
    import concourse.bacc as bacc
    from concourse.bass_utils import run_bass_kernel_spmd

    a = np.asarray
    split = lambda w, n: a(w).reshape(P, 2, 8, n, 512).transpose(3, 1, 0, 2, 4).reshape(2 * n, P, HALF)
    plain = lambda w, k, n: a(w).reshape(k, 8, P, n, 512).transpose(3, 0, 2, 1, 4).reshape(k * n, P, HALF)
    halves = np.concatenate([split(w_in[0], N_IN), plain(w_up_hgrn[0], 1, 4), plain(w_up_moba[0], 1, 4),
                             plain(w_out[0], 2, N_OUT), split(w_ple_gate[0], N_PLE)], 0)
    cols = lambda g: a(g).reshape(P, DC)
    learned = np.concatenate([cols(norm_mix_g), cols(norm_ffn_g), cols(norm_ple_g),
                              a(hgrn_norm_g).reshape(P, 1),
                              a(hgrn_lb_raw).reshape(2, HEADS, P).transpose(2, 0, 1).reshape(P, 16)], 1)
    router = np.concatenate([a(w_router_group[0]).reshape(P, DC, GROUPS),
                             a(w_router_expert[0]).reshape(P, DC, EXPERTS)], 2)
    pt = a(p).reshape(TOK, 2, P).transpose(2, 1, 0)
    proj = a(w_ple_proj[0]).reshape(2, P, D).transpose(1, 0, 2)
    consts, masks, iota_row = shape_constants()
    arrays = dict(x=a(x).reshape(TOK, D), pt=pt, halves=halves, ple_proj=proj, learned=learned, router=router,
                  consts=consts, iota_row=iota_row, masks=masks, w_gate=a(w_exp_gate[0]), w_up=a(w_exp_up[0]),
                  w_down=a(w_exp_down[0]), g_final=a(norm_final_g).reshape(1, D))
    nc = bacc.Bacc("TRN2", target_bir_lowering=False, num_devices=1)
    arrays = {n: np.ascontiguousarray(v) for n, v in arrays.items()}
    aps = [nc.dram_tensor("in_" + n, v.shape, mybir.dt.from_np(v.dtype), kind="ExternalInput").ap()
           for n, v in arrays.items()]
    out = nc.dram_tensor("out", (TOK, D), F32, kind="ExternalOutput").ap()
    build_layer(nc, *aps, out)
    r = run_bass_kernel_spmd(nc, [{"in_" + n: v for n, v in arrays.items()}], core_ids=[0])
    return r.results[0]["out"].reshape(1, TOK, D)
```
